# Optimizing a Trainium2 kernel written in Bass

```python
import math
import jax
import jax.numpy as jnp
from jax import lax
import numpy as np

D_MODEL = 1024
BATCH = 1
SEQ = 1024
DEPTH = 2
DEC_BATCH = 8
DEC_SEQ = 8
PAST_LEN = 256
PAGE_SIZE = 128

HEAD_DIM = 64
A_HEADS = 8
A_KV_HEADS = 2
IDX_HEADS = 8
IDX_DIM = 64
TOPK_MAX = 256
B_GROUPS = ((128, 1), (512, 4), (2048, 16))
N_GROUPS = 3
B_HEADS = 4
N_BUCKETS = 32
MAX_DISTANCE = 2048
N_BIAS_HEADS = A_HEADS + N_GROUPS * B_HEADS
D_RNN = D_MODEL
LRU_BLOCKS = 8
LRU_BLOCK = D_RNN // LRU_BLOCKS
LRU_C = 8.0
CONV_W = 4
D_FF = 4 * D_MODEL
N_ATTN_LAYERS = (DEPTH + 1) // 2
N_REC_LAYERS = DEPTH // 2
Q_BLOCK = 128
EPS = 1e-6
NEG = -1e30
A_Q_W = A_HEADS * HEAD_DIM
A_KV_W = A_KV_HEADS * HEAD_DIM
IDX_Q_W = IDX_HEADS * IDX_DIM
B_W = N_GROUPS * 3 * B_HEADS * HEAD_DIM
ATTN_IN_W = A_Q_W + 2 * A_KV_W + IDX_Q_W + IDX_DIM + IDX_HEADS + B_W
ATTN_OUT_W = A_Q_W + B_HEADS * HEAD_DIM
SPLIT_POINTS = (A_Q_W, A_Q_W + A_KV_W, A_Q_W + 2 * A_KV_W, A_Q_W + 2 * A_KV_W + IDX_Q_W,
                A_Q_W + 2 * A_KV_W + IDX_Q_W + IDX_DIM, A_Q_W + 2 * A_KV_W + IDX_Q_W + IDX_DIM + IDX_HEADS)

kernel_name = 'dsa_dilated_rglru_hybrid_step'

f32 = jnp.float32

def rmsnorm(x, g):
    xf = x.astype(f32)
    y = xf * lax.rsqrt(jnp.mean(xf * xf, axis=-1, keepdims=True) + EPS)
    return (y * g.astype(f32)).astype(x.dtype)

def rel_bucket(dist):
    max_exact = N_BUCKETS // 2
    d = jnp.maximum(dist, 0)
    df = jnp.maximum(d, 1).astype(f32)
    large = max_exact + (jnp.log(df / max_exact) / math.log(MAX_DISTANCE / max_exact)
                         * (N_BUCKETS - max_exact)).astype(jnp.int32)
    large = jnp.minimum(large, N_BUCKETS - 1)
    return jnp.where(d < max_exact, d, large)

def group_bias(rel_bias, g):
    win, dil = B_GROUPS[g]
    dist = jnp.arange(win // dil + 1, dtype=jnp.int32) * dil
    lo = A_HEADS + g * B_HEADS
    return rel_bias[rel_bucket(dist)][:, lo:lo + B_HEADS].T.astype(f32)

def take_rows(a, idx):
    return jax.vmap(lambda r, i: r[i])(a, idx)

def attn_projections(xn, w_in, a_q_norm, a_k_norm, b_q_norm, b_k_norm):
    bsz, t = xn.shape[:2]
    h = jnp.einsum('btd,de->bte', xn, w_in)
    qa, ka, va, qi, ki, wi, hb = jnp.split(h, list(SPLIT_POINTS), axis=-1)
    q_a = rmsnorm(qa.reshape(bsz, t, A_HEADS, HEAD_DIM), a_q_norm)
    k_a = rmsnorm(ka.reshape(bsz, t, A_KV_HEADS, HEAD_DIM), a_k_norm)
    v_a = va.reshape(bsz, t, A_KV_HEADS, HEAD_DIM)
    qi = qi.reshape(bsz, t, IDX_HEADS, IDX_DIM)
    wi = wi * IDX_HEADS ** -0.5
    hb = hb.reshape(bsz, t, N_GROUPS, 3, B_HEADS, HEAD_DIM)
    q_b = rmsnorm(hb[:, :, :, 0], b_q_norm[:, None, :])
    k_b = rmsnorm(hb[:, :, :, 1], b_k_norm[:, None, :])
    v_b = hb[:, :, :, 2]
    return q_a, k_a, v_a, qi, ki, wi, q_b, k_b, v_b

def index_scores(qi, wi, ki):
    dots = jnp.einsum('bqhd,bsd->bqhs', qi.astype(f32), ki.astype(f32)) * IDX_DIM ** -0.5
    return jnp.einsum('bqh,bqhs->bqs', wi.astype(f32), jax.nn.relu(dots))

def sparse_attend(q, k_sel, v_sel, valid, dist, table_a):
    bsz, nq, nk = dist.shape
    rep = A_HEADS // A_KV_HEADS
    qg = q.reshape(bsz, nq, A_KV_HEADS, rep, HEAD_DIM)
    s = jnp.einsum('bqgrd,bqkgd->bqgrk', qg, k_sel).astype(f32) * HEAD_DIM ** -0.5
    bias = jnp.moveaxis(table_a[rel_bucket(dist)].astype(f32), -1, 2).reshape(bsz, nq, A_KV_HEADS, rep, nk)
    s = jnp.where(valid[:, :, None, None, :], s + bias, NEG)
    p = jax.nn.softmax(s, axis=-1).astype(v_sel.dtype)
    o = jnp.einsum('bqgrk,bqkgd->bqgrd', p, v_sel)
    return o.reshape(bsz, nq, A_Q_W)

def dilated_attend(q, k, v, q_idx, dilation, n_keys, bias_g):
    kidx = q_idx[:, None] - jnp.arange(n_keys, dtype=jnp.int32)[None, :] * dilation
    valid = kidx >= 0
    kc = jnp.maximum(kidx, 0)
    k_sel = k[:, kc]
    v_sel = v[:, kc]
    s = jnp.einsum('bqhd,bqkhd->bqhk', q, k_sel).astype(f32) * HEAD_DIM ** -0.5 + bias_g[None, None]
    s = jnp.where(valid[None, :, None, :], s, NEG)
    lse = jax.nn.logsumexp(s, axis=-1)
    p = jnp.exp(s - lse[..., None])
    o = jnp.einsum('bqhk,bqkhd->bqhd', p, v_sel.astype(f32))
    return o, lse

def merge_groups(outs, lses):
    wts = jax.nn.softmax(jnp.stack(lses, 0), axis=0)
    o = jnp.sum(wts[..., None] * jnp.stack(outs, 0), axis=0)
    return o.reshape(o.shape[0], o.shape[1], B_HEADS * HEAD_DIM)

def to_blocks(a, nblk):
    return a.reshape((a.shape[0], nblk, Q_BLOCK) + a.shape[2:]).swapaxes(0, 1)

def attn_mixer_prompt(xn, w_in, w_out, a_q_norm, a_k_norm, b_q_norm, b_k_norm, rel_bias):
    bsz, s = xn.shape[:2]
    q_a, k_a, v_a, qi, ki, wi, q_b, k_b, v_b = attn_projections(xn, w_in, a_q_norm, a_k_norm, b_q_norm, b_k_norm)
    topk = min(TOPK_MAX, s // 4)
    nblk = s // Q_BLOCK
    pos = jnp.arange(s, dtype=jnp.int32)
    table_a = rel_bias[:, :A_HEADS]
    biases = [group_bias(rel_bias, g) for g in range(N_GROUPS)]

    def body(args):
        qa_blk, qi_blk, wi_blk, qb_blk, tb = args
        sc = index_scores(qi_blk, wi_blk, ki)
        sc = jnp.where(pos[None, None, :] <= tb[None, :, None], sc, NEG)
        _, idx = lax.top_k(sc, topk)
        dist = tb[None, :, None] - idx
        o_a = sparse_attend(qa_blk, take_rows(k_a, idx), take_rows(v_a, idx), dist >= 0, dist, table_a)
        outs, lses = [], []
        for g, (win, dil) in enumerate(B_GROUPS):
            o, l = dilated_attend(qb_blk[:, :, g], k_b[:, :, g], v_b[:, :, g], tb, dil, win // dil + 1, biases[g])
            outs.append(o)
            lses.append(l)
        o_b = merge_groups(outs, lses).astype(o_a.dtype)
        return jnp.concatenate([o_a, o_b], axis=-1)

    o = lax.map(body, (to_blocks(q_a, nblk), to_blocks(qi, nblk), to_blocks(wi, nblk),
                       to_blocks(q_b, nblk), pos.reshape(nblk, Q_BLOCK)))
    o = o.swapaxes(0, 1).reshape(bsz, s, ATTN_OUT_W)
    y = jnp.einsum('bte,ed->btd', o, w_out)
    kv_a = jnp.stack([k_a, v_a], axis=2)
    bufs = []
    for g, (win, dil) in enumerate(B_GROUPS):
        wl = min(win, s)
        bufs.append(jnp.stack([k_b[:, s - wl:, g], v_b[:, s - wl:, g]], axis=2))
    return y, kv_a, ki, bufs

def attn_mixer_sample(xn, kv_pool, kidx_pool, bufs, page_table, w_in, w_out, a_q_norm, a_k_norm,
                      b_q_norm, b_k_norm, rel_bias):
    bsz, t = xn.shape[:2]
    q_a, k_a, v_a, qi, ki, wi, q_b, k_b, v_b = attn_projections(xn, w_in, a_q_norm, a_k_norm, b_q_norm, b_k_norm)
    past = page_table.shape[1] * PAGE_SIZE
    n_keys = past + t
    tq = past + jnp.arange(t, dtype=jnp.int32)
    ki_past = kidx_pool[page_table].reshape(bsz, past, IDX_DIM).astype(ki.dtype)
    ki_all = jnp.concatenate([ki_past, ki], axis=1)
    sc = index_scores(qi, wi, ki_all)
    sc = jnp.where(jnp.arange(n_keys, dtype=jnp.int32)[None, None, :] <= tq[None, :, None], sc, NEG)
    _, idx = lax.top_k(sc, min(TOPK_MAX, n_keys // 4))
    dist = tq[None, :, None] - idx
    ip = jnp.minimum(idx, past - 1)
    phys = jnp.take_along_axis(page_table, (ip // PAGE_SIZE).reshape(bsz, -1), axis=1).reshape(idx.shape)
    kv_past = kv_pool[phys, ip % PAGE_SIZE].astype(k_a.dtype)
    kv_new = jnp.stack([k_a, v_a], axis=2)
    kv_cur = take_rows(kv_new, jnp.clip(idx - past, 0, t - 1))
    kv_sel = jnp.where((idx < past)[..., None, None, None], kv_past, kv_cur)
    o_a = sparse_attend(q_a, kv_sel[:, :, :, 0], kv_sel[:, :, :, 1], dist >= 0, dist, rel_bias[:, :A_HEADS])
    outs, lses, new_bufs = [], [], []
    for g, (win, dil) in enumerate(B_GROUPS):
        buf = bufs[g].astype(k_b.dtype)
        wl = buf.shape[1]
        kv_all = jnp.concatenate([buf, jnp.stack([k_b[:, :, g], v_b[:, :, g]], axis=2)], axis=1)
        o, l = dilated_attend(q_b[:, :, g], kv_all[:, :, 0], kv_all[:, :, 1], wl + jnp.arange(t, dtype=jnp.int32),
                              dil, win // dil + 1, group_bias(rel_bias, g))
        outs.append(o)
        lses.append(l)
        new_bufs.append(kv_all[:, t:])
    o_b = merge_groups(outs, lses).astype(o_a.dtype)
    y = jnp.einsum('bte,ed->btd', jnp.concatenate([o_a, o_b], axis=-1), w_out)
    return y, kv_new, ki, new_bufs

def linear_scan(a, b, h0):
    b = b.at[:, 0].add(a[:, 0] * h0)

    def comb(left, right):
        al, bl = left
        ar, br = right
        return al * ar, ar * bl + br

    _, h = lax.associative_scan(comb, (a, b), axis=1)
    return h

def rec_mixer(xn, conv_state, h0, w_in, conv_w, conv_b, ga_w, ga_b, gx_w, gx_b, lru_a, w_out):
    bsz, t = xn.shape[:2]
    gate_in, x_in = jnp.split(jnp.einsum('btd,de->bte', xn, w_in), 2, axis=-1)
    gate = jax.nn.gelu(gate_in)
    xc = jnp.concatenate([conv_state.astype(x_in.dtype), x_in], axis=1)
    conv = conv_b + sum(xc[:, i:i + t] * conv_w[i] for i in range(CONV_W))
    xb = conv.reshape(bsz, t, LRU_BLOCKS, LRU_BLOCK)
    r = jax.nn.sigmoid((jnp.einsum('btni,nij->btnj', xb, ga_w).reshape(bsz, t, D_RNN) + ga_b).astype(f32))
    i_g = jax.nn.sigmoid((jnp.einsum('btni,nij->btnj', xb, gx_w).reshape(bsz, t, D_RNN) + gx_b).astype(f32))
    log_a = LRU_C * r * jax.nn.log_sigmoid(lru_a.astype(f32))
    a = jnp.exp(log_a)
    b = jnp.sqrt(-jnp.expm1(2.0 * log_a)) * i_g * conv.astype(f32)
    h = linear_scan(a, b, h0.astype(f32))
    y = jnp.einsum('bte,ed->btd', h.astype(xn.dtype) * gate, w_out)
    return y, xc[:, t:], h[:, -1]

def sq_relu_mlp(xn, w1, w2):
    h = jax.nn.relu(jnp.einsum('btd,df->btf', xn, w1))
    return jnp.einsum('btf,fd->btd', h * h, w2)

def setup_inputs(seed: int = 0) -> dict:
    key = jax.random.key(seed)
    ks = iter(jax.random.split(key, 40))

    def nrm(shape, scale):
        return jax.random.normal(next(ks), shape, f32) * scale

    n_pages = PAST_LEN // PAGE_SIZE
    n_used = DEC_BATCH * n_pages
    n_phys = (5 * n_used + 3) // 4
    page_table = jax.random.permutation(next(ks), n_phys)[:n_used].reshape(DEC_BATCH, n_pages).astype(jnp.int32)
    wb = [min(win, PAST_LEN) for win, _ in B_GROUPS]
    u = jax.random.uniform(next(ks), (N_REC_LAYERS, D_RNN), f32, minval=0.9, maxval=0.999)
    return {
        'x_prompt': nrm((BATCH, SEQ, D_MODEL), 1.0),
        'x_sample': nrm((DEC_BATCH, DEC_SEQ, D_MODEL), 1.0),
        'cache_a_kv': nrm((N_ATTN_LAYERS, n_phys, PAGE_SIZE, 2, A_KV_HEADS, HEAD_DIM), 1.0),
        'cache_a_kidx': nrm((N_ATTN_LAYERS, n_phys, PAGE_SIZE, IDX_DIM), 1.0),
        'cache_b_kv_w128': nrm((N_ATTN_LAYERS, DEC_BATCH, wb[0], 2, B_HEADS, HEAD_DIM), 1.0),
        'cache_b_kv_w512': nrm((N_ATTN_LAYERS, DEC_BATCH, wb[1], 2, B_HEADS, HEAD_DIM), 1.0),
        'cache_b_kv_w2048': nrm((N_ATTN_LAYERS, DEC_BATCH, wb[2], 2, B_HEADS, HEAD_DIM), 1.0),
        'state_c_h': nrm((N_REC_LAYERS, DEC_BATCH, D_RNN), 0.5),
        'state_c_conv': nrm((N_REC_LAYERS, DEC_BATCH, CONV_W - 1, D_RNN), 1.0),
        'page_table': page_table,
        'norm_mix': 1.0 + nrm((DEPTH, D_MODEL), 0.02),
        'norm_mlp': 1.0 + nrm((DEPTH, D_MODEL), 0.02),
        'rel_bias': nrm((N_BUCKETS, N_BIAS_HEADS), 0.2),
        'attn_w_in': nrm((N_ATTN_LAYERS, D_MODEL, ATTN_IN_W), D_MODEL ** -0.5),
        'attn_w_out': nrm((N_ATTN_LAYERS, ATTN_OUT_W, D_MODEL), ATTN_OUT_W ** -0.5),
        'a_q_norm': 1.0 + nrm((N_ATTN_LAYERS, HEAD_DIM), 0.02),
        'a_k_norm': 1.0 + nrm((N_ATTN_LAYERS, HEAD_DIM), 0.02),
        'b_q_norm': 1.0 + nrm((N_ATTN_LAYERS, N_GROUPS, HEAD_DIM), 0.02),
        'b_k_norm': 1.0 + nrm((N_ATTN_LAYERS, N_GROUPS, HEAD_DIM), 0.02),
        'rec_w_in': nrm((N_REC_LAYERS, D_MODEL, 2 * D_RNN), D_MODEL ** -0.5),
        'rec_conv_w': nrm((N_REC_LAYERS, CONV_W, D_RNN), CONV_W ** -0.5),
        'rec_conv_b': nrm((N_REC_LAYERS, D_RNN), 0.02),
        'rec_gate_a_w': nrm((N_REC_LAYERS, LRU_BLOCKS, LRU_BLOCK, LRU_BLOCK), LRU_BLOCK ** -0.5),
        'rec_gate_a_b': nrm((N_REC_LAYERS, D_RNN), 0.02),
        'rec_gate_x_w': nrm((N_REC_LAYERS, LRU_BLOCKS, LRU_BLOCK, LRU_BLOCK), LRU_BLOCK ** -0.5),
        'rec_gate_x_b': nrm((N_REC_LAYERS, D_RNN), 0.02),
        'rec_lru_a': jnp.log(u) - jnp.log1p(-u),
        'rec_w_out': nrm((N_REC_LAYERS, D_RNN, D_MODEL), D_RNN ** -0.5),
        'mlp_w1': nrm((DEPTH, D_MODEL, D_FF), D_MODEL ** -0.5),
        'mlp_w2': nrm((DEPTH, D_FF, D_MODEL), 0.5 * D_FF ** -0.5),
    }

def reference(x_prompt, x_sample, cache_a_kv, cache_a_kidx, cache_b_kv_w128, cache_b_kv_w512, cache_b_kv_w2048,
              state_c_h, state_c_conv, page_table, norm_mix, norm_mlp, rel_bias, attn_w_in, attn_w_out,
              a_q_norm, a_k_norm, b_q_norm, b_k_norm, rec_w_in, rec_conv_w, rec_conv_b, rec_gate_a_w,
              rec_gate_a_b, rec_gate_x_w, rec_gate_x_b, rec_lru_a, rec_w_out, mlp_w1, mlp_w2):
    xp, xs = x_prompt, x_sample
    b_caches = (cache_b_kv_w128, cache_b_kv_w512, cache_b_kv_w2048)
    pa_kv, pa_ki, sa_kv, sa_ki = [], [], [], []
    pb = [[] for _ in range(N_GROUPS)]
    sb = [[] for _ in range(N_GROUPS)]
    pc_h, pc_conv, sc_h, sc_conv = [], [], [], []
    for layer in range(DEPTH):
        xpn = rmsnorm(xp, norm_mix[layer])
        xsn = rmsnorm(xs, norm_mix[layer])
        if layer % 2 == 0:
            li = layer // 2
            aw = (attn_w_in[li], attn_w_out[li], a_q_norm[li], a_k_norm[li], b_q_norm[li], b_k_norm[li], rel_bias)
            yp, kv_p, ki_p, bufs_p = attn_mixer_prompt(xpn, *aw)
            ys, kv_s, ki_s, bufs_s = attn_mixer_sample(xsn, cache_a_kv[li], cache_a_kidx[li],
                                                       [c[li] for c in b_caches], page_table, *aw)
            pa_kv.append(kv_p)
            pa_ki.append(ki_p)
            sa_kv.append(kv_s)
            sa_ki.append(ki_s)
            for g in range(N_GROUPS):
                pb[g].append(bufs_p[g])
                sb[g].append(bufs_s[g])
        else:
            ri = layer // 2
            rw = (rec_w_in[ri], rec_conv_w[ri], rec_conv_b[ri], rec_gate_a_w[ri], rec_gate_a_b[ri],
                  rec_gate_x_w[ri], rec_gate_x_b[ri], rec_lru_a[ri], rec_w_out[ri])
            conv0 = jnp.zeros((xpn.shape[0], CONV_W - 1, D_RNN), xpn.dtype)
            h0 = jnp.zeros((xpn.shape[0], D_RNN), f32)
            yp, cp, hp = rec_mixer(xpn, conv0, h0, *rw)
            ys, cs, hs = rec_mixer(xsn, state_c_conv[ri], state_c_h[ri], *rw)
            pc_h.append(hp)
            pc_conv.append(cp)
            sc_h.append(hs)
            sc_conv.append(cs)
        xp = xp + yp
        xs = xs + ys
        xp = xp + sq_relu_mlp(rmsnorm(xp, norm_mlp[layer]), mlp_w1[layer], mlp_w2[layer])
        xs = xs + sq_relu_mlp(rmsnorm(xs, norm_mlp[layer]), mlp_w1[layer], mlp_w2[layer])
    return (xp, xs,
            jnp.stack(pa_kv), jnp.stack(pa_ki), jnp.stack(pb[0]), jnp.stack(pb[1]), jnp.stack(pb[2]),
            jnp.stack(pc_h), jnp.stack(pc_conv),
            jnp.stack(sa_kv), jnp.stack(sa_ki), jnp.stack(sb[0]), jnp.stack(sb[1]), jnp.stack(sb[2]),
            jnp.stack(sc_h), jnp.stack(sc_conv))


_drawn_inputs = setup_inputs


def setup_inputs(seed=0):
    import zlib

    import numpy as np

    out = dict(_drawn_inputs(seed))
    spreads = {}
    factors = {'norm_mlp': 3.525,
     'a_q_norm': 8.0,
     'a_k_norm': 4.03,
     'b_q_norm': 8.0,
     'b_k_norm': 3.9,
     'rec_gate_a_b': 8.0,
     'rec_gate_x_b': 7.28}
    for name, (base, spread) in spreads.items():
        noise = np.random.default_rng([zlib.crc32(name.encode()), seed]).standard_normal(out[name].shape)
        drawn = base * np.exp(spread * noise) if base else spread * noise
        out[name] = jnp.asarray(drawn.astype(out[name].dtype))
    for name, factor in factors.items():
        out[name] = (out[name] * factor).astype(out[name].dtype)
    return out
```

```python
import math
from contextlib import ExitStack

import numpy as np

import concourse.bass as bass
from concourse import mybir

F32 = mybir.dt.float32
F32R = mybir.dt.float32r
I32 = mybir.dt.int32
ALU = mybir.AluOpType
ACT = mybir.ActivationFunctionType
AX_X = mybir.AxisListType.X

P = 128
D = 1024
KD = D // P
SEQ = 1024
DB, DT = 8, 8
TS = DB * DT
CH, NCH = 364, 3
TOK = CH * NCH
NT = 9
HD = 64
AH, AG = 8, 2
REP = AH // AG
IH, IDX = 8, 64
NG, BH = 3, 4
WIN, DIL = (128, 512, 2048), (1, 4, 16)
BW = BH * HD
PAST, PAGE = 256, 128
NPAGE = PAST // PAGE
WL = tuple(min(w, PAST) for w in WIN)
TOPK = min(256, SEQ // 4)
STOPK = min(256, (PAST + DT) // 4)
SKEYS = PAST + DT
NBUCKET, MAXDIST = 32, 2048
NBH = AH + NG * BH
FF = 4 * D
FBLK = 1024
CONVW = 4
EPS = 1e-6
NEG = -1e30
SENT = -3.0e38
HUGE = 3.0e38
LRU_C = 8.0

PROJ_W = AH * HD + 2 * AG * HD + NG * 3 * BW
GROUPS = [("kiwi", 72, None), ("qi", 512, None), ("qa", 512, 0), ("kva", 256, 512)]
for _g in range(NG):
    GROUPS += [(f"qk{_g}", 512, 768 + 768 * _g), (f"v{_g}", 256, 768 + 768 * _g + 512)]
GOFF = [sum(g[1] for g in GROUPS[:i]) for i in range(len(GROUPS) + 1)]
IN_W = GOFF[-1]
N_GAIN = 2 + 2 * NG

TAB_A = SEQ + P
TAB_B = 384
TAB_S = tuple(-(-(wl + 15) // 16) * 16 for wl in WL)
TAB_OFF_B = [TAB_A + TAB_B * g for g in range(NG)]
TAB_OFF_S = [TAB_A + TAB_B * NG + sum(TAB_S[:g]) for g in range(NG)]
NTAB = TAB_A + TAB_B * NG + sum(TAB_S)


def bucket(dist):
    half = NBUCKET // 2
    d = np.maximum(dist, 0)
    df = np.maximum(d, 1).astype(np.float32)
    large = half + (np.log(df / np.float32(half)) / np.float32(math.log(MAXDIST / half))
                    * np.float32(NBUCKET - half)).astype(np.int32)
    return np.where(d < half, d, np.minimum(large, NBUCKET - 1))


def bias_selector():
    cols = np.zeros((NBUCKET + 1, NTAB), np.float32)

    def put(off, dist, ok):
        b = bucket(dist)
        for i in range(len(dist)):
            if ok[i]:
                cols[b[i], off + i] = 1.0
            else:
                cols[NBUCKET, off + i] = NEG

    d = SEQ - 1 - np.arange(TAB_A)
    put(0, d, d >= 0)
    for g in range(NG):
        s = 255 - np.arange(TAB_B)
        put(TAB_OFF_B[g], s * DIL[g], (s >= 0) & (s <= P))
        d = WL[g] + 7 - np.arange(TAB_S[g])
        put(TAB_OFF_S[g], d, (d >= 0) & (d <= WIN[g]) & (d % DIL[g] == 0))
    return cols


def tile_col(i):
    return 0 if i == 0 else TS + P * (i - 1)


def tile_rows(i):
    return TS if i == 0 else P


SEL_TILES = list(range(2, 8))
WORK_OFF = {}
_o = 0
for _j in SEL_TILES:
    WORK_OFF[_j] = _o
    _o += P * (_j + 1)
WORK_W = _o


def build_program(nc, a, o):
    def dram(name, *shape):
        return nc.dram_tensor(name, shape, F32).ap()

    proj = dram("proj_rows", TS + SEQ, PROJ_W)
    kiwi = dram("kiwi_rows", TS + SEQ, 72)
    table = dram("bias_rows", NBH, NTAB)
    strips = dram("bias_strips", AH, P, SEQ)
    wstrips = dram("window_strips", NG * BH, P, 2 * P)
    smask = dram("sample_mask", TS, SKEYS)
    oa = dram("sparse_rows", TS + SEQ, AH * HD)
    obp = [dram(f"window_rows{g}", TS + SEQ, OBW) for g in range(NG)]
    oas = dram("sample_sparse_rows", DB // 2, P, P)
    obs = dram("sample_window_rows", NG, DB // 4, P, OBW)
    with ExitStack() as ctx:
        ident = ctx.enter_context(nc.sbuf_tensor("ident", [P, P], F32))
        with ExitStack() as c1:
            work = c1.enter_context(nc.sbuf_tensor("select_work", [P, WORK_W], F32))
            with ExitStack() as c2:
                xh = c2.enter_context(nc.sbuf_tensor("x_high", [P, KD, TOK], F32R))
                xl = c2.enter_context(nc.sbuf_tensor("x_low", [P, KD, TOK], F32R))
                rstd = c2.enter_context(nc.sbuf_tensor("rstd_rows", [P, NT], F32))
                stage_start(nc, a, xh, xl, rstd, ident, table)
                stage_project(nc, a, xh, xl, rstd, ident, work, proj, kiwi, smask, table, strips, wstrips)
            stage_sparse(nc, a, o, ident, work, proj, kiwi, strips, oa)
        stage_window(nc, a, ident, proj, wstrips, obp)
        stage_sample(nc, a, ident, proj, table, smask, oas, obs)
        d = Dense(nc, ctx, a)
        with ExitStack() as c1:
            oth = c1.enter_context(nc.sbuf_tensor("mixed_high", [P, 6, NCH, CH], F32R))
            otl = c1.enter_context(nc.sbuf_tensor("mixed_low", [P, 6, NCH, CH], F32R))
            stage_merge(nc, a, ident, oa, obp, oas, obs, oth[:, :, :, :].rearrange("p k c n -> p k (c n)"),
                        otl[:, :, :, :].rearrange("p k c n -> p k (c n)"))
            stage_out_projection(nc, a, d, oth, otl)
        stage_mlp(nc, a, d, 0, 0)
        stage_recurrent(nc, a, d, 1, o["state_out"])
        stage_mlp(nc, a, d, 1, 2, o["y_t"])


def stage_start(nc, a, xh, xl, rstd, ident, table):
    with ExitStack() as ctx:
        def sb(name, shape, dt=F32):
            return ctx.enter_context(nc.sbuf_tensor(name, shape, dt))

        def sem(name):
            return ctx.enter_context(nc.semaphore(name))

        xraw = sb("s0_x", [P, 2, TOK])
        xv = sb("s0_xg", [P, 2, TOK])
        sq = sb("s0_sq", [P, 2, TOK])
        ssum = sb("s0_sum", [P, TOK])
        gain = sb("s0_gain", [P, KD])
        ones = sb("s0_ones", [P, 2])
        relb = sb("s0_relb", [NBUCKET + 1, NBH])
        pick = sb("s0_pick", [NBUCKET + 1, NTAB])
        tab = sb("s0_tab", [NBH, NTAB])
        ms = sb("s0_ms", [P, 2, NT])
        ps_t = [ctx.enter_context(nc.psum_tensor(f"s0_ps{i}", [P, 512], F32)) for i in range(7)]
        NTC = -(-NTAB // 512)
        assert NTC <= 6
        x_in = [sem(f"s0_x_in{i}") for i in range(2)]
        gain_in, tab_in = sem("s0_gain_in"), sem("s0_tab_in")
        high, squared, scaled, low, summed = (sem(f"s0_{n}") for n in ("high", "squared", "scaled", "low", "summed"))
        filled, tab_mm, tab_sb, tab_out = (sem(f"s0_{n}") for n in ("filled", "tab_mm", "tab_sb", "tab_out"))
        sum_mm, ms_dve, root = (sem(f"s0_{n}") for n in ("sum_mm", "ms_dve", "root"))
        block = ctx.enter_context(nc.Block())

        @block.sync
        def _(sp):
            sp.dma_start(gain[:, :], a["norm_mix0"]).then_inc(gain_in, 16)
            for k in range(KD):
                if k >= 2:
                    sp.wait_ge(squared, k - 1)
                    sp.wait_ge(scaled, k - 1)
                sp.dma_start(xraw[:, k % 2, :], a["xt"][k]).then_inc(x_in[k % 2], 16)
                if k == 1:
                    sp.wait_ge(filled, 1)
                    sp.dma_start(relb[0:NBUCKET, :], a["rel_bias"]).then_inc(tab_in, 16)
                    sp.dma_start(pick[:, :], a["bias_pick"]).then_inc(tab_in, 16)
            sp.wait_ge(tab_sb, NTC)
            sp.dma_start(table, tab[:, :]).then_inc(tab_out, 16)
            sp.wait_ge(tab_out, 16)

        @block.gpsimd
        def _(pool):
            nc.gpsimd.memset(relb[:, :], 1.0).then_inc(filled, 1)
            nc.gpsimd.memset(ones[:, :], 1.0).then_inc(filled, 1)
            nc.gpsimd.memset(ident[:, :], 0.0).then_inc(filled, 1)
            pool.wait_ge(filled, 3)
            nc.gpsimd.affine_select(out=ident[:, :], in_=ident[:, :], compare_op=ALU.not_equal, fill=1.0,
                                    base=0, pattern=[[-1, P]], channel_multiplier=1).then_inc(filled, 1)
            for k in range(KD):
                pool.wait_ge(squared, k + 1)
                if k == 0:
                    continue
                if k >= 2:
                    pool.wait_ge(summed, k - 1)
                first = sq[:, 0, :] if k == 1 else ssum[:, :]
                nc.gpsimd.tensor_tensor(ssum[:, :], first, sq[:, k % 2, :], ALU.add).then_inc(summed, 1)

        @block.scalar
        def _(act):
            act.wait_ge(gain_in, 16)
            for k in range(KD):
                act.wait_ge(x_in[k % 2], 16 * (k // 2 + 1))
                nc.scalar.activation(xh[:, k, :], xraw[:, k % 2, :], ACT.Copy, scale=gain[:, k:k + 1]).then_inc(high, 1)
                if k >= 2:
                    act.wait_ge(summed, k - 1)
                nc.scalar.activation(sq[:, k % 2, :], xraw[:, k % 2, :], ACT.Square).then_inc(squared, 1)
            for c in range(NTC):
                w = min(512, NTAB - 512 * c)
                act.wait_ge(tab_mm, c + 1)
                nc.scalar.activation(tab[:, 512 * c:512 * c + w], ps_t[c][0:NBH, 0:w], ACT.Copy).then_inc(tab_sb, 1)
            act.wait_ge(ms_dve, 1)
            nc.scalar.activation(ms[:, 1, :], ms[:, 0, :], ACT.Sqrt).then_inc(root, 1)

        @block.vector
        def _(dve):
            dve.wait_ge(gain_in, 16)
            for k in range(KD):
                dve.wait_ge(x_in[k % 2], 16 * (k // 2 + 1))
                if k >= 2:
                    dve.wait_ge(low, k - 1)
                nc.vector.tensor_scalar(xv[:, k % 2, :], xraw[:, k % 2, :], gain[:, k:k + 1], None, ALU.mult).then_inc(scaled, 1)
                dve.wait_ge(high, k + 1)
                dve.wait_ge(scaled, k + 1)
                nc.vector.tensor_tensor(xl[:, k, :], xv[:, k % 2, :], xh[:, k, :].bitcast(F32), ALU.subtract).then_inc(low, 1)
            dve.wait_ge(sum_mm, 1)
            nc.vector.tensor_scalar(ms[:, 0, :], ps_t[6][:, 0:NT], 1.0 / D, EPS, ALU.mult, ALU.add).then_inc(ms_dve, 1)
            dve.wait_ge(root, 1)
            nc.vector.reciprocal(rstd[:, :], ms[:, 1, :]).then_inc(ms_dve, 1)

        @block.tensor
        def _(pe):
            pe.wait_ge(filled, 4)
            pe.wait_ge(tab_in, 32)
            for c in range(NTC):
                w = min(512, NTAB - 512 * c)
                nc.tensor.matmul(ps_t[c][0:NBH, 0:w], relb[:, :], pick[:, 512 * c:512 * c + w],
                                 start=True, stop=True).then_inc(tab_mm, 1)
            pe.wait_ge(summed, KD - 1)
            for i in range(NT):
                c0 = tile_col(i)
                last = nc.tensor.matmul(ps_t[6][:, i:i + 1], ssum[:, c0:c0 + P], ones[:, 0:1], start=True, stop=True)
            last.then_inc(sum_mm, 1)


def stage_project(nc, a, xh, xl, rstd, ident, work, proj, kiwi, smask, table, strips, wstrips):
    NGR = len(GROUPS)
    SELS = [(j, h) for j in SEL_TILES for h in range(IH)]
    ROUNDS = [(j, r) for j in SEL_TILES for r in range(TOPK // 8)]
    SR = STOPK // 8
    SREST = STOPK % 8
    SPAD = 8 - SREST
    with ExitStack() as ctx:
        def sb(name, shape, dt=F32):
            return ctx.enter_context(nc.sbuf_tensor(name, shape, dt))

        def sem(name):
            return ctx.enter_context(nc.semaphore("p1_" + name))

        NST = 3
        wh = [sb(f"w_high{i}", [P, KD, 512], F32R) for i in range(2)]
        wl = [sb(f"w_low{i}", [P, KD, 512], F32R) for i in range(2)]
        wraw = sb("w_raw", [P, 2, 512])
        st = sb("rows", [P, NST, 512])
        sqr = sb("rows_sq", [P, 2, 512])
        gains = sb("gain_rows", [P, N_GAIN, HD])
        hs = sb("head_sums", [P, 2, 8])
        hm = sb("head_means", [P, 2, 8])
        hr = sb("head_roots", [P, 2, 8])
        hi = sb("head_inverse", [P, 2, 8])
        kk = sb("kiwi_sb", [P, NT, 136])
        wsc = sb("index_weights", [P, NT, 8])
        kit = sb("index_keys_t", [P, TS + SEQ])
        qt = sb("index_queries_t", [P, 2, 512])
        qst = sb("sample_queries_t", [HD, DB, IH * DT])
        rl = sb("relu_scores", [P, 2, SEQ])
        kpt = sb("page_keys_t", [HD, DB * NPAGE, PAGE])
        wks = sb("sample_work", [TS, SKEYS + SPAD])
        m8 = sb("top8", [P, 8])
        wt = sb("sample_w_t", [TS, DB])
        wts = sb("sample_w_scaled", [TS, DB])
        wb = sb("sample_w_blocks", [TS, DB, TS])
        same = sb("same_mask", [TS, DT])
        late = sb("later_mask", [TS, DT])
        pt = sb("pages", [1, DB * NPAGE], I32)
        ps = [ctx.enter_context(nc.psum_tensor(f"proj_ps{i}", [P, 512], F32)) for i in range(3)]
        pss = [ctx.enter_context(nc.psum_tensor(f"score_ps{i}", [P, 1024], F32)) for i in range(2)]
        psx = ctx.enter_context(nc.psum_tensor("turn_ps", [P, 512], F32))

        names = ("w_high w_low proj copied squared summed meaned rooted inverted normed gained "
                 "small_in pages_in keys_in kiwi_copied kiwi_out wt_in w_scaled turned turn_taken "
                 "scored relued added masked topk wt_ready zeroed s_mixed s_taken mask_out strips_out").split()
        S = {n: sem(n) for n in names}
        stored = [sem(f"stored{i}") for i in range(NST)]
        w_in = [sem(f"w_in{i}") for i in range(2)]
        block = ctx.enter_context(nc.Block())

        def width(gi):
            return GROUPS[gi][1]

        def rows_n(gi, i):
            return NT * (gi - 1) + i

        def kinds(gi):
            name = GROUPS[gi][0]
            if name == "qa":
                return [(0, 8, 0, True)]
            if name == "kva":
                return [(0, AG, 1, False)]
            if name[:2] == "qk":
                g = int(name[2])
                return [(0, BH, 2 + 2 * g, True), (BH, BH, 3 + 2 * g, False)]
            return []

        NORMED = [(gi, i) for gi in range(NGR) if kinds(gi) for i in range(NT)]
        NORM_AT = {x: n for n, x in enumerate(NORMED)}
        GAIN_OPS = {x: sum(len(kinds(y[0])) for y in NORMED[:n + 1]) for n, x in enumerate(NORMED)}
        TURN_Q = {0: 4, **{j: 5 + n for n, j in enumerate(SEL_TILES)}}

        TURN_ROWS = {0: TURN_Q[0], **{j + 1: TURN_Q[j] for j in SEL_TILES}}
        KEY_TURNS = [(0, TS + 3 * P), (TS + 3 * P, TS + 7 * P), (TS + 7 * P, TS + 8 * P)]

        @block.sync
        def _(sp):
            sp.dma_start(pt[:, :], a["page_table"]).then_inc(S["pages_in"], 16)
            sp.dma_start(gains[:, :, :], a["head_gains"].partition_broadcast(P)).then_inc(S["small_in"], 16)
            sp.dma_start(same[:, :], a["same_step"]).then_inc(S["small_in"], 16)
            sp.dma_start(late[:, :], a["later_step"]).then_inc(S["small_in"], 16)

            def load_w(gi, k):
                u = KD * gi + k
                if u >= 2:
                    sp.wait_ge(S["w_low"], u - 1)
                sp.dma_start(wraw[:, u % 2, 0:width(gi)],
                             a["w_in"][k, :, GOFF[gi]:GOFF[gi + 1]]).then_inc(w_in[u % 2], 16)

            for k in range(KD):
                load_w(0, k)
            sp.wait_ge(S["pages_in"], 16)
            for n in range(DB * NPAGE):
                page = sp.value_load(pt[0:1, n:n + 1], min_val=0, max_val=a["kidx_t"].shape[0] - 1)
                sp.dma_start(kpt[:, n, :], a["kidx_t"][bass.ds(page, 1), :, :].rearrange("o d n -> d (o n)")
                             ).then_inc(S["keys_in"], 16)
            def store(gi, i):
                r, c = tile_rows(i), tile_col(i)
                n = rows_n(gi, i)
                if kinds(gi):
                    sp.wait_ge(S["gained"], GAIN_OPS[gi, i])
                sp.wait_ge(S["copied"], n + 1)
                off = GROUPS[gi][2]
                sp.dma_start(proj[c:c + r, off:off + width(gi)], st[0:r, n % NST, 0:width(gi)]
                             ).then_inc(stored[n % NST], 16)

            shifts = [(strips[h:h + 2], h * NTAB, 2, SEQ) for h in range(0, AH, 2)]
            shifts += [(wstrips[BH * g:BH * (g + 1)], (AH + BH * g) * NTAB + TAB_OFF_B[g], BH, 2 * P) for g in range(NG)]
            steps = [(gi, i) for gi in range(NGR) for i in range(NT)]
            for x, (gi, i) in enumerate(steps):
                if gi == 1 and i < len(shifts):
                    dst, off, nh, w = shifts[i]
                    sp.dma_start(dst, bass.AP(tensor=table.tensor, offset=off + P - 1, ap=[[NTAB, nh], [-1, P], [1, w]])
                                 ).then_inc(S["strips_out"], 16)
                if gi + 1 < NGR and i < KD:
                    load_w(gi + 1, i)
                if gi == 0:
                    r, c = tile_rows(i), tile_col(i)
                    sp.wait_ge(S["kiwi_copied"], i + 1)
                    sp.dma_start(kiwi[c:c + r, :], kk[0:r, i, 64:136]).then_inc(S["kiwi_out"], 16)
                    if i == 1:
                        sp.wait_ge(S["kiwi_out"], 16 * 2)
                        for h in range(IH):
                            src = bass.AP(tensor=kiwi.tensor, offset=64 + h, ap=[[72, DT], [72 * DT, DB]])
                            with nc.allow_non_contiguous_dma(reason="512 words, once"):
                                sp.dma_start(wt[DT * h:DT * h + DT, :], src).then_inc(S["wt_in"], 16)
                if steps[x - 2][0] >= 2 and x >= 2:
                    store(*steps[x - 2])
            store(*steps[-2])
            store(*steps[-1])
            sp.wait_ge(S["topk"], 2 * SR + 2 * (SREST > 0) + 1)
            sp.dma_start(smask, wks[:, 0:SKEYS]).then_inc(S["mask_out"], 16)
            sp.wait_ge(S["mask_out"], 16)
            sp.wait_ge(S["strips_out"], 16 * len(shifts))
            for q in range(NST):
                sp.wait_ge(stored[q], 16 * len([n for n in range(NT, NT * (NGR - 1)) if n % NST == q]))
            sp.wait_ge(S["kiwi_out"], 16 * NT)

        def split_unit_low(pool, gi, k):
            u = KD * gi + k
            w = width(gi)
            pool.wait_ge(S["w_high"], u + 1)
            if k == 0 and gi >= 2:
                pool.wait_ge(S["proj"], NT * (gi - 1))
            nc.gpsimd.tensor_tensor(wl[gi % 2][:, k, 0:w], wraw[:, u % 2, 0:w],
                                    wh[gi % 2][:, k, 0:w].bitcast(F32), ALU.subtract).then_inc(S["w_low"], 1)

        @block.gpsimd
        def _(pool):
            for k in range(KD):
                split_unit_low(pool, 0, k)
            pool.wait_ge(S["small_in"], 48)
            for gi in range(NGR):
                for i in range(NT):
                    if gi + 1 < NGR and i < KD:
                        split_unit_low(pool, gi + 1, i)
                    for h0, hn, row, _ in kinds(gi):
                        n = rows_n(gi, i)
                        pool.wait_ge(S["normed"], NORM_AT[gi, i] + 1)
                        v = st[:, n % NST, HD * h0:HD * (h0 + hn)].rearrange("p (h d) -> p h d", h=hn)
                        nc.gpsimd.tensor_tensor(v, v, gains[:, row:row + 1, :].broadcast_to([P, hn, HD]),
                                                ALU.mult).then_inc(S["gained"], 1)
                if gi == 1:
                    for n, j in enumerate(SEL_TILES):
                        pool.wait_ge(S["added"], IH * (n + 1))
                        v = work[:, WORK_OFF[j] + P * j:WORK_OFF[j] + P * (j + 1)]
                        nc.gpsimd.affine_select(out=v, in_=v, compare_op=ALU.is_ge, fill=NEG, base=0,
                                                pattern=[[-1, P]], channel_multiplier=1).then_inc(S["masked"], 1)

        def take_turn(act, j):
            act.wait_ge(S["turned"], TURN_Q[j])
            if j - 2 in SEL_TILES:
                act.wait_ge(S["scored"], SELS.index((j - 2, IH - 1)) + 1)
            nc.scalar.activation(qt[:, j % 2, :], psx[:, :], ACT.Copy).then_inc(S["turn_taken"], 1)

        @block.scalar
        def _(act):
            def relu(s):
                j, h = SELS[s]
                w = P * (j + 1)
                act.wait_ge(S["scored"], s + 1)
                if s >= 2:
                    act.wait_ge(S["added"], s - 1)
                nc.scalar.activation(rl[:, s % 2, 0:w], pss[s % 2][:, 0:w], ACT.Relu).then_inc(S["relued"], 1)

            def root(gi, i):
                m = NORM_AT[gi, i]
                act.wait_ge(S["meaned"], sum(len(kinds(y[0])) for y in NORMED[:m + 1]))
                if m >= 2:
                    act.wait_ge(S["inverted"], m - 1)
                nh = sum(x[1] for x in kinds(gi))
                nc.scalar.activation(hr[:, m % 2, 0:nh], hm[:, m % 2, 0:nh], ACT.Sqrt).then_inc(S["rooted"], 1)

            pending = None
            for gi in range(NGR):
                for i in range(NT):
                    p = NT * gi + i
                    w = width(gi)
                    act.wait_ge(S["proj"], p + 1)
                    if gi == 0:
                        nc.scalar.activation(kk[:, i, 0:64], ps[p % 3][:, 0:64], ACT.Copy, scale=rstd[:, i:i + 1])
                        nc.scalar.activation(kk[:, i, 64:136], ps[p % 3][:, 0:72], ACT.Copy,
                                             scale=rstd[:, i:i + 1]).then_inc(S["kiwi_copied"], 1)
                        continue
                    n = rows_n(gi, i)
                    if n >= NST:
                        if gi >= 2 and n - NST >= NT:
                            act.wait_ge(stored[n % NST], 16 * ((n - NT) // NST))
                        elif n - NST in TURN_ROWS:
                            act.wait_ge(S["turned"], TURN_ROWS[n - NST])
                        else:
                            act.wait_ge(S["copied"], n - NST + 1)
                    nc.scalar.activation(st[:, n % NST, 0:w], ps[p % 3][:, 0:w], ACT.Copy,
                                         scale=rstd[:, i:i + 1]).then_inc(S["copied"], 1)
                    if gi == 1:
                        if i == 0:
                            for t, (x0, x1) in enumerate(KEY_TURNS):
                                act.wait_ge(S["turned"], t + 1)
                                nc.scalar.activation(kit[:, x0:x1], psx[:, 0:x1 - x0], ACT.Copy).then_inc(S["turn_taken"], 1)
                        if i == 1:
                            act.wait_ge(S["turned"], TURN_Q[0])
                            nc.scalar.activation(
                                qst[:, :, :].rearrange("d b (h t) -> d h b t", t=DT),
                                psx[0:HD, :].rearrange("d (h b t) -> d h b t", h=IH, t=DT), ACT.Copy).then_inc(S["turn_taken"], 1)
                        if i - 2 in TURN_Q and i >= 4:
                            take_turn(act, i - 2)
                        if i - 3 in TURN_Q and i >= 5:
                            for h in range(IH):
                                relu(SELS.index((i - 3, h)))
                    if kinds(gi):
                        m = NORM_AT[gi, i]
                        if m >= 2:
                            act.wait_ge(S["summed"], m - 1)
                        act.wait_ge(S["copied"], n + 1)
                        nh = sum(x[1] for x in kinds(gi))
                        nc.scalar.activation(sqr[:, m % 2, 0:HD * nh], st[:, n % NST, 0:HD * nh],
                                             ACT.Square).then_inc(S["squared"], 1)
                        if pending:
                            root(*pending)
                        pending = (gi, i)
                    elif pending:
                        root(*pending)
                        pending = None
                if gi == 1:
                    take_turn(act, 7)
                    for j in (6, 7):
                        for h in range(IH):
                            relu(SELS.index((j, h)))
                    for b in range(DB):
                        s = len(SELS) + b
                        act.wait_ge(S["scored"], s + 1)
                        if b < 2:
                            act.wait_ge(S["added"], s - 1)
                        else:
                            act.wait_ge(S["s_mixed"], b - 1)
                        nc.scalar.activation(rl[0:TS, s % 2, 0:SKEYS], pss[s % 2][0:TS, 0:SKEYS],
                                             ACT.Relu).then_inc(S["relued"], 1)
            if pending:
                root(*pending)

        @block.tensor
        def _(pe):
            def project(gi, i):
                p = NT * gi + i
                w, c = width(gi), tile_col(i)
                if i == 0:
                    pe.wait_ge(S["w_low"], KD * (gi + 1))
                if p >= 3:
                    q = p - 3
                    if q < NT:
                        pe.wait_ge(S["kiwi_copied"], q + 1)
                    else:
                        pe.wait_ge(S["copied"], q - NT + 1)
                passes = [(x, y, k) for k in range(KD) for x, y in ((xh, wh), (xh, wl), (xl, wh))]
                for n, (x, y, k) in enumerate(passes):
                    last = nc.tensor.matmul(ps[p % 3][:, 0:w], x[:, k, c:c + P], y[gi % 2][:, k, 0:w],
                                            start=(n == 0), stop=(n == len(passes) - 1))
                last.then_inc(S["proj"], 1)

            def turn_free(t):
                if t > 1:
                    pe.wait_ge(S["turn_taken"], t - 1)

            def turn_queries(j):
                pe.wait_ge(S["copied"], (0 if j == 0 else j + 1) + 1)
                turn_free(TURN_Q[j])
                if j == 0:
                    for h in range(IH):
                        last = nc.tensor.transpose(psx[0:HD, TS * h:TS * h + TS], st[0:TS, 0, HD * h:HD * h + HD],
                                                   ident[0:TS, 0:TS])
                else:
                    for q in range(4):
                        last = nc.tensor.transpose(psx[:, P * q:P * q + P], st[:, (j + 1) % NST, P * q:P * q + P],
                                                   ident[:, :])
                last.then_inc(S["turned"], 1)

            def scores(j):
                pe.wait_ge(S["turn_taken"], TURN_Q[j])
                w = P * (j + 1)
                for h in range(IH):
                    s = SELS.index((j, h))
                    b = 64 * (h % 2)
                    if s >= 2:
                        pe.wait_ge(S["relued"], s - 1)
                    for x in range(0, w, 512):
                        y = min(512, w - x)
                        last = nc.tensor.matmul(pss[s % 2][:, x:x + y],
                                                qt[b:b + HD, j % 2, P * (h // 2):P * (h // 2) + P],
                                                kit[b:b + HD, TS + x:TS + x + y], start=True, stop=True)
                    last.then_inc(S["scored"], 1)

            for i in range(NT):
                project(0, i)
            project(1, 0)
            pe.wait_ge(S["kiwi_copied"], NT)
            for t, (x0, x1) in enumerate(KEY_TURNS):
                turn_free(t + 1)
                for i in range(NT):
                    if x0 <= tile_col(i) < x1:
                        r = tile_rows(i)
                        last = nc.tensor.transpose(psx[:, tile_col(i) - x0:tile_col(i) - x0 + r], kk[0:r, i, 0:P],
                                                   ident[0:r, 0:r])
                last.then_inc(S["turned"], 1)
            for i in range(1, NT):
                project(1, i)
                if i == 1:
                    turn_queries(0)
                if i - 2 in SEL_TILES:
                    turn_queries(i - 2)
                if i - 3 in SEL_TILES:
                    scores(i - 3)
            turn_queries(7)
            scores(6)
            scores(7)
            pe.wait_ge(S["keys_in"], 16 * DB * NPAGE)
            pe.wait_ge(S["wt_ready"], 1 + DB)

            def mix(b):
                s = len(SELS) + b
                pe.wait_ge(S["relued"], s + 1)
                nc.tensor.matmul(psx[0:TS, 0:SKEYS], wb[:, b, :], rl[0:TS, s % 2, 0:SKEYS],
                                 start=(b == 0), stop=(b == DB - 1)).then_inc(S["s_mixed"], 1)

            pe.wait_ge(S["turn_taken"], TURN_Q[7])
            for b in range(DB):
                s = len(SELS) + b
                pe.wait_ge(S["relued"], s - 1)
                for q in range(NPAGE):
                    nc.tensor.matmul(pss[s % 2][0:TS, PAGE * q:PAGE * (q + 1)], qst[:, b, :], kpt[:, NPAGE * b + q, :],
                                     start=True, stop=True)
                nc.tensor.matmul(pss[s % 2][0:TS, PAST:SKEYS], qst[:, b, :], kit[0:HD, DT * b:DT * (b + 1)],
                                 start=True, stop=True).then_inc(S["scored"], 1)
                if b:
                    mix(b - 1)
            mix(DB - 1)
            for gi in range(2, NGR):
                for i in range(NT):
                    project(gi, i)

        @block.vector
        def _(dve):
            tk = [0]

            def link(ins):
                tk[0] += 1
                ins.then_inc(S["topk"], 1)
                dve.wait_ge(S["topk"], tk[0])

            def split_high(gi, k):
                u = KD * gi + k
                w = width(gi)
                dve.wait_ge(w_in[u % 2], 16 * (u // 2 + 1))
                if k == 0 and gi >= 2:
                    dve.wait_ge(S["proj"], NT * (gi - 1))
                nc.vector.tensor_copy(wh[gi % 2][:, k, 0:w], wraw[:, u % 2, 0:w]).then_inc(S["w_high"], 1)

            def add_scores(j):
                w = P * (j + 1)
                v = work[:, WORK_OFF[j]:WORK_OFF[j] + w]
                for h in range(IH):
                    s = SELS.index((j, h))
                    dve.wait_ge(S["relued"], s + 1)
                    if h == 0:
                        nc.vector.tensor_scalar(v, rl[:, s % 2, 0:w], wsc[:, j + 1, 0:1], None, ALU.mult).then_inc(S["added"], 1)
                    else:
                        dve.wait_ge(S["added"], s)
                        nc.vector.scalar_tensor_tensor(out=v, in0=rl[:, s % 2, 0:w], scalar=wsc[:, j + 1, h:h + 1], in1=v,
                                                       op0=ALU.mult, op1=ALU.add).then_inc(S["added"], 1)

            def norm_sum(gi, i):
                m = NORM_AT[gi, i]
                nh = sum(x[1] for x in kinds(gi))
                dve.wait_ge(S["squared"], m + 1)
                if m >= 2:
                    dve.wait_ge(S["rooted"], m - 1)
                nc.vector.reduce_sum(hs[:, m % 2, 0:nh], sqr[:, m % 2, 0:HD * nh].rearrange("p (h d) -> p h d", h=nh),
                                     AX_X).then_inc(S["summed"], 1)
                dve.wait_ge(S["summed"], m + 1)
                for h0, hn, _, query in kinds(gi):
                    f = 1.0 if query else 1.0 / HD
                    nc.vector.tensor_scalar(hm[:, m % 2, h0:h0 + hn], hs[:, m % 2, h0:h0 + hn], f, EPS * HD * f,
                                            ALU.mult, ALU.add).then_inc(S["meaned"], 1)

            def norm_apply(gi, i):
                m, n = NORM_AT[gi, i], rows_n(gi, i)
                nh = sum(x[1] for x in kinds(gi))
                dve.wait_ge(S["rooted"], m + 1)
                nc.vector.reciprocal(hi[:, m % 2, 0:nh], hr[:, m % 2, 0:nh]).then_inc(S["inverted"], 1)
                dve.wait_ge(S["inverted"], m + 1)
                v = st[:, n % NST, 0:HD * nh].rearrange("p (h d) -> p h d", h=nh)
                r = hi[:, m % 2, 0:nh].rearrange("p (h o) -> p h o", o=1).broadcast_to([P, nh, HD])
                nc.vector.tensor_tensor(v, v, r, ALU.mult).then_inc(S["normed"], 1)

            def topk_round(n):
                j, r = ROUNDS[n]
                v = work[:, WORK_OFF[j]:WORK_OFF[j] + P * (j + 1)]
                if r == 0:
                    dve.wait_ge(S["masked"], SEL_TILES.index(j) + 1)
                link(nc.vector.max(m8[:, :], v))
                link(nc.vector.match_replace(v, m8[:, :], v, SENT))
                if r == TOPK // 8 - 1:
                    link(nc.vector.tensor_scalar(v, v, SENT, NEG, ALU.not_equal, ALU.mult))

            def topk_sample():
                for r in range(SR):
                    link(nc.vector.max(m8[0:TS, :], wks[:, 0:SKEYS]))
                    link(nc.vector.match_replace(wks[:, 0:SKEYS], m8[0:TS, :], wks[:, 0:SKEYS], SENT))
                if SREST:
                    link(nc.vector.max(m8[0:TS, :], wks[:, :]))
                    link(nc.vector.match_replace(wks[:, :], m8[0:TS, :], wks[:, :], SENT))
                link(nc.vector.tensor_scalar(wks[:, 0:SKEYS], wks[:, 0:SKEYS], SENT, NEG, ALU.not_equal, ALU.mult))

            for k in range(KD):
                split_high(0, k)
            for k in range(KD):
                split_high(1, k)
            nc.vector.memset(wb[:, :, :], 0.0).then_inc(S["zeroed"], 1)
            nc.vector.memset(wks[:, SKEYS:SKEYS + SPAD], HUGE).then_inc(S["zeroed"], 1)
            dve.wait_ge(S["kiwi_copied"], NT)
            nc.vector.tensor_scalar(wsc[:, :, :], kk[:, :, 128:136], IH ** -0.5, HD ** -0.5, ALU.mult, ALU.mult).then_inc(S["w_scaled"], 1)
            dve.wait_ge(S["wt_in"], 16 * IH)
            nc.vector.tensor_scalar(wts[:, :], wt[:, :], IH ** -0.5, HD ** -0.5, ALU.mult, ALU.mult).then_inc(S["wt_ready"], 1)
            dve.wait_ge(S["small_in"], 48)
            dve.wait_ge(S["wt_ready"], 1)
            dve.wait_ge(S["zeroed"], 2)
            for b in range(DB):
                nc.vector.tensor_scalar(wb[:, b, DT * b:DT * (b + 1)], same[:, :], wts[:, b:b + 1], None,
                                        ALU.mult).then_inc(S["wt_ready"], 1)
            dve.wait_ge(S["w_scaled"], 1)
            for k in range(KD):
                if k < 2:
                    split_high(2, k)
            for j in SEL_TILES:
                add_scores(j)
                if j < 7:
                    split_high(2, j)
            split_high(2, 7)
            dve.wait_ge(S["s_mixed"], DB)
            nc.vector.tensor_copy(wks[:, 0:SKEYS], psx[0:TS, 0:SKEYS]).then_inc(S["s_taken"], 1)
            dve.wait_ge(S["s_taken"], 1)
            nc.vector.tensor_tensor(wks[:, PAST:SKEYS], wks[:, PAST:SKEYS], late[:, :], ALU.add).then_inc(S["s_taken"], 1)
            dve.wait_ge(S["s_taken"], 2)
            topk_sample()
            steps = [(gi, i) for gi in range(2, NGR) for i in range(NT)]
            before, r0 = None, 0
            for n, (gi, i) in enumerate(steps):
                if gi + 1 < NGR and i < KD:
                    split_high(gi + 1, i)
                if kinds(gi):
                    norm_sum(gi, i)
                    if before:
                        norm_apply(*before)
                    before = (gi, i)
                elif before:
                    norm_apply(*before)
                    before = None
                r1 = len(ROUNDS) * (n + 1) // len(steps)
                for r in range(r0, r1):
                    topk_round(r)
                r0 = r1


def stage_sparse(nc, a, o, ident, work, proj, kiwi, strips, oa):
    used = sorted(int(s) for s in nc.released_uncleared_semaphores)
    assert used == list(range(used[0], used[0] + len(used)))
    ITEMS = [(j, h) for j in range(SEQ // P) for h in range(AH)]
    NI = len(ITEMS)
    LAST_J = SEQ // P - 1
    with ExitStack() as ctx:
        def sb(name, shape, dt=F32):
            return ctx.enter_context(nc.sbuf_tensor("sa_" + name, shape, dt))

        def sem(name):
            return ctx.enter_context(nc.semaphore("sa_" + name))

        strip = sb("bias_strip", [P, AH, SEQ])
        kr = sb("keys", [P, 8, P])
        v = sb("values", [P, 8, P])
        kt = sb("keys_t", [P, SEQ])
        q = sb("queries", [P, 2, 512])
        qt = sb("queries_t", [P, 2, 512])
        um = sb("bias_mask", [P, 2, SEQ])
        s = sb("scores", [P, 3, SEQ])
        pt = sb("probs_t", [P, 2, SEQ])
        mx = sb("row_max", [P, 4])
        nm = sb("neg_max", [P, 4])
        ls = sb("row_sum", [P, 2, AH])
        li = sb("inv_sum", [P, 2, AH])
        ob = sb("out_rows", [P, 2, 512])
        pss = [ctx.enter_context(nc.psum_tensor(f"sa_ps_s{i}", [P, SEQ], F32)) for i in range(2)]
        pst = [ctx.enter_context(nc.psum_tensor(f"sa_ps_t{i}", [P, 512], F32)) for i in range(2)]
        pso = ctx.enter_context(nc.psum_tensor("sa_ps_o", [P, 512], F32))
        psx = ctx.enter_context(nc.psum_tensor("sa_ps_x", [P, 512], F32))
        kv_in, strip_in, cache_out = sem("kv_in"), sem("strip_in"), sem("cache_out")
        caches = [(o["kv_a"], proj[:, 512:768]), (o["ki"], kiwi[:, 0:IDX])]
        for g in range(NG):
            wp, ws, c = min(WIN[g], SEQ), WL[g], 768 * (g + 1) + BW
            caches += [(o[f"p_win{g}"], proj[TS + SEQ - wp:TS + SEQ, c:c + 2 * BW]),
                       (o[f"s_win{g}"][:, 0:ws - DT, :], a[f"win_cache{g}"][:, DT:ws, :]),
                       (o[f"s_win{g}"][:, ws - DT:ws, :], proj[0:TS, c:c + 2 * BW].rearrange("(b t) c -> b t c", t=DT))]
        q_in = [sem(f"q_in{i}") for i in range(2)]
        o_out = [sem(f"o_out{i}") for i in range(2)]
        (turned, turn_taken, scored, masked, maxed, negated, exped, probs_turned, probs_taken, pv_done, inverted,
         normed) = (sem(n) for n in ("turned", "turn_taken", "scored", "masked", "maxed", "negated", "exped",
                                     "probs_turned", "probs_taken", "pv_done", "inverted", "normed"))
        block = ctx.enter_context(nc.Block())

        def units(t):
            return sum(-(-(j + 1) // 4) for j, _ in ITEMS[:t])

        UNITS = [units(t) for t in range(NI + 1)]
        MASKED = [t for t in range(NI) if ITEMS[t][0] in SEL_TILES]

        @block.sync
        def _(sp):
            rows = proj[TS:TS + SEQ, :].rearrange("(n p) c -> p n c", p=P)
            sp.dma_start(kr[:, :, :], rows[:, :, 512:640]).then_inc(kv_in, 16)

            def load_q(j):
                if j >= 2:
                    sp.wait_ge(turned, 2 + j - 1)
                dst = q[:, j % 2, :].rearrange("p (r g d) -> p g r d", r=REP, g=AG)
                for g in range(AG):
                    sp.dma_start(dst[:, g], proj[TS + P * j:TS + P * (j + 1), 256 * g:256 * (g + 1)].rearrange(
                        "p (r d) -> p r d", r=REP)).then_inc(q_in[j % 2], 16)

            load_q(0)
            for h in range(AH):
                sp.dma_start(strip[:, h, :], strips[h]).then_inc(strip_in, 16)
                if h == 0:
                    sp.dma_start(v[:, :, :], rows[:, :, 640:768]).then_inc(kv_in, 16)
            load_q(1)
            for dst, src in caches:
                sp.dma_start(dst, src).then_inc(cache_out, 16)
            for j in range(SEQ // P):
                sp.wait_ge(normed, j + 1)
                sp.dma_start(oa[TS + P * j:TS + P * (j + 1), :], ob[:, j % 2, :]).then_inc(o_out[j % 2], 16)
                if j + 2 <= LAST_J:
                    load_q(j + 2)
            for i in range(2):
                sp.wait_ge(o_out[i], 16 * 4)
            sp.wait_ge(cache_out, 16 * len(caches))

        @block.gpsimd
        def _(pool):
            nc.gpsimd.sem_clear(range(used[0], used[-1] + 1))
            pool.wait_ge(strip_in, 16 * AH)
            for m, t in enumerate(MASKED):
                j, h = ITEMS[t]
                w = P * (j + 1)
                if m >= 2:
                    pool.wait_ge(maxed, MASKED[m - 2] + 1)
                nc.gpsimd.tensor_tensor(um[:, m % 2, 0:w], strip[:, h, P * (7 - j):SEQ],
                                        work[:, WORK_OFF[j]:WORK_OFF[j] + w], ALU.add).then_inc(masked, 1)

        @block.scalar
        def _(act):
            def take_turn(n):
                act.wait_ge(turned, n + 1)
                if n < 2:
                    dst = kt[:, 512 * n:512 * (n + 1)]
                else:
                    j = n - 2
                    if j >= 2:
                        act.wait_ge(scored, AH * (j - 1))
                    dst = qt[:, j % 2, :]
                nc.scalar.activation(dst, psx[:, :], ACT.Copy).then_inc(turn_taken, 1)

            for n in range(3):
                take_turn(n)
            for t in range(NI + 1):
                if t < NI:
                    j, h = ITEMS[t]
                    w = P * (j + 1)
                    act.wait_ge(maxed, t + 1)
                    if t >= 4:
                        act.wait_ge(exped, t - 3)
                    nc.scalar.mul(nm[:, t % 4:t % 4 + 1], mx[:, t % 4:t % 4 + 1], -1.0).then_inc(negated, 1)
                    act.wait_ge(negated, t + 1)
                    if h == 0 and j >= 2:
                        act.wait_ge(inverted, j - 1)
                    nc.scalar.activation(s[:, t % 3, 0:w], s[:, t % 3, 0:w], ACT.Exp, bias=nm[:, t % 4:t % 4 + 1],
                                         accum_out=ls[:, j % 2, h:h + 1]).then_inc(exped, 1)
                if t >= 1:
                    j, h = ITEMS[t - 1]
                    if t - 1 >= 2:
                        act.wait_ge(pv_done, t - 2)
                    for u in range(UNITS[t - 1], UNITS[t]):
                        x = 512 * (u - UNITS[t - 1])
                        y = min(512, P * (j + 1) - x)
                        act.wait_ge(probs_turned, u + 1)
                        nc.scalar.activation(pt[:, (t - 1) % 2, x:x + y], pst[u % 2][:, 0:y], ACT.Copy).then_inc(probs_taken, 1)
                    if h == 5 and j < LAST_J:
                        take_turn(3 + j)

        @block.tensor
        def _(pe):
            def turn_keys(n):
                if n:
                    pe.wait_ge(turn_taken, n)
                for i in range(4):
                    last = nc.tensor.transpose(psx[:, P * i:P * (i + 1)], kr[:, 4 * n + i, :], ident[:, :])
                last.then_inc(turned, 1)

            def turn_queries(j):
                pe.wait_ge(q_in[j % 2], 32 * (j // 2 + 1))
                pe.wait_ge(turn_taken, 2 + j)
                for i in range(4):
                    last = nc.tensor.transpose(psx[:, P * i:P * (i + 1)], q[:, j % 2, P * i:P * (i + 1)], ident[:, :])
                last.then_inc(turned, 1)

            def scores(t):
                j, h = ITEMS[t]
                b, r, w = HD * (h // REP), h % REP, P * (j + 1)
                if h == 0:
                    pe.wait_ge(turn_taken, 3 + j)
                if t >= 2:
                    pe.wait_ge(maxed, t - 1)
                for x in range(0, w, 512):
                    y = min(512, w - x)
                    last = nc.tensor.matmul(pss[t % 2][:, x:x + y], qt[b:b + HD, j % 2, P * r:P * (r + 1)],
                                            kt[b:b + HD, x:x + y], start=True, stop=True)
                last.then_inc(scored, 1)

            def turn_probs(t):
                j, h = ITEMS[t]
                pe.wait_ge(exped, t + 1)
                for u in range(UNITS[t], UNITS[t + 1]):
                    if u >= 2:
                        pe.wait_ge(probs_taken, u - 1)
                    k0 = 4 * (u - UNITS[t])
                    for k in range(k0, min(k0 + 4, j + 1)):
                        last = nc.tensor.transpose(pst[u % 2][:, P * (k - k0):P * (k - k0 + 1)],
                                                   s[:, t % 3, P * k:P * (k + 1)], ident[:, :])
                    last.then_inc(probs_turned, 1)

            def outputs(t):
                j, h = ITEMS[t]
                pe.wait_ge(probs_taken, UNITS[t + 1])
                if h == 0 and j:
                    pe.wait_ge(normed, j)
                g = h // REP
                for k in range(j + 1):
                    last = nc.tensor.matmul(pso[:, HD * h:HD * (h + 1)], pt[:, t % 2, P * k:P * (k + 1)],
                                            v[:, k, HD * g:HD * (g + 1)], start=(k == 0), stop=(k == j))
                last.then_inc(pv_done, 1)

            pe.wait_ge(kv_in, 32)
            turn_keys(0)
            turn_keys(1)
            turn_queries(0)
            for t in range(NI + 2):
                if t < NI:
                    scores(t)
                if 1 <= t <= NI:
                    turn_probs(t - 1)
                    if ITEMS[t - 1][1] == 5 and ITEMS[t - 1][0] < LAST_J:
                        turn_queries(ITEMS[t - 1][0] + 1)
                if t >= 2:
                    outputs(t - 2)

        @block.vector
        def _(dve):
            dve.wait_ge(strip_in, 16 * AH)
            for t in range(NI + 2):
                if t < NI:
                    j, h = ITEMS[t]
                    w = P * (j + 1)
                    dve.wait_ge(scored, t + 1)
                    if t in MASKED:
                        m = MASKED.index(t)
                        dve.wait_ge(masked, m + 1)
                        add = um[:, m % 2, 0:w]
                    else:
                        add = strip[:, h, P * (7 - j):SEQ]
                    if t >= 3:
                        dve.wait_ge(probs_turned, UNITS[t - 2])
                    if t >= 4:
                        dve.wait_ge(negated, t - 3)
                    nc.vector.tensor_tensor_reduce(out=s[:, t % 3, 0:w], in0=pss[t % 2][:, 0:w], in1=add, scale=1.0,
                                                   scalar=NEG, op0=ALU.add, op1=ALU.max,
                                                   accum_out=mx[:, t % 4:t % 4 + 1]).then_inc(maxed, 1)
                if t >= 2 and ITEMS[t - 2][1] == AH - 1:
                    j = ITEMS[t - 2][0]
                    dve.wait_ge(pv_done, t - 1)
                    nc.vector.reciprocal(li[:, j % 2, :], ls[:, j % 2, :]).then_inc(inverted, 1)
                    dve.wait_ge(inverted, j + 1)
                    if j >= 2:
                        dve.wait_ge(o_out[j % 2], 16 * (j // 2))
                    nc.vector.tensor_tensor(
                        ob[:, j % 2, :].rearrange("p (h d) -> p h d", h=AH), pso[:, :].rearrange("p (h d) -> p h d", h=AH),
                        li[:, j % 2, :].rearrange("p (h o) -> p h o", o=1).broadcast_to([P, AH, HD]), ALU.mult
                    ).then_inc(normed, 1)


OBW = BW + 2 * BH


def stage_window(nc, a, ident, proj, wstrips, obp):
    JOBS = []
    for g in range(NG):
        d = DIL[g]
        n = SEQ // d
        if n >= P:
            JOBS += [(g, [(TS + c + d * P * i, P)], i > 0) for c in range(d) for i in range(n // P)]
        else:
            JOBS += [(g, [(TS + c + x, n) for x in range(P // n)], False) for c in range(0, d, P // n)]
    NJ = len(JOBS)
    with ExitStack() as ctx:
        def sb(name, shape, dt=F32):
            return ctx.enter_context(nc.sbuf_tensor("sw_" + name, shape, dt))

        def sem(name):
            return ctx.enter_context(nc.semaphore("sw_" + name))

        NR = 5
        tb = [sb(f"bias{g}", [P, BH, 2 * P]) for g in range(NG)]
        rows = sb("rows", [P, NR, 3 * BW])
        qk = sb("turned", [P, 4, 512])
        s = sb("scores", [P, 3, BH * 2 * P])
        pt = sb("probs_t", [P, 2, SEQ])
        nm = sb("neg_max", [P, 2, BH])
        ob = sb("out_rows", [P, 4, OBW])
        pss = [ctx.enter_context(nc.psum_tensor(f"sw_ps_s{i}", [P, 1024], F32)) for i in range(2)]
        pst = [ctx.enter_context(nc.psum_tensor(f"sw_ps_t{i}", [P, 512], F32)) for i in range(2)]
        pso = ctx.enter_context(nc.psum_tensor("sw_ps_o", [P, 512], F32))
        psx = ctx.enter_context(nc.psum_tensor("sw_ps_x", [P, 512], F32))
        tb_in = sem("tb_in")
        rows_in = [sem(f"rows_in{i}") for i in range(NR)]
        o_out = [sem(f"o_out{i}") for i in range(4)]
        (fenced, turned, turn_taken, scored, maxed, negated, exped, probs_turned, probs_taken, pv_done,
         copied) = (sem(n) for n in ("fenced", "turned", "turn_taken", "scored", "maxed", "negated", "exped",
                                     "probs_turned", "probs_taken", "pv_done", "copied"))
        block = ctx.enter_context(nc.Block())
        RUNS = [len(JOBS[t][1]) for t in range(NJ)]

        def slot_total(count, t, n):
            return 16 * sum(count[x] for x in range(t % n, t + 1, n))

        def blocks(t):
            return [(h, x) for h in range(BH) for x in ((0, P) if JOBS[t][2] else (P,))]

        def place(h):
            return 2 * P * (2 * (h % 2) + h // 2)

        UNITS = [0]
        for _t in range(NJ):
            UNITS.append(UNITS[-1] + len(blocks(_t)) // 4)

        def dram_rows(dram, row, n, g, c0, c1):
            return dram[row:row + DIL[g] * (n - 1) + 1:DIL[g], c0:c1]

        @block.sync
        def _(sp):
            def load(t):
                g, runs, _ = JOBS[t]
                if t >= NR:
                    sp.wait_ge(pv_done, t - NR + 2)
                at = 0
                for row, n in runs:
                    sp.dma_start(rows[at:at + n, t % NR, :],
                                 dram_rows(proj, row, n, g, 768 + 768 * g, 768 + 768 * (g + 1))).then_inc(rows_in[t % NR], 16)
                    at += n

            load(0)
            load(1)
            for g in range(NG):
                sp.dma_start(tb[g][:, :, :], wstrips[BH * g:BH * (g + 1)].rearrange("h p n -> p h n")).then_inc(tb_in, 16)
            load(2)
            for t in range(NJ):
                if t + 3 < NJ:
                    load(t + 3)
                sp.wait_ge(copied, t + 1)
                g, runs, _ = JOBS[t]
                at = 0
                for row, n in runs:
                    sp.dma_start(dram_rows(obp[g], row, n, g, 0, OBW), ob[at:at + n, t % 4, :]).then_inc(o_out[t % 4], 16)
                    at += n
            for t in range(NJ - 4, NJ):
                sp.wait_ge(o_out[t % 4], slot_total(RUNS, t, 4))

        @block.gpsimd
        def _(pool):
            n = SEQ // DIL[2]
            pool.wait_ge(tb_in, 16 * NG)
            nc.gpsimd.memset(tb[2][n:P, :, P:P + n], NEG).then_inc(fenced, 1)

        @block.scalar
        def _(act):
            for t in range(NJ + 2):
                if t < NJ:
                    act.wait_ge(turned, t + 1)
                    if t >= 4:
                        act.wait_ge(scored, t - 2)
                    nc.scalar.activation(qk[:, t % 4, :], psx[:, :], ACT.Copy).then_inc(turn_taken, 1)
                if 1 <= t <= NJ:
                    x = t - 1
                    c0 = 0 if JOBS[x][2] else P
                    act.wait_ge(maxed, BH * (x + 1))
                    if x >= 2:
                        act.wait_ge(exped, BH * (x - 1))
                    nc.scalar.mul(nm[:, x % 2, :], ob[:, x % 4, BW:BW + BH], -1.0).then_inc(negated, 1)
                    act.wait_ge(negated, x + 1)
                    for h in range(BH):
                        nc.scalar.activation(s[:, x % 3, place(h) + c0:place(h) + 2 * P], s[:, x % 3, place(h) + c0:place(h) + 2 * P], ACT.Exp, bias=nm[:, x % 2, h:h + 1],
                                             accum_out=ob[:, x % 4, BW + BH + h:BW + BH + h + 1]).then_inc(exped, 1)
                if t >= 2:
                    x = t - 2
                    if x >= 2:
                        act.wait_ge(pv_done, x - 1)
                    for u in range(UNITS[x], UNITS[x + 1]):
                        act.wait_ge(probs_turned, u + 1)
                        c = 512 * (u - UNITS[x])
                        nc.scalar.activation(pt[:, x % 2, c:c + 512], pst[u % 2][:, :], ACT.Copy).then_inc(probs_taken, 1)

        @block.tensor
        def _(pe):
            def turn_rows(t):
                pe.wait_ge(rows_in[t % NR], slot_total(RUNS, t, NR))
                if t:
                    pe.wait_ge(turn_taken, t)
                for i in range(4):
                    last = nc.tensor.transpose(psx[:, P * i:P * (i + 1)], rows[:, t % NR, P * i:P * (i + 1)], ident[:, :])
                last.then_inc(turned, 1)

            def scores(t):
                pe.wait_ge(turn_taken, t + 1)
                if t >= 2:
                    pe.wait_ge(maxed, BH * (t - 1))
                for h in range(BH):
                    pair, b = h // 2, HD * (h % 2)
                    for back in ((1, 0) if JOBS[t][2] else (0,)):
                        x = place(h) + P * (1 - back)
                        last = nc.tensor.matmul(pss[t % 2][:, x:x + P], qk[b:b + HD, t % 4, P * pair:P * (pair + 1)],
                                                qk[b:b + HD, (t - back) % 4, P * (2 + pair):P * (3 + pair)],
                                                start=True, stop=True)
                last.then_inc(scored, 1)

            def turn_probs(t):
                pe.wait_ge(exped, BH * (t + 1))
                todo = blocks(t)
                for u in range(UNITS[t], UNITS[t + 1]):
                    if u >= 2:
                        pe.wait_ge(probs_taken, u - 1)
                    for i in range(4):
                        h, x = todo[4 * (u - UNITS[t]) + i]
                        last = nc.tensor.transpose(pst[u % 2][:, P * i:P * (i + 1)],
                                                   s[:, t % 3, place(h) + x:place(h) + x + P], ident[:, :])
                    last.then_inc(probs_turned, 1)

            def outputs(t):
                pe.wait_ge(probs_taken, UNITS[t + 1])
                if t:
                    pe.wait_ge(copied, t)
                per = len(blocks(t)) // BH
                for i, (h, x) in enumerate(blocks(t)):
                    back = 1 if x == 0 else 0
                    last = nc.tensor.matmul(pso[:, HD * h:HD * (h + 1)], pt[:, t % 2, P * i:P * (i + 1)],
                                            rows[:, (t - back) % NR, 2 * BW + HD * h:2 * BW + HD * (h + 1)],
                                            start=(i % per == 0), stop=(i % per == per - 1))
                last.then_inc(pv_done, 1)

            for t in range(NJ + 3):
                if t < NJ:
                    turn_rows(t)
                if 1 <= t <= NJ:
                    scores(t - 1)
                if 2 <= t <= NJ + 1:
                    turn_probs(t - 2)
                if t >= 3:
                    outputs(t - 3)

        @block.vector
        def _(dve):
            dve.wait_ge(tb_in, 16 * NG)
            for t in range(NJ + 2):
                if t < NJ:
                    g, _, prev = JOBS[t]
                    if g == 2:
                        dve.wait_ge(fenced, 1)
                    c0 = 0 if prev else P
                    dve.wait_ge(scored, t + 1)
                    if t >= 3:
                        dve.wait_ge(probs_turned, UNITS[t - 2])
                    if t >= 4:
                        dve.wait_ge(o_out[t % 4], slot_total(RUNS, t - 4, 4))
                    for h in range(BH):
                        x, y = place(h) + c0, place(h) + 2 * P
                        nc.vector.tensor_tensor_reduce(out=s[:, t % 3, x:y],
                                                       in0=pss[t % 2][:, x:y], in1=tb[g][:, h, c0:2 * P],
                                                       scale=1.0, scalar=NEG, op0=ALU.add, op1=ALU.max,
                                                       accum_out=ob[:, t % 4, BW + h:BW + h + 1]).then_inc(maxed, 1)
                if t >= 2:
                    x = t - 2
                    dve.wait_ge(pv_done, x + 1)
                    nc.vector.tensor_copy(ob[:, x % 4, 0:BW], pso[:, 0:BW]).then_inc(copied, 1)


def stage_sample(nc, a, ident, proj, table, smask, oas, obs):
    ITEMS = [("a", 0, i) for i in range(DB // 2)] + [("b", g, i) for g in range(NG) for i in range(DB // 4)]
    NI = len(ITEMS)
    NA = DB // 2
    with ExitStack() as ctx:
        def sb(name, shape, dt=F32):
            return ctx.enter_context(nc.sbuf_tensor("ss_" + name, shape, dt))

        def sem(name):
            return ctx.enter_context(nc.semaphore("ss_" + name))

        MAXW = max(WL)
        srow = sb("rows", [TS, PROJ_W])
        kpa = sb("page_keys", [P, DB * NPAGE, PAGE])
        vpa = sb("page_values", [P, DB * NPAGE, P])
        vna = sb("new_values_a", [DT, DB, P])
        vnb = sb("new_values_b", [DT, NG, DB, BW])
        NW = 3
        kb = sb("window_keys", [P, NW, 4 * 2 * MAXW])
        vb = sb("window_values", [P, NW, 4 * 2 * BW])
        smr = sb("masks", [P, NA, SKEYS])
        ua = sb("bias_a", [P, SKEYS])
        uma = sb("bias_mask_a", [P, NA, SKEYS])
        ub = [sb(f"bias_b{g}", [P, WL[g] + DT]) for g in range(NG)]
        qba = sb("queries_a", [P, DB, HD])
        kna = sb("new_keys_a", [P, TS])
        qbb = sb("queries_b", [P, NG, 2, DB, 32])
        knb = sb("new_keys_b", [P, NG, 2, TS])
        s = sb("scores", [P, 3, MAXW + DT])
        pt = sb("probs_t", [P, 2, 3 * P])
        nm = sb("neg_max", [P, 4])
        st = sb("stats", [P, 4, 2])
        ob = sb("out_rows", [P, 3, OBW])
        pages = sb("pages", [1, DB * NPAGE], I32)
        pss = [ctx.enter_context(nc.psum_tensor(f"ss_ps_s{i}", [P, 512], F32)) for i in range(2)]
        pst = [ctx.enter_context(nc.psum_tensor(f"ss_ps_t{i}", [P, 512], F32)) for i in range(2)]
        pso = [ctx.enter_context(nc.psum_tensor(f"ss_ps_o{i}", [P, 512], F32)) for i in range(2)]
        psx = [ctx.enter_context(nc.psum_tensor(f"ss_ps_x{i}", [P, 512], F32)) for i in range(2)]
        rows_in, pages_in, kv_in, new_in, bias_in = (sem(n) for n in ("rows_in", "pages_in", "kv_in", "new_in", "bias_in"))
        win_in = [sem(f"win_in{i}") for i in range(NW)]
        o_out = [sem(f"o_out{i}") for i in range(3)]
        (zeroed, turned, turn_taken, masked, scored, maxed, negated, exped, probs_turned, probs_taken, pv_done,
         inverted, copied) = (sem(n) for n in ("zeroed", "turned", "turn_taken", "masked", "scored", "maxed", "negated",
                                               "exped", "probs_turned", "probs_taken", "pv_done", "inverted", "copied"))
        block = ctx.enter_context(nc.Block())

        def keys(t):
            kind, g, _ = ITEMS[t]
            return PAST if kind == "a" else WL[g]

        @block.sync
        def _(sp):
            sp.dma_start(pages[:, :], a["page_table"]).then_inc(pages_in, 16)
            qv = srow[:, 0:512].rearrange("p (r g d) -> p g r d", r=REP, g=AG)
            for g in range(AG):
                sp.dma_start(qv[:, g], proj[0:TS, 256 * g:256 * (g + 1)].rearrange("p (r d) -> p r d", r=REP)
                             ).then_inc(rows_in, 16)
            sp.dma_start(srow[:, 512:PROJ_W], proj[0:TS, 512:PROJ_W]).then_inc(rows_in, 16)
            sp.wait_ge(pages_in, 16)
            top = a["kv_keys_t"].shape[0] - 1
            for n in range(DB * NPAGE):
                page = sp.value_load(pages[0:1, n:n + 1], min_val=0, max_val=top)
                sp.dma_start(kpa[:, n, :], a["kv_keys_t"][bass.ds(page, 1), :, :].rearrange("o d n -> d (o n)")).then_inc(kv_in, 16)
                sp.dma_start(vpa[:, n, :], a["kv_values"][bass.ds(page, 1), :, :].rearrange("o n d -> n (o d)")).then_inc(kv_in, 16)
            for b in range(2):
                src = bass.AP(tensor=table.tensor, offset=SEQ - PAST - DT + DT - 1, ap=[[NTAB, AH], [-1, DT], [1, SKEYS]])
                sp.dma_start(ua[64 * b:64 * (b + 1), :], src).then_inc(bias_in, 16)
            for i in range(NA):
                for b in range(2):
                    src = bass.AP(tensor=smask.tensor, offset=DT * (2 * i + b) * SKEYS, ap=[[0, AH], [SKEYS, DT], [1, SKEYS]])
                    sp.dma_start(smr[64 * b:64 * (b + 1), i, :], src).then_inc(bias_in, 16)
            for g in range(NG):
                for b in range(4):
                    src = bass.AP(tensor=table.tensor, offset=(AH + BH * g) * NTAB + TAB_OFF_S[g] + DT - 1,
                                  ap=[[NTAB, BH], [-1, DT], [1, WL[g] + DT]])
                    sp.dma_start(ub[g][32 * b:32 * (b + 1), :], src).then_inc(bias_in, 16)
            new = proj[0:TS, :].rearrange("(b t) c -> t b c", t=DT)
            sp.dma_start(vna[:, :, :], new[:, :, 640:768]).then_inc(new_in, 16)
            for g in range(NG):
                sp.dma_start(vnb[:, g, :, :], new[:, :, 768 * (g + 1) + 2 * BW:768 * (g + 1) + 3 * BW]).then_inc(new_in, 16)

            def load_window(t):
                _, g, i = ITEMS[t]
                w = WL[g]
                x = (t - NA) % NW
                if t - NA >= NW:
                    sp.wait_ge(pv_done, t - NW + 1)
                sp.dma_start(kb[:, x, 0:4 * 2 * w].rearrange("p (b k) -> p b k", b=4),
                             a[f"win_keys_t{g}"][4 * i:4 * (i + 1)].rearrange("b d k -> d b k")).then_inc(win_in[x], 16)
                for b in range(4):
                    sp.dma_start(vb[:, x, 2 * BW * b:2 * BW * b + w // P * BW].rearrange("p (n c) -> p n c", c=BW),
                                 a[f"win_cache{g}"][4 * i + b, :, BW:2 * BW].rearrange("(n p) c -> p n c", p=P)).then_inc(win_in[x], 16)

            load_window(NA)
            load_window(NA + 1)
            for t in range(NI):
                kind, g, i = ITEMS[t]
                if NA <= t < NI - 2:
                    load_window(t + 2)
                sp.wait_ge(copied, t + 1)
                if kind == "a":
                    sp.dma_start(oas[i], ob[:, t % 3, 0:P]).then_inc(o_out[t % 3], 16)
                else:
                    sp.dma_start(obs[g][i][:, 0:BW + 2], ob[:, t % 3, 0:BW + 2]).then_inc(o_out[t % 3], 16)
            for x in range(3):
                sp.wait_ge(o_out[x], 16 * len([t for t in range(NI) if t % 3 == x]))

        @block.gpsimd
        def _(pool):
            nc.gpsimd.memset(qba[:, :, :], 0.0).then_inc(zeroed, 1)
            nc.gpsimd.memset(qbb[:, :, :, :, :], 0.0).then_inc(zeroed, 1)
            pool.wait_ge(bias_in, 16 * (2 + 2 * NA + 4 * NG))
            for i in range(NA):
                nc.gpsimd.tensor_tensor(uma[:, i, :], ua[:, :], smr[:, i, :], ALU.add).then_inc(masked, 1)

        @block.scalar
        def _(act):
            act.wait_ge(zeroed, 2)
            for n in range(2 + NG):
                act.wait_ge(turned, n + 1)
                x = psx[n % 2]
                if n == 0:
                    for g in range(AG):
                        last = nc.scalar.activation(
                            qba[HD * g:HD * (g + 1), :, 32 * g:32 * (g + 1)].rearrange("p b (r t) -> p r b t", t=DT),
                            x[HD * g:HD * (g + 1), 0:256].rearrange("p (r b t) -> p r b t", r=REP, t=DT), ACT.Copy)
                elif n == 1:
                    last = nc.scalar.activation(kna[:, :], x[:, 0:TS], ACT.Copy)
                else:
                    g = n - 2
                    for pair in range(2):
                        for hh in range(2):
                            h = 2 * pair + hh
                            nc.scalar.activation(qbb[HD * hh:HD * (hh + 1), g, pair, :, DT * h:DT * (h + 1)],
                                                 x[HD * hh:HD * (hh + 1), TS * pair:TS * (pair + 1)].rearrange(
                                                     "p (b t) -> p b t", t=DT), ACT.Copy)
                    last = nc.scalar.activation(knb[:, g, :, :], x[:, 2 * TS:4 * TS].rearrange("p (a t) -> p a t", a=2), ACT.Copy)
                last.then_inc(turn_taken, 1)
            for t in range(NI + 1):
                if t < NI:
                    w = keys(t) + DT
                    act.wait_ge(maxed, t + 1)
                    if t >= 4:
                        act.wait_ge(exped, t - 3)
                    nc.scalar.mul(nm[:, t % 4:t % 4 + 1], st[:, t % 4, 0:1], -1.0).then_inc(negated, 1)
                    act.wait_ge(negated, t + 1)
                    if t >= 4:
                        act.wait_ge(copied, t - 3)
                    nc.scalar.activation(s[:, t % 3, 0:w], s[:, t % 3, 0:w], ACT.Exp, bias=nm[:, t % 4:t % 4 + 1],
                                         accum_out=st[:, t % 4, 1:2]).then_inc(exped, 1)
                if t >= 1:
                    x = t - 1
                    w = keys(x)
                    act.wait_ge(probs_turned, x + 1)
                    if x >= 2:
                        act.wait_ge(pv_done, x - 1)
                    nc.scalar.activation(pt[:, x % 2, 0:w], pst[x % 2][:, 0:w], ACT.Copy)
                    nc.scalar.activation(pt[0:DT, x % 2, w:w + P], pst[x % 2][0:DT, w:w + P], ACT.Copy).then_inc(probs_taken, 1)

        @block.tensor
        def _(pe):
            pe.wait_ge(rows_in, 48)

            def turn(n, parts):
                if n >= 2:
                    pe.wait_ge(turn_taken, n - 1)
                for i, c in enumerate(parts):
                    last = nc.tensor.transpose(psx[n % 2][:, TS * i:TS * (i + 1)], srow[:, c:c + P], ident[0:TS, 0:TS])
                last.then_inc(turned, 1)

            turn(0, [P * r for r in range(REP)])
            turn(1, [512])
            for g in range(NG):
                turn(2 + g, [768 * (g + 1) + P * i for i in range(4)])
            pe.wait_ge(turn_taken, 2 + NG)
            pe.wait_ge(kv_in, 32 * DB * NPAGE)
            pe.wait_ge(new_in, 16 * (1 + NG))

            def scores(t):
                kind, g, i = ITEMS[t]
                w = keys(t)
                if t >= 2:
                    pe.wait_ge(maxed, t - 1)
                z = pss[t % 2]
                if kind == "a":
                    for bb in range(2):
                        b = 2 * i + bb
                        o = z[64 * bb:64 * (bb + 1), :]
                        for n in range(NPAGE):
                            nc.tensor.matmul(o[:, PAGE * n:PAGE * (n + 1)], qba[:, b, :], kpa[:, NPAGE * b + n, :], start=True, stop=True)
                        last = nc.tensor.matmul(o[:, w:w + DT], qba[:, b, :], kna[:, DT * b:DT * (b + 1)], start=True, stop=True)
                else:
                    x = (t - NA) % NW
                    pe.wait_ge(win_in[x], 16 * 5 * ((t - NA) // NW + 1))
                    for bb in range(4):
                        b = 4 * i + bb
                        o = z[32 * bb:32 * (bb + 1), :]
                        for pair in range(2):
                            nc.tensor.matmul(o[:, 0:w], qbb[:, g, pair, b, :], kb[:, x, 2 * w * bb + w * pair:2 * w * bb + w * (pair + 1)],
                                             start=(pair == 0), stop=(pair == 1), tile_position=(0, 32 * bb))
                        for pair in range(2):
                            last = nc.tensor.matmul(o[:, w:w + DT], qbb[:, g, pair, b, :], knb[:, g, pair, DT * b:DT * (b + 1)],
                                                    start=(pair == 0), stop=(pair == 1), tile_position=(0, 32 * bb))
                last.then_inc(scored, 1)

            def turn_probs(t):
                w = keys(t)
                pe.wait_ge(exped, t + 1)
                if t >= 2:
                    pe.wait_ge(probs_taken, t - 1)
                for n in range(w // P):
                    nc.tensor.transpose(pst[t % 2][:, P * n:P * (n + 1)], s[:, t % 3, P * n:P * (n + 1)], ident[:, :])
                nc.tensor.transpose(pst[t % 2][0:DT, w:w + P], s[:, t % 3, w:w + DT], ident[:, :]).then_inc(probs_turned, 1)

            def outputs(t):
                kind, g, i = ITEMS[t]
                w = keys(t)
                pe.wait_ge(probs_taken, t + 1)
                if t >= 2:
                    pe.wait_ge(copied, t - 1)
                m, nb, ow = (64, 2, P) if kind == "a" else (32, 4, BW)
                for bb in range(nb):
                    b = nb * i + bb
                    o = pso[t % 2][m * bb:m * (bb + 1), 0:ow]
                    for n in range(w // P):
                        val = vpa[:, NPAGE * b + n, :] if kind == "a" else \
                            vb[:, (t - NA) % NW, 2 * BW * bb + BW * n:2 * BW * bb + BW * (n + 1)]
                        nc.tensor.matmul(o, pt[:, t % 2, P * n + m * bb:P * n + m * (bb + 1)], val, start=(n == 0), stop=False,
                                         tile_position=(0, m * bb))
                    val = vna[:, b, :] if kind == "a" else vnb[:, g, b, :]
                    last = nc.tensor.matmul(o, pt[0:DT, t % 2, w + m * bb:w + m * (bb + 1)], val, start=False, stop=True,
                                            tile_position=(0, m * bb))
                last.then_inc(pv_done, 1)

            for t in range(NI + 2):
                if t < NI:
                    scores(t)
                if 1 <= t <= NI:
                    turn_probs(t - 1)
                if t >= 2:
                    outputs(t - 2)

        @block.vector
        def _(dve):
            dve.wait_ge(bias_in, 16 * (2 + 2 * NA + 4 * NG))
            for t in range(NI + 2):
                if t < NI:
                    kind, g, i = ITEMS[t]
                    w = keys(t) + DT
                    dve.wait_ge(scored, t + 1)
                    if kind == "a":
                        dve.wait_ge(masked, i + 1)
                    if t >= 3:
                        dve.wait_ge(probs_turned, t - 2)
                    if t >= 4:
                        dve.wait_ge(negated, t - 3)
                        dve.wait_ge(copied, t - 3)
                    nc.vector.tensor_tensor_reduce(out=s[:, t % 3, 0:w], in0=pss[t % 2][:, 0:w],
                                                   in1=uma[:, i, :] if kind == "a" else ub[g][:, :], scale=1.0, scalar=NEG,
                                                   op0=ALU.add, op1=ALU.max, accum_out=st[:, t % 4, 0:1]).then_inc(maxed, 1)
                if t >= 2:
                    x = t - 2
                    dve.wait_ge(pv_done, x + 1)
                    if x >= 3:
                        dve.wait_ge(o_out[x % 3], 16 * (x // 3))
                    if ITEMS[x][0] == "a":
                        nc.vector.reciprocal(ob[:, x % 3, P:P + 1], st[:, x % 4, 1:2]).then_inc(inverted, 1)
                        dve.wait_ge(inverted, x + 1)
                        nc.vector.tensor_scalar(ob[:, x % 3, 0:P], pso[x % 2][:, 0:P], ob[:, x % 3, P:P + 1], None,
                                                ALU.mult).then_inc(copied, 1)
                    else:
                        nc.vector.tensor_copy(ob[:, x % 3, BW:BW + 2], st[:, x % 4, :])
                        nc.vector.tensor_copy(ob[:, x % 3, 0:BW], pso[x % 2][:, 0:BW]).then_inc(copied, 1)


def stage_merge(nc, a, ident, oa, obp, oas, obs, oth, otl):
    with ExitStack() as ctx:
        def sb(name, shape, dt=F32):
            return ctx.enter_context(nc.sbuf_tensor("sm_" + name, shape, dt))

        def sem(name):
            return ctx.enter_context(nc.semaphore("sm_" + name))

        ra = sb("rows_a", [P, 2, 512])
        rb = sb("rows_b", [P, 2, NG, OBW])
        mm = sb("top", [P, 2, BH])
        df = sb("below", [P, 2, NG, BH])
        ww = sb("weights", [P, 2, NG, BH])
        lw = sb("weighted_sums", [P, 2, NG, BH])
        ll = sb("total", [P, 2, BH])
        wn = sb("shares", [P, 2, NG, BH])
        tt = sb("shared", [P, 2, NG, BW])
        om = sb("merged", [P, 2, BW])
        ps = [ctx.enter_context(nc.psum_tensor(f"sm_ps{i}", [P, 1024], F32)) for i in range(2)]
        rows_in = [sem(f"rows_in{i}") for i in range(2)]
        (step, below, weighed, merged, turned, high, low, cleared) = (sem(n) for n in (
            "step", "below", "weighed", "merged", "turned", "high", "low", "cleared"))
        block = ctx.enter_context(nc.Block())
        N_IN = [DB * AG + NG * DB * 3] + [1 + NG] * (NT - 1)

        @block.sync
        def _(sp):
            for i in [*range(1, NT), 0]:
                n = (i - 1) % NT
                if n >= 2:
                    sp.wait_ge(turned, n - 1)
                x = rows_in[n % 2]
                if i:
                    c = tile_col(i)
                    sp.dma_start(ra[:, n % 2, :], oa[c:c + P, :]).then_inc(x, 16)
                    for g in range(NG):
                        sp.dma_start(rb[:, n % 2, g, :], obp[g][c:c + P, :]).then_inc(x, 16)
                    continue
                for b in range(DB):
                    for g in range(AG):
                        src = bass.AP(tensor=oas.tensor, offset=((b // 2) * P + 64 * (b % 2) + 32 * g) * P + HD * g,
                                      ap=[[P, DT], [DT * P, REP], [1, HD]])
                        sp.dma_start(ra[DT * b:DT * (b + 1), n % 2, 256 * g:256 * (g + 1)].rearrange("p (r d) -> p r d", r=REP),
                                     src).then_inc(x, 16)
                    for g in range(NG):
                        base = ((g * (DB // 4) + b // 4) * P + 32 * (b % 4)) * OBW
                        src = bass.AP(tensor=obs.tensor, offset=base, ap=[[OBW, DT], [DT * OBW + HD, BH], [1, HD]])
                        sp.dma_start(rb[DT * b:DT * (b + 1), n % 2, g, 0:BW].rearrange("p (h d) -> p h d", h=BH), src).then_inc(x, 16)
                        for m in range(2):
                            src = bass.AP(tensor=obs.tensor, offset=base + BW + m, ap=[[OBW, DT], [DT * OBW, BH]])
                            with nc.allow_non_contiguous_dma(reason="32 words"):
                                sp.dma_start(rb[DT * b:DT * (b + 1), n % 2, g, BW + BH * m:BW + BH * (m + 1)], src).then_inc(x, 16)

        def order():
            for n in range(NT):
                i = n + 1 if n < NT - 1 else 0
                yield n, i, tile_rows(i), tile_col(i)

        def total_in(n):
            i = n + 1 if n < NT - 1 else 0
            return 16 * (N_IN[i] + sum(N_IN[1] for m in range(n % 2, n, 2)))

        def put_high(act, n):
            i = n + 1 if n < NT - 1 else 0
            r, c = tile_rows(i), tile_col(i)
            act.wait_ge(turned, n + 1)
            nc.scalar.activation(oth[:, :, c:c + r], ps[n % 2][:, 0:6 * P].rearrange("p (k t) -> p k t", k=6)[:, :, 0:r],
                                 ACT.Copy).then_inc(high, 1)

        def put_low(dve, n):
            i = n + 1 if n < NT - 1 else 0
            r, c = tile_rows(i), tile_col(i)
            dve.wait_ge(high, n + 1)
            nc.vector.tensor_tensor(otl[:, :, c:c + r], ps[n % 2][:, 0:6 * P].rearrange("p (k t) -> p k t", k=6)[:, :, 0:r],
                                    oth[:, :, c:c + r].bitcast(F32), ALU.subtract).then_inc(low, 1)


        @block.scalar
        def _(act):
            for n, i, r, c in order():
                act.wait_ge(below, n + 1)
                if n >= 2:
                    act.wait_ge(merged, n - 1)
                nc.scalar.activation(ww[0:r, n % 2, :, :], df[0:r, n % 2, :, :], ACT.Exp).then_inc(weighed, 1)
                if n:
                    put_high(act, n - 1)
            put_high(act, NT - 1)

        @block.tensor
        def _(pe):
            for n, i, r, c in order():
                pe.wait_ge(rows_in[n % 2], total_in(n))
                pe.wait_ge(merged, n + 1)
                if n >= 2:
                    pe.wait_ge(low, n - 1)
                for k in range(6):
                    src = ra[0:r, n % 2, P * k:P * (k + 1)] if k < 4 else om[0:r, n % 2, P * (k - 4):P * (k - 3)]
                    last = nc.tensor.transpose(ps[n % 2][:, P * k:P * k + r], src, ident[0:r, 0:r])
                last.then_inc(turned, 1)

        @block.vector
        def _(dve):
            nc.vector.memset(otl[:, :, TS + SEQ:TOK].bitcast(F32), 0.0).then_inc(cleared, 1)
            nc.vector.memset(oth[:, :, TS + SEQ:TOK].bitcast(F32), 0.0).then_inc(cleared, 1)
            count = [0]

            def link(ins):
                count[0] += 1
                ins.then_inc(step, 1)
                dve.wait_ge(step, count[0])

            for n, i, r, c in order():
                dve.wait_ge(rows_in[n % 2], total_in(n))
                x, y = n % 2, n % 2

                def m(g):
                    return rb[0:r, x, g, BW:BW + BH]

                link(nc.vector.tensor_tensor(mm[0:r, y, :], m(0), m(1), ALU.max))
                link(nc.vector.tensor_tensor(mm[0:r, y, :], mm[0:r, y, :], m(2), ALU.max))
                top = mm[0:r, y:y + 1, :].broadcast_to([r, NG, BH])
                nc.vector.tensor_tensor(df[0:r, y, :, :], rb[0:r, x, :, BW:BW + BH], top, ALU.subtract).then_inc(below, 1)
                dve.wait_ge(weighed, n + 1)
                link(nc.vector.tensor_tensor(lw[0:r, y, :, :], ww[0:r, y, :, :], rb[0:r, x, :, BW + BH:OBW], ALU.mult))
                link(nc.vector.tensor_tensor(ll[0:r, y, :], lw[0:r, y, 0, :], lw[0:r, y, 1, :], ALU.add))
                link(nc.vector.tensor_tensor(ll[0:r, y, :], ll[0:r, y, :], lw[0:r, y, 2, :], ALU.add))
                link(nc.vector.reciprocal(ll[0:r, y, :], ll[0:r, y, :]))
                tot = ll[0:r, y:y + 1, :].broadcast_to([r, NG, BH])
                link(nc.vector.tensor_tensor(wn[0:r, y, :, :], ww[0:r, y, :, :], tot, ALU.mult))
                for g in range(NG):
                    share = wn[0:r, y, g, :].rearrange("p (h o) -> p h o", o=1).broadcast_to([r, BH, HD])
                    last = nc.vector.tensor_tensor(tt[0:r, y, g, :].rearrange("p (h d) -> p h d", h=BH),
                                                   rb[0:r, x, g, 0:BW].rearrange("p (h d) -> p h d", h=BH), share, ALU.mult)
                link(last)
                if n >= 2:
                    dve.wait_ge(turned, n - 1)
                link(nc.vector.tensor_tensor(om[0:r, y, :], tt[0:r, y, 0, :], tt[0:r, y, 1, :], ALU.add))
                nc.vector.tensor_tensor(om[0:r, y, :], om[0:r, y, :], tt[0:r, y, 2, :], ALU.add).then_inc(merged, 1)
                if n:
                    put_low(dve, n - 1)
            put_low(dve, NT - 1)

NF = 4
NBLK = FF // (NF * P)
BLK_U, BLK_R = 2 * NF, NF + KD
U_OUT = 0
U_MLP = [U_OUT + KD, U_OUT + KD + NBLK * BLK_U + 3 * KD]
U_REC = U_MLP[0] + NBLK * BLK_U
U_REC_OUT = U_REC + 2 * KD
U_END = U_MLP[1] + NBLK * BLK_U
R_OUT = 0
R_MLP = [KD, 0]
R_REC = R_MLP[0] + 1 + NBLK * BLK_R
R_REC_OUT = R_REC + 1 + 4 * KD
R_MLP[1] = R_REC_OUT + KD
SEG = CONVW - 1 + DT
PCOL = DB * SEG
EXT = PCOL + CONVW - 1 + SEQ
CONV = EXT - (CONVW - 1)
CC = -(-CONV // NCH)
NPAR = 3 + CONVW + 4
PAR_CONV, PAR_CB, PAR_GA, PAR_GX, PAR_LRU = 3, 3 + CONVW, 4 + CONVW, 5 + CONVW, 6 + CONVW


class Dense:

    def __init__(self, nc, ctx, a):
        self.nc, self.a = nc, a

        def sb(name, shape, dt=F32):
            return ctx.enter_context(nc.sbuf_tensor(name, shape, dt))

        def sem(name):
            return ctx.enter_context(nc.semaphore("d_" + name))

        self.x = sb("x_t", [P, KD, NCH, CH])
        self.gh = sb("xg_high", [P, KD, NCH, CH], F32R)
        self.gl = sb("xg_low", [P, KD, NCH, CH], F32R)
        self.raw = sb("unit_raw", [P, 2, KD * P])
        self.wh = [sb(f"unit_high{i}", [P, KD * P], F32R) for i in range(2)]
        self.wl = [sb(f"unit_low{i}", [P, KD * P], F32R) for i in range(2)]
        self.par = sb("params", [P, NPAR, KD])
        self.ones = sb("ones_square", [P, P])
        self.ssum = sb("square_sum", [P, NCH, CH])
        self.rstd = sb("rstd_all", [P, NCH, CH])
        self.w_in = [sem(f"w_in{i}") for i in range(2)]
        self.w_high, self.w_low = sem("w_high"), sem("w_low")
        self.made = sem("made")
        self.taken = [sem(f"taken{i}") for i in range(2)]
        self.x_high, self.x_low, self.x_squared, self.x_summed = (
            sem(n) for n in ("x_high", "x_low", "x_squared", "x_summed"))
        self.root_done, self.rstd_done, self.ready = sem("root_done"), sem("rstd_done"), sem("ready")

    def load(self, sp, u, slot):
        sp.wait_ge(self.w_low, u - 1)
        sp.wait_ge(self.ready, 1)
        sp.dma_start(self.raw[:, slot, :], self.a["w_units"][bass.ds(u, 1), :, :].rearrange("o p n -> p (o n)")
                     ).then_inc(self.w_in[slot], 16)

    def split_high(self, dve, slot, half, made):
        dve.wait_ge(self.w_in[slot], 16 * half + 16)
        dve.wait_ge(self.made, made)
        self.nc.vector.tensor_copy(self.wh[slot][:, :], self.raw[:, slot, :]).then_inc(self.w_high, 1)

    def split_low(self, pool, u, slot):
        pool.wait_ge(self.w_high, u + 1)
        self.nc.gpsimd.tensor_tensor(self.wl[slot][:, :], self.raw[:, slot, :], self.wh[slot][:, :].bitcast(F32),
                                     ALU.subtract).then_inc(self.w_low, 1)

    def product(self, pe, ps, wslot, at, nk, high, low, k_ready=None):
        for k in range(nk):
            if k_ready:
                k_ready(k)
            wk = slice(P * (at + k), P * (at + k + 1))
            for n, (w, v) in enumerate(((self.wh, high), (self.wl, high), (self.wh, low))):
                for c in range(NCH):
                    last = self.nc.tensor.matmul(ps[:, c, 0:CH], w[wslot][:, wk], v[:, k, c, :],
                                                 start=(k == 0 and n == 0), stop=(k == nk - 1 and n == 2))
        last.then_inc(self.made, 1)

    def part_high(self, act, n, gain):
        self.nc.scalar.activation(self.gh[:, n, :, :], self.x[:, n, :, :], ACT.Copy, scale=self.par[:, gain, n:n + 1]
                                  ).then_inc(self.x_high, 1)

    def part_low(self, dve, n, seen, gain):
        dve.wait_ge(self.x_high, seen + n + 1)
        self.nc.vector.scalar_tensor_tensor(out=self.gl[:, n, :, :], in0=self.x[:, n, :, :], scalar=self.par[:, gain, n:n + 1],
                                            in1=self.gh[:, n, :, :].bitcast(F32), op0=ALU.mult, op1=ALU.subtract
                                            ).then_inc(self.x_low, 1)

    def square(self, act, sq, n, seen):
        if n >= 2:
            act.wait_ge(self.x_summed, (seen // KD) * (KD - 1) + n - 1)
        self.nc.scalar.activation(sq[n % 2], self.x[:, n, :, :], ACT.Square).then_inc(self.x_squared, 1)

    def sum_up(self, pool, sq, n, seen):
        pool.wait_ge(self.x_squared, seen + n + 1)
        if n == 0:
            return
        if n >= 2:
            pool.wait_ge(self.x_summed, (seen // KD) * (KD - 1) + n - 1)
        first = sq[0] if n == 1 else self.ssum[:, :, :]
        self.nc.gpsimd.tensor_tensor(self.ssum[:, :, :], first, sq[n % 2], ALU.add).then_inc(self.x_summed, 1)

    def sums_pe(self, pe, ps, nth, ring):
        pe.wait_ge(self.x_summed, (KD - 1) * (nth + 1))
        pe.wait_ge(self.taken[ring % 2], ring // 2)
        for c in range(NCH):
            last = self.nc.tensor.matmul(ps[ring % 2][:, c, 0:CH], self.ones[:, :], self.ssum[:, c, :], start=True, stop=True)
        last.then_inc(self.made, 1)

    def sums_dve(self, dve, ps, nth, ring):
        dve.wait_ge(self.made, ring + 1)
        self.nc.vector.tensor_scalar(self.rstd[:, :, :], ps[ring % 2][:, :, 0:CH], 1.0 / D, EPS, ALU.mult, ALU.add
                                     ).then_inc(self.taken[ring % 2], 1)
        dve.wait_ge(self.root_done, nth + 1)
        self.nc.vector.reciprocal(self.rstd[:, :, :], self.rstd[:, :, :]).then_inc(self.rstd_done, 1)
        dve.wait_ge(self.rstd_done, nth + 1)

    def sums_act(self, act, nth, ring):
        act.wait_ge(self.taken[ring % 2], ring // 2 + 1)
        self.nc.scalar.activation(self.rstd[:, :, :], self.rstd[:, :, :], ACT.Sqrt).then_inc(self.root_done, 1)


def slots(nc, ctx, tag):
    return [ctx.enter_context(nc.psum_tensor(f"{tag}_ps{i}", [P, NCH, 512], F32)) for i in range(2)]


def stage_out_projection(nc, a, d, oth, otl):
    with ExitStack() as ctx:
        sq = [ctx.enter_context(nc.sbuf_tensor(f"op_sq{i}", [P, NCH, CH], F32))[:, :, :] for i in range(2)]
        x_in = ctx.enter_context(nc.semaphore("op_x_in"))
        par_in = ctx.enter_context(nc.semaphore("op_par_in"))
        ps = slots(nc, ctx, "op")
        block = ctx.enter_context(nc.Block())

        @block.sync
        def _(sp):
            for u in range(2):
                sp.dma_start(d.raw[:, u, :], a["w_units"][u]).then_inc(d.w_in[u], 16)
            sp.dma_start(d.par[:, :, :], a["dense_params"]).then_inc(par_in, 16)
            sp.dma_start(d.x[:, :, :, :].rearrange("p k c n -> p k (c n)"), a["xt"].rearrange("k p n -> p k n")).then_inc(x_in, 16)
            for u in range(2, KD + 2):
                d.load(sp, u, u % 2)
            sp.wait_ge(x_in, 16)

        @block.gpsimd
        def _(pool):
            nc.gpsimd.memset(d.ones[:, :], 1.0).then_inc(d.ready, 1)
            d.split_low(pool, 0, 0)
            d.split_low(pool, 1, 1)
            for n in range(KD):
                d.split_low(pool, n + 2, n % 2)
                d.sum_up(pool, sq, n, 0)

        @block.scalar
        def _(act):
            act.wait_ge(par_in, 16)
            for n in range(KD):
                act.wait_ge(d.taken[n % 2], n // 2 + 1)
                d.part_high(act, n, 0)
                d.square(act, sq, n, 0)

        @block.tensor
        def _(pe):
            for u in range(KD):
                pe.wait_ge(d.w_low, u + 1)
                if u >= 2:
                    pe.wait_ge(d.taken[u % 2], u // 2)
                d.product(pe, ps[u % 2], u % 2, 0, 6, oth, otl)

        @block.vector
        def _(dve):
            for u in range(2):
                dve.wait_ge(d.w_in[u], 16)
                nc.vector.tensor_copy(d.wh[u][:, :], d.raw[:, u, :]).then_inc(d.w_high, 1)
            dve.wait_ge(x_in, 16)
            dve.wait_ge(par_in, 16)
            for n in range(KD):
                dve.wait_ge(d.made, n + 1)
                nc.vector.tensor_tensor(d.x[:, n, :, :], d.x[:, n, :, :], ps[n % 2][:, :, 0:CH], ALU.add
                                        ).then_inc(d.taken[n % 2], 1)
                d.split_high(dve, n % 2, (n + 2) // 2, n + 1)
                dve.wait_ge(d.taken[n % 2], n // 2 + 1)
                d.part_low(dve, n, 0, 0)


def stage_mlp(nc, a, d, layer, nth, y=None):
    U0, R0 = U_MLP[layer], R_MLP[layer] + 1
    FREE = 2
    seen = KD * (nth + 1)
    with ExitStack() as ctx:
        def sem(name):
            return ctx.enter_context(nc.semaphore(f"m{layer}_{name}"))

        def sb(name, shape, dt=F32):
            return ctx.enter_context(nc.sbuf_tensor(f"m{layer}_{name}", shape, dt))

        hh = sb("hidden_high", [P, NF, NCH, CH], F32R)
        hl = sb("hidden_low", [P, NF, NCH, CH], F32R)
        r = sb("relu", [P, 2, NCH, CH])
        v = sb("square", [P, 2, NCH, CH])
        ps = slots(nc, ctx, f"m{layer}")
        relu_scaled, h_high, squared, h_low, y_out = (sem(n) for n in ("relu_scaled", "h_high", "squared", "h_low", "y_out"))
        block = ctx.enter_context(nc.Block())

        def run(eng, up, down, last=None):
            up(0)
            with eng.Fori(0, NBLK - 1) as b:
                down(b)
                up(b + 1)
            (last or down)(NBLK - 1)

        def up_at(b, i):
            return (U0 + i + BLK_U * b, i % 2, (U0 + i) // 2 + BLK_U // 2 * b,
                    R0 + i + BLK_R * b, (R0 + i) % 2, (R0 + i) // 2 + BLK_R // 2 * b)

        def down_at(b, m):
            i, q = NF + m, NF + 2 * m
            return (U0 + i + BLK_U * b, i % 2, (U0 + i) // 2 + BLK_U // 2 * b,
                    R0 + q + BLK_R * b, (R0 + q) % 2, (R0 + q) // 2 + BLK_R // 2 * b)

        @block.sync
        def _(sp):
            def up(b):
                for i in range(NF):
                    u, slot = up_at(b, i)[:2]
                    d.load(sp, u + 2, slot)

            def down(b):
                for m in range(NF):
                    u, slot = down_at(b, m)[:2]
                    if not isinstance(u, int) or u + 2 < U_END:
                        d.load(sp, u + 2, slot)

            run(sp, up, down)
            if y is not None:
                for n in range(KD):
                    _, _, _, _, slot, used = down_at(NBLK - 1, n // 2)
                    sp.wait_ge(d.taken[(slot + n) % 2], used + (slot + n % 2) // 2 + 1)
                    sp.dma_start(y[n], d.x[:, n, :, :].rearrange("p c n -> p (c n)")).then_inc(y_out, 16)
                sp.wait_ge(y_out, 16 * KD)

        @block.gpsimd
        def _(pool):
            nc.gpsimd.sem_inc(squared, FREE)
            nc.gpsimd.sem_inc(h_low, FREE)

            def up(b):
                for i in range(NF):
                    u, slot = up_at(b, i)[:2]
                    n = NF * b + i
                    d.split_low(pool, u + 2, slot)
                    pool.wait_ge(h_high, n + 1)
                    pool.wait_ge(squared, n + 1 + FREE)
                    nc.gpsimd.tensor_tensor(hl[:, i, :, :], v[:, i % 2, :, :], hh[:, i, :, :].bitcast(F32), ALU.subtract
                                            ).then_inc(h_low, 1)

            def down(b):
                for m in range(NF):
                    u, slot = down_at(b, m)[:2]
                    if not isinstance(u, int) or u + 2 < U_END:
                        d.split_low(pool, u + 2, slot)
                    if isinstance(b, int) and y is None:
                        for n in (2 * m, 2 * m + 1):
                            d.sum_up(pool, [v[:, 0, :, :], v[:, 1, :, :]], n, seen)

            run(pool, up, down)

        @block.scalar
        def _(act):
            d.sums_act(act, nth, R_MLP[layer])

            def up(b):
                for i in range(NF):
                    _, _, _, use, slot, _ = up_at(b, i)
                    n = NF * b + i
                    act.wait_ge(d.made, use + 1)
                    act.wait_ge(squared, n + 1)
                    nc.scalar.activation(r[:, i % 2, :, :], ps[slot][:, :, 0:CH], ACT.Relu).then_inc(d.taken[slot], 1)
                    act.wait_ge(relu_scaled, n + 1)
                    nc.scalar.activation(hh[:, i, :, :], r[:, i % 2, :, :], ACT.Square).then_inc(h_high, 1)

            def down(b):
                if isinstance(b, int) and y is None:
                    for n in range(KD):
                        _, _, _, _, slot, used = down_at(b, n // 2)
                        act.wait_ge(d.taken[(slot + n) % 2], used + (slot + n % 2) // 2 + 1)
                        d.part_high(act, n, layer + 1)
                        d.square(act, [v[:, 0, :, :], v[:, 1, :, :]], n, seen)

            run(act, up, down)

        @block.tensor
        def _(pe):
            d.sums_pe(pe, ps, nth, R_MLP[layer])
            pe.wait_ge(d.x_low, seen)

            def up(b):
                for i in range(NF):
                    u, wslot, _, _, slot, used = up_at(b, i)
                    pe.wait_ge(d.w_low, u + 1)
                    pe.wait_ge(d.taken[slot], used)
                    d.product(pe, ps[slot], wslot, 0, KD, d.gh, d.gl)

            def down(b):
                for m in range(NF):
                    u, wslot, _, _, slot, used = down_at(b, m)
                    pe.wait_ge(d.w_low, u + 1)
                    for x in range(2):
                        s = (slot + x) % 2
                        pe.wait_ge(d.taken[s], used + (slot + x) // 2)
                        d.product(pe, ps[s], wslot, NF * x, NF, hh, hl,
                                  (lambda k: pe.wait_ge(h_low, NF * b + k + 1 + FREE)) if m == 0 and x == 0 else None)

            run(pe, up, down)

        @block.vector
        def _(dve):
            d.sums_dve(dve, ps, nth, R_MLP[layer])

            def up(b):
                for i in range(NF):
                    _, wslot, half, use, slot, used = up_at(b, i)
                    n = NF * b + i
                    dve.wait_ge(d.taken[slot], used + 1)
                    nc.vector.tensor_tensor(r[:, i % 2, :, :], r[:, i % 2, :, :], d.rstd[:, :, :], ALU.mult).then_inc(relu_scaled, 1)
                    d.split_high(dve, wslot, half + 1, use + 1)
                    dve.wait_ge(relu_scaled, n + 1)
                    dve.wait_ge(h_low, n + 1)
                    nc.vector.tensor_tensor(v[:, i % 2, :, :], r[:, i % 2, :, :], r[:, i % 2, :, :], ALU.mult).then_inc(squared, 1)

            def down(b):
                for m in range(NF):
                    u, wslot, half, use, slot, used = down_at(b, m)
                    for x in range(2):
                        s, n = (slot + x) % 2, 2 * m + x
                        dve.wait_ge(d.made, use + x + 1)
                        nc.vector.tensor_tensor(d.x[:, n, :, :], d.x[:, n, :, :], ps[s][:, :, 0:CH], ALU.add).then_inc(d.taken[s], 1)
                    if not isinstance(u, int) or u + 2 < U_END:
                        d.split_high(dve, wslot, half + 1, use + 2)
                    if isinstance(b, int) and y is None:
                        for x in range(2):
                            dve.wait_ge(d.taken[(slot + x) % 2], used + (slot + x) // 2 + 1)
                            d.part_low(dve, 2 * m + x, seen, layer + 1)

            run(dve, up, down)


def stage_recurrent(nc, a, d, nth, state_out):
    seen = KD * (nth + 1)
    R1 = R_REC + 1
    ORDER = [("x", 0), ("g", 0)]
    for _n in range(1, KD):
        ORDER += [("x", _n), ("g", _n), ("a", _n - 1), ("i", _n - 1)]
    ORDER += [("a", KD - 1), ("i", KD - 1)]
    USE = {k: R1 + i for i, k in enumerate(ORDER)}
    with ExitStack() as ctx:
        def sem(name):
            return ctx.enter_context(nc.semaphore("r_" + name))

        def sb(name, shape, dt=F32):
            return ctx.enter_context(nc.sbuf_tensor("r_" + name, shape, dt))

        xs = sb("conv_in", [P, EXT])
        cv = sb("conv", [P, 2, NCH, CC])
        ra = sb("decay", [P, NCH, CC])
        ig = sb("input_gate", [P, NCH, CC])
        th = sb("tanh", [P, NCH, CC])
        gm = [sb("gate", [P, TOK]), d.ssum[:, :, :].rearrange("p c n -> p (c n)")]
        hg = sb("gated", [P, KD, NCH, CH])
        st = sb("states", [P, KD, DB * 3])
        h0 = sb("first_state", [P, KD, DB + 1])
        gw = sb("gate_weights", [P, 2, 2, P])
        so = sb("state_out", [P, KD, 36])
        ls = sb("log_sigmoid", [P, 8, KD])
        ps = slots(nc, ctx, "r")
        names = ("small_in states_copied conv_done tails gelu tanh decay squared_a "
                 "dual root gated_in drive fixed scanned h_out hg_done gh gl lru pad st_out").split()
        S = {n: sem(n) for n in names}
        gw_in = [sem(f"gw_in{i}") for i in range(2)]
        block = ctx.enter_context(nc.Block())
        flat = {id(t): t[:, :, :].rearrange("p c n -> p (c n)") for t in (ra, ig, th)}
        raf, igf, thf = (flat[id(t)] for t in (ra, ig, th))
        sqf = xs[:, 0:NCH * CC]
        xsq = [t[:, :, 0:CH] for t in (ra, ig)]
        LRU_STEPS = 12
        LS8, NLS8 = 6, 7

        def samples(v, width):
            return v[:, 0:PCOL].rearrange("p (b s) -> p b s", s=SEG)[:, :, SEG - width:SEG]

        @block.sync
        def _(sp):
            sp.dma_start(st[:, :, :], a["conv_states"]).then_inc(S["small_in"], 16)
            sp.dma_start(h0[:, :, :], a["first_states"]).then_inc(S["small_in"], 16)

            def load_gates(n):
                if n >= 2:
                    sp.wait_ge(d.made, USE["i", n - 2] + 1)
                sp.dma_start(gw[:, n % 2, :, :], a["gate_w"][n]).then_inc(gw_in[n % 2], 16)

            for n in range(KD):
                if n < 2:
                    load_gates(n)
                for x in range(2):
                    d.load(sp, U_REC + 2 * n + x + 2, x)
                if n >= 2:
                    load_gates(n)
            for n in range(KD):
                d.load(sp, U_REC_OUT + n + 2, n % 2)
            sp.wait_ge(S["h_out"], KD)
            sp.wait_ge(S["tails"], KD)
            sp.dma_start(state_out, so[:, :, :]).then_inc(S["st_out"], 16)
            sp.wait_ge(S["st_out"], 16)

        @block.gpsimd
        def _(pool):
            nc.gpsimd.memset(xs[:, :], 0.0).then_inc(S["pad"], 1)
            nc.gpsimd.memset(cv[:, :, :, :], 0.0).then_inc(S["pad"], 1)
            nc.gpsimd.memset(hg[:, :, NCH - 1, TS + SEQ - CH * (NCH - 1):CH], 0.0).then_inc(S["pad"], 1)
            for n in range(KD + 1):
                if n < KD:
                    for x in range(2):
                        d.split_low(pool, U_REC + 2 * n + x + 2, x)
                if n >= 1:
                    m = n - 1
                    pool.wait_ge(S["decay"], m + 1)
                    pool.wait_ge(S["conv_done"], 4 * min(m + 2, KD))
                    pool.wait_ge(S["tails"], min(m + 2, KD))
                    if m == KD - 1:
                        pool.wait_ge(S["dual"], m)
                    nc.gpsimd.tensor_tensor(sqf, raf, raf, ALU.mult).then_inc(S["squared_a"], 1)
                    pool.wait_ge(S["conv_done"], 4 * (m + 1))
                    nc.gpsimd.tensor_tensor(ig[:, :, :], ig[:, :, :], cv[:, m % 2, :, :], ALU.mult).then_inc(S["gated_in"], 1)
            for n in range(KD):
                d.split_low(pool, U_REC_OUT + n + 2, n % 2)
                d.sum_up(pool, xsq, n, seen)

        @block.scalar
        def _(act):
            d.sums_act(act, nth, R_REC)
            lru = d.par[:, PAR_LRU, :]
            nc.scalar.activation(ls[:, 0, :], lru, ACT.Abs).then_inc(S["lru"], 1)
            act.wait_ge(S["lru"], 1)
            nc.scalar.activation(ls[:, 1, :], ls[:, 0, :], ACT.Exp, scale=-1.0).then_inc(S["lru"], 1)
            act.wait_ge(S["lru"], 3)
            nc.scalar.activation(ls[:, 3, :], ls[:, 2, :], ACT.Ln).then_inc(S["lru"], 1)

            def gelu(n):
                use = USE["g", n]
                act.wait_ge(d.taken[use % 2], use // 2 + 1)
                nc.scalar.activation(gm[n % 2][:, :], gm[n % 2][:, :], ACT.Gelu_apprx_tanh).then_inc(S["gelu"], 1)

            gelu(0)
            for n in range(1, KD + 1):
                m = n - 1
                if m == 0:
                    act.wait_ge(S["lru"], LRU_STEPS)
                for kind, dst, bias in (("a", ra, PAR_GA), ("i", ig, PAR_GX)):
                    use = USE[kind, m]
                    act.wait_ge(d.made, use + 1)
                    if m:
                        act.wait_ge(S["scanned"], m)
                    nc.scalar.activation(dst[:, :, :], ps[use % 2][:, :, 0:CC], ACT.Sigmoid, bias=d.par[:, bias, m:m + 1]
                                         ).then_inc(d.taken[use % 2], 1)
                act.wait_ge(d.taken[USE["a", m] % 2], USE["a", m] // 2 + 1)
                act.wait_ge(d.taken[USE["i", m] % 2], USE["i", m] // 2 + 1)
                if m:
                    act.wait_ge(S["hg_done"], 2 * m)
                    act.wait_ge(S["h_out"], m)
                nc.scalar.activation(thf, raf, ACT.Tanh, scale=ls[:, NLS8, m:m + 1]).then_inc(S["tanh"], 1)
                act.wait_ge(S["tanh"], m + 1)
                nc.scalar.activation(raf, raf, ACT.Exp, scale=ls[:, LS8, m:m + 1]).then_inc(S["decay"], 1)
                act.wait_ge(S["decay"], m + 1)
                act.wait_ge(S["dual"], m + 1)
                nc.scalar.activation(thf, thf, ACT.Sqrt).then_inc(S["root"], 1)
                if n < KD:
                    gelu(n)
            for k in range(KD):
                act.wait_ge(S["hg_done"], 2 * (k + 1))
                act.wait_ge(d.made, USE["g", KD - 1] + 1)
                act.wait_ge(S["pad"], 3)
                nc.scalar.activation(d.gh[:, k, :, :], hg[:, k, :, :], ACT.Copy).then_inc(S["gh"], 1)
            for n in range(KD):
                r = R_REC_OUT + n
                act.wait_ge(d.taken[r % 2], r // 2 + 1)
                d.square(act, xsq, n, seen)
            act.wait_ge(d.made, R_REC_OUT + KD)
            for n in range(KD):
                d.part_high(act, n, 2)

        @block.tensor
        def _(pe):
            d.sums_pe(pe, ps, nth, R_REC)
            pe.wait_ge(d.x_low, seen)

            def inputs(n):
                for x, kind in enumerate("xg"):
                    use, u = USE[kind, n], U_REC + 2 * n + x
                    pe.wait_ge(d.w_low, u + 1)
                    pe.wait_ge(d.taken[use % 2], use // 2)
                    d.product(pe, ps[use % 2], x, 0, KD, d.gh, d.gl)

            def gates(n):
                pe.wait_ge(gw_in[n % 2], 16 * (n // 2 + 1))
                pe.wait_ge(S["conv_done"], 4 * (n + 1))
                for x, kind in enumerate("ai"):
                    use = USE[kind, n]
                    pe.wait_ge(d.taken[use % 2], use // 2)
                    for c in range(NCH):
                        last = nc.tensor.matmul(ps[use % 2][:, c, 0:CC], gw[:, n % 2, x, :], cv[:, n % 2, c, :],
                                                start=True, stop=True)
                    last.then_inc(d.made, 1)

            inputs(0)
            for n in range(1, KD):
                inputs(n)
                gates(n - 1)
            gates(KD - 1)
            for n in range(KD):
                r = R_REC_OUT + n
                pe.wait_ge(d.w_low, U_REC_OUT + n + 1)
                pe.wait_ge(d.taken[r % 2], r // 2)
                d.product(pe, ps[r % 2], n % 2, 0, KD, d.gh, d.gl,
                          (lambda k: pe.wait_ge(S["gl"], k + 1)) if n == 0 else None)

        @block.vector
        def _(dve):
            def lru_step(ins):
                ins.then_inc(S["lru"], 1)

            d.sums_dve(dve, ps, nth, R_REC)
            e, u, ln, den, val = (ls[:, i, :] for i in (1, 2, 3, 4, 5))
            dve.wait_ge(S["lru"], 2)
            lru_step(nc.vector.tensor_scalar(u, e, 1.0, None, ALU.add))
            dve.wait_ge(S["lru"], 4)
            lru_step(nc.vector.tensor_scalar(den, u, 1.0, 1e-30, ALU.subtract, ALU.max))
            dve.wait_ge(S["lru"], 5)
            lru_step(nc.vector.reciprocal(val, den))
            dve.wait_ge(S["lru"], 6)
            lru_step(nc.vector.tensor_tensor(val, val, e, ALU.mult))
            dve.wait_ge(S["lru"], 7)
            lru_step(nc.vector.tensor_tensor(val, val, ln, ALU.mult))
            dve.wait_ge(S["lru"], 8)
            lru_step(nc.vector.scalar_tensor_tensor(out=den, in0=u, scalar=1.0, in1=e, op0=ALU.is_equal, op1=ALU.mult))
            dve.wait_ge(S["lru"], 9)
            lru_step(nc.vector.tensor_tensor(val, val, den, ALU.add))
            dve.wait_ge(S["lru"], 10)
            lru_step(nc.vector.scalar_tensor_tensor(out=den, in0=d.par[:, PAR_LRU, :], scalar=0.0, in1=val,
                                                    op0=ALU.min, op1=ALU.subtract))
            dve.wait_ge(S["lru"], 11)
            nc.vector.tensor_scalar(ls[:, LS8, :], den, LRU_C, None, ALU.mult)
            lru_step(nc.vector.tensor_scalar(ls[:, NLS8, :], den, -LRU_C, None, ALU.mult))
            dve.wait_ge(S["small_in"], 32)
            dve.wait_ge(S["pad"], 3)

            def convolve(n):
                use = USE["x", n]
                z = ps[use % 2]
                dve.wait_ge(d.made, use + 1)
                if n:
                    dve.wait_ge(S["tails"], n)
                    dve.wait_ge(S["conv_done"], 4 * n)
                if n >= 2:
                    dve.wait_ge(S["dual"], n - 1)
                nc.vector.memset(xs[:, PCOL:PCOL + CONVW - 1], 0.0).then_inc(S["states_copied"], 1)
                nc.vector.tensor_copy(xs[:, 0:PCOL].rearrange("p (b s) -> p b s", s=SEG)[:, :, 0:CONVW - 1],
                                      st[:, n, :].rearrange("p (b s) -> p b s", b=DB)).then_inc(S["states_copied"], 1)
                nc.vector.tensor_tensor(samples(xs, DT), z[:, 0, 0:TS].rearrange("p (b t) -> p b t", b=DB),
                                        d.rstd[:, 0, 0:TS].rearrange("p (b t) -> p b t", b=DB), ALU.mult)
                at = PCOL + CONVW - 1
                for c in range(NCH):
                    lo, hi = (TS if c == 0 else 0), (CH if c < NCH - 1 else TS + SEQ - CH * (NCH - 1))
                    last = nc.vector.tensor_tensor(xs[:, at:at + hi - lo], z[:, c, lo:hi], d.rstd[:, c, lo:hi], ALU.mult)
                    at += hi - lo
                last.then_inc(d.taken[use % 2], 1)
                dve.wait_ge(d.taken[use % 2], use // 2 + 1)
                if n >= 2:
                    dve.wait_ge(d.made, USE["i", n - 2] + 1)
                    dve.wait_ge(S["gated_in"], n - 1)
                dve.wait_ge(S["states_copied"], 2 * (n + 1))
                v = cv[:, n % 2, :, :].rearrange("p c n -> p (c n)")[:, 0:CONV]
                par = lambda i: d.par[:, i, n:n + 1]
                nc.vector.tensor_scalar(v, xs[:, 0:CONV], par(PAR_CONV), par(PAR_CB), ALU.mult, ALU.add).then_inc(S["conv_done"], 1)
                for i in range(1, CONVW):
                    dve.wait_ge(S["conv_done"], 4 * n + i)
                    nc.vector.scalar_tensor_tensor(out=v, in0=xs[:, i:i + CONV], scalar=par(PAR_CONV + i), in1=v,
                                                   op0=ALU.mult, op1=ALU.add).then_inc(S["conv_done"], 1)
                nc.vector.tensor_copy(so[:, n, 0:24].rearrange("p (b s) -> p b s", b=DB), samples(xs, CONVW - 1))
                nc.vector.tensor_copy(so[:, n, 24:27], xs[:, EXT - (CONVW - 1):EXT]).then_inc(S["tails"], 1)

            def scale_gate(n):
                use = USE["g", n]
                dve.wait_ge(d.made, use + 1)
                if n >= 2:
                    dve.wait_ge(S["hg_done"], 2 * (n - 1))
                nc.vector.tensor_tensor(gm[n % 2][:, :].rearrange("p (c n) -> p c n", c=NCH), ps[use % 2][:, :, 0:CH],
                                        d.rstd[:, :, :], ALU.mult).then_inc(d.taken[use % 2], 1)

            def recur(m):
                dve.wait_ge(S["squared_a"], m + 1)
                dve.wait_ge(S["tanh"], m + 1)
                nc.vector.scalar_tensor_tensor(out=thf, in0=sqf, scalar=1.0, in1=thf, op0=ALU.add, op1=ALU.mult).then_inc(S["dual"], 1)
                dve.wait_ge(S["root"], m + 1)
                dve.wait_ge(S["gated_in"], m + 1)
                nc.vector.tensor_tensor(igf, igf, thf, ALU.mult).then_inc(S["drive"], 1)
                dve.wait_ge(S["drive"], m + 1)
                last_of = lambda v: v[:, 0:PCOL].rearrange("p (b s) -> p b s", s=SEG)[:, :, SEG - 1:SEG]
                nc.vector.memset(last_of(raf), 0.0).then_inc(S["fixed"], 1)
                nc.vector.tensor_copy(last_of(igf), h0[:, m, 1:DB + 1].rearrange("p (b o) -> p b o", o=1)).then_inc(S["fixed"], 1)
                dve.wait_ge(S["fixed"], 2 * (m + 1))
                nc.vector.tensor_tensor_scan(thf[:, 0:CONV], raf[:, 0:CONV], igf[:, 0:CONV], h0[:, m, 0:1], ALU.mult, ALU.add
                                             ).then_inc(S["scanned"], 1)
                dve.wait_ge(S["scanned"], m + 1)
                dve.wait_ge(S["gelu"], m + 1)
                hgf = hg[:, m, :, :].rearrange("p c n -> p (c n)")
                seq = lambda v: v[:, 0:TS].rearrange("p (b t) -> p b t", b=DB)
                nc.vector.tensor_tensor(seq(hgf), thf[:, 0:PCOL].rearrange("p (b s) -> p b s", s=SEG)[:, :, 0:DT],
                                        seq(gm[m % 2][:, :]), ALU.mult).then_inc(S["hg_done"], 1)
                nc.vector.tensor_tensor(hgf[:, TS:TS + SEQ], thf[:, PCOL:CONV], gm[m % 2][:, TS:TS + SEQ], ALU.mult
                                        ).then_inc(S["hg_done"], 1)
                nc.vector.tensor_copy(so[:, m, 27:35].rearrange("p (b o) -> p b o", o=1),
                                      thf[:, 0:PCOL].rearrange("p (b s) -> p b s", s=SEG)[:, :, DT - 1:DT])
                nc.vector.tensor_copy(so[:, m, 35:36], thf[:, CONV - 1:CONV]).then_inc(S["h_out"], 1)

            for n in range(KD):
                convolve(n)
                d.split_high(dve, 0, (U_REC + 2 * n + 2) // 2, USE["x", n] + 1)
                scale_gate(n)
                d.split_high(dve, 1, (U_REC + 2 * n + 3) // 2, USE["g", n] + 1)
                if n:
                    recur(n - 1)
            recur(KD - 1)
            for k in range(KD):
                dve.wait_ge(S["gh"], k + 1)
                nc.vector.tensor_tensor(d.gl[:, k, :, :], hg[:, k, :, :], d.gh[:, k, :, :].bitcast(F32), ALU.subtract
                                        ).then_inc(S["gl"], 1)
            for n in range(KD):
                r = R_REC_OUT + n
                dve.wait_ge(d.made, r + 1)
                nc.vector.tensor_tensor(d.x[:, n, :, :], d.x[:, n, :, :], ps[r % 2][:, :, 0:CH], ALU.add
                                        ).then_inc(d.taken[r % 2], 1)
                d.split_high(dve, n % 2, (U_REC_OUT + n + 2) // 2, r + 1)
            dve.wait_ge(d.taken[(R_REC_OUT + KD - 1) % 2], (R_REC_OUT + KD - 1) // 2 + 1)
            for n in range(KD):
                d.part_low(dve, n, seen, 2)


def device_inputs(x):
    f = lambda v: np.ascontiguousarray(v, dtype=np.float32)
    tok = np.zeros((TOK, D), np.float32)
    tok[0:TS] = np.asarray(x["x_sample"]).reshape(TS, D)
    tok[TS:TS + SEQ] = np.asarray(x["x_prompt"]).reshape(SEQ, D)
    w = np.asarray(x["attn_w_in"])[0]
    qa, ka, va, qi, ki, wi, hb = np.split(w, [512, 640, 768, 1280, 1344, 1352], axis=1)
    w = np.concatenate([ki, wi, qi, qa, ka, va, hb], axis=1).reshape(KD, P, IN_W)
    norms = [np.asarray(x["a_q_norm"])[0], np.asarray(x["a_k_norm"])[0]]
    for g in range(NG):
        norms += [np.asarray(x["b_q_norm"])[0, g], np.asarray(x["b_k_norm"])[0, g]]
    steps = np.arange(TS) % DT
    d = {
        "xt": f(tok.T.reshape(KD, P, TOK)),
        "norm_mix0": f(np.asarray(x["norm_mix"])[0].reshape(KD, P).T),
        "rel_bias": f(x["rel_bias"]),
        "bias_pick": bias_selector(),
        "w_in": f(w),
        "head_gains": f(np.stack(norms)),
        "same_step": f(steps[:, None] == np.arange(DT)[None]),
        "later_step": f(np.where(np.arange(DT)[None] > steps[:, None], NEG, 0.0)),
        "page_table": np.ascontiguousarray(np.asarray(x["page_table"]).reshape(1, -1), dtype=np.int32),
        "kv_keys_t": f(np.asarray(x["cache_a_kv"])[0, :, :, 0].reshape(-1, PAGE, P).transpose(0, 2, 1)),
        "kv_values": f(np.asarray(x["cache_a_kv"])[0, :, :, 1].reshape(-1, PAGE, P)),
        "kidx_t": f(np.asarray(x["cache_a_kidx"])[0].transpose(0, 2, 1)),
    }
    for g in range(NG):
        c = np.asarray(x[f"cache_b_kv_w{WIN[g]}"])[0]
        d[f"win_keys_t{g}"] = f(c[:, :, 0].reshape(DB, WL[g], 2, P).transpose(0, 3, 2, 1).reshape(DB, P, 2 * WL[g]))
        d[f"win_cache{g}"] = f(c.reshape(DB, WL[g], 2 * BW))
    units = np.zeros((U_END, P, KD, P), np.float32)

    def tiles(w):
        return np.asarray(w).reshape(w.shape[0] // P, P, w.shape[1] // P, P)

    units[U_OUT:U_OUT + KD, :, 0:6] = tiles(np.asarray(x["attn_w_out"])[0]).transpose(2, 1, 0, 3)
    for l in range(2):
        up = tiles(np.asarray(x["mlp_w1"])[l]).transpose(2, 1, 0, 3)
        down = tiles(np.asarray(x["mlp_w2"])[l])
        for b in range(NBLK):
            u = U_MLP[l] + BLK_U * b
            units[u:u + NF] = up[NF * b:NF * (b + 1)]
            for m in range(NF):
                units[u + NF + m] = down[NF * b:NF * (b + 1), :, 2 * m:2 * m + 2].transpose(1, 2, 0, 3).reshape(P, KD, P)
    rec = tiles(np.asarray(x["rec_w_in"])[0]).transpose(2, 1, 0, 3)
    units[U_REC:U_REC_OUT:2] = rec[KD:]
    units[U_REC + 1:U_REC_OUT:2] = rec[:KD]
    units[U_REC_OUT:U_REC_OUT + KD] = tiles(np.asarray(x["rec_w_out"])[0]).transpose(2, 1, 0, 3)
    d["w_units"] = units.reshape(U_END, P, KD * P)
    par = [np.asarray(x["norm_mlp"])[0], np.asarray(x["norm_mix"])[1], np.asarray(x["norm_mlp"])[1],
           *np.asarray(x["rec_conv_w"])[0], np.asarray(x["rec_conv_b"])[0], np.asarray(x["rec_gate_a_b"])[0],
           np.asarray(x["rec_gate_x_b"])[0], np.asarray(x["rec_lru_a"])[0]]
    d["dense_params"] = f(np.stack(par).reshape(NPAR, KD, P).transpose(2, 0, 1))
    d["conv_states"] = f(np.asarray(x["state_c_conv"])[0].reshape(DB, CONVW - 1, KD, P).transpose(3, 2, 0, 1).reshape(P, KD, -1))
    h0 = np.zeros((P, KD, DB + 1), np.float32)
    h0[:, :, 0:DB] = np.asarray(x["state_c_h"])[0].reshape(DB, KD, P).transpose(2, 1, 0)
    d["first_states"] = h0
    d["gate_w"] = f(np.stack([np.asarray(x["rec_gate_a_w"])[0], np.asarray(x["rec_gate_x_w"])[0]], 2))
    return d


def device_outputs():
    out = {"y_t": (KD, P, TOK), "kv_a": (TS + SEQ, 2 * AG * HD), "ki": (TS + SEQ, IDX), "state_out": (P, KD, 36)}
    for g in range(NG):
        out[f"p_win{g}"] = (min(WIN[g], SEQ), 2 * BW)
        out[f"s_win{g}"] = (DB, WL[g], 2 * BW)
    return out


def results(r):
    y = r["y_t"].reshape(D, TOK).T
    kv = r["kv_a"].reshape(TS + SEQ, 2, AG, HD)
    so = r["state_out"].transpose(2, 1, 0).reshape(36, D)
    shape = lambda v, *s: np.ascontiguousarray(v).reshape(s)
    pw = [shape(r[f"p_win{g}"], 1, 1, min(WIN[g], SEQ), 2, BH, HD) for g in range(NG)]
    sw = [shape(r[f"s_win{g}"], 1, DB, WL[g], 2, BH, HD) for g in range(NG)]
    return (shape(y[TS:TS + SEQ], 1, SEQ, D), shape(y[0:TS], DB, DT, D),
            shape(kv[TS:], 1, 1, SEQ, 2, AG, HD), shape(r["ki"][TS:], 1, 1, SEQ, IDX), *pw,
            shape(so[35], 1, 1, D), shape(so[24:27], 1, 1, CONVW - 1, D),
            shape(kv[:TS], 1, DB, DT, 2, AG, HD), shape(r["ki"][:TS], 1, DB, DT, IDX), *sw,
            shape(so[27:35], 1, DB, D), shape(so[0:24], 1, DB, CONVW - 1, D))


def kernel(**inputs):
    from concourse import bacc
    from concourse.bass_utils import run_bass_kernel_spmd

    arrays = device_inputs(inputs)
    nc = bacc.Bacc("TRN2", target_bir_lowering=False, num_devices=1)
    a = {k: nc.dram_tensor(k, v.shape, mybir.dt.from_np(v.dtype), kind="ExternalInput").ap() for k, v in arrays.items()}
    o = {k: nc.dram_tensor(k, s, F32, kind="ExternalOutput").ap() for k, s in device_outputs().items()}
    build_program(nc, a, o)
    r = run_bass_kernel_spmd(nc, [arrays], core_ids=[0])
    return results(r.results[0])
```

```python
import math
from contextlib import ExitStack

import numpy as np

import concourse.bass as bass
from concourse import mybir

F32 = mybir.dt.float32
F32R = mybir.dt.float32r
I32 = mybir.dt.int32
ALU = mybir.AluOpType
ACT = mybir.ActivationFunctionType
AX_X = mybir.AxisListType.X

P = 128
D = 1024
KD = D // P
SEQ = 1024
DB, DT = 8, 8
TS = DB * DT
CH, NCH = 364, 3
TOK = CH * NCH
NT = 9
HD = 64
AH, AG = 8, 2
REP = AH // AG
IH, IDX = 8, 64
NG, BH = 3, 4
WIN, DIL = (128, 512, 2048), (1, 4, 16)
BW = BH * HD
PAST, PAGE = 256, 128
NPAGE = PAST // PAGE
WL = tuple(min(w, PAST) for w in WIN)
TOPK = min(256, SEQ // 4)
STOPK = min(256, (PAST + DT) // 4)
SKEYS = PAST + DT
NBUCKET, MAXDIST = 32, 2048
NBH = AH + NG * BH
FF = 4 * D
FBLK = 1024
CONVW = 4
EPS = 1e-6
NEG = -1e30
SENT = -3.0e38
HUGE = 3.0e38
LRU_C = 8.0

PROJ_W = AH * HD + 2 * AG * HD + NG * 3 * BW
KIWI = IDX + IH
GROUPS = [("kikv", KIWI + 256, [(0, 256, 512)]), ("qi", 512, []), ("qa", 512, [(0, 512, 0)])]
GROUPS += [(f"qk{_g}", 512, [(0, 512, 768 + 768 * _g)]) for _g in range(NG)]
GROUPS += [("v01", 512, [(256 * _g, 256, 768 + 768 * _g + 512) for _g in range(2)]), ("v2", 256, [(0, 256, 768 * 3 + 512)])]
GOFF = [sum(g[1] for g in GROUPS[:i]) for i in range(len(GROUPS) + 1)]
IN_W = GOFF[-1]
N_GAIN = 2 + 2 * NG

TAB_A = SEQ + P
TAB_B = 384
TAB_S = tuple(-(-(wl + 15) // 16) * 16 for wl in WL)
TAB_OFF_B = [TAB_A + TAB_B * g for g in range(NG)]
TAB_OFF_S = [TAB_A + TAB_B * NG + sum(TAB_S[:g]) for g in range(NG)]
NTAB = TAB_A + TAB_B * NG + sum(TAB_S)


def bucket(dist):
    half = NBUCKET // 2
    d = np.maximum(dist, 0)
    df = np.maximum(d, 1).astype(np.float32)
    large = half + (np.log(df / np.float32(half)) / np.float32(math.log(MAXDIST / half))
                    * np.float32(NBUCKET - half)).astype(np.int32)
    return np.where(d < half, d, np.minimum(large, NBUCKET - 1))


def bias_selector():
    cols = np.zeros((NBUCKET + 1, NTAB), np.float32)

    def put(off, dist, ok):
        b = bucket(dist)
        for i in range(len(dist)):
            if ok[i]:
                cols[b[i], off + i] = 1.0
            else:
                cols[NBUCKET, off + i] = NEG

    d = SEQ - 1 - np.arange(TAB_A)
    put(0, d, d >= 0)
    for g in range(NG):
        s = 255 - np.arange(TAB_B)
        put(TAB_OFF_B[g], s * DIL[g], (s >= 0) & (s <= P))
        d = WL[g] + 7 - np.arange(TAB_S[g])
        put(TAB_OFF_S[g], d, (d >= 0) & (d <= WIN[g]) & (d % DIL[g] == 0))
    return cols


def tile_col(i):
    return 0 if i == 0 else TS + P * (i - 1)


def tile_rows(i):
    return TS if i == 0 else P


SEL_TILES = list(range(2, 8))
WORK_OFF = {}
_o = 0
for _j in SEL_TILES:
    WORK_OFF[_j] = _o
    _o += P * (_j + 1)
WORK_W = _o
ROUNDS = [(j, r) for j in SEL_TILES for r in range(TOPK // 8)]
ROUNDS_1, ROUNDS_2 = 114, 142
assert ROUNDS[ROUNDS_2][0] >= SEL_TILES[-2]


def build_program(nc, a, o):
    def dram(name, *shape):
        return nc.dram_tensor(name, shape, F32).ap()

    proj = dram("proj_rows", TS + SEQ, PROJ_W)
    kiwi = dram("kiwi_rows", TS + SEQ, 72)
    table = dram("bias_rows", NBH, NTAB)
    strips = dram("bias_strips", AH, P, SEQ)
    wstrips = dram("window_strips", NG * BH, P, 2 * P)
    smask = dram("sample_mask", TS, SKEYS)
    oa = dram("sparse_rows", TS + SEQ, AH * HD)
    obp = dram("window_rows", NG, TS + SEQ, OBW)
    oas = dram("sample_sparse_rows", DB // 2, P, P)
    obs = dram("sample_window_rows", NG, DB // 4, P, OBW)
    with ExitStack() as ctx:
        ident = ctx.enter_context(nc.sbuf_tensor("ident", [P, P], F32))
        own = OwnRows(nc, ctx, oas, obs)
        with ExitStack() as c1:
            work = c1.enter_context(nc.sbuf_tensor("select_work", [P, WORK_W], F32))
            with ExitStack() as c2:
                xh = c2.enter_context(nc.sbuf_tensor("x_high", [P, KD, TOK], F32R))
                xl = c2.enter_context(nc.sbuf_tensor("x_low", [P, KD, TOK], F32R))
                rstd = c2.enter_context(nc.sbuf_tensor("rstd_rows", [P, NT], F32))
                stage_start(nc, a, xh, xl, rstd, ident, table)
                stage_project(nc, a, xh, xl, rstd, ident, work, proj, kiwi, smask, table, strips, wstrips)
            used = sorted(int(s) for s in nc.released_uncleared_semaphores)
            assert used == list(range(used[0], used[0] + len(used)))
            with ExitStack() as c2:
                smp = Samples(nc, c2)
                with ExitStack() as c3:
                    keys = SparseKeys(nc, c3)
                    stage_window(nc, a, ident, work, proj, wstrips, obp, keys, strips)
                    stage_sparse(nc, a, ident, work, proj, oa, keys, smp, table, smask, used)
                stage_sample(nc, a, ident, smp, proj, oas, obs, own)
        d = Dense(nc, ctx, a)
        with ExitStack() as c1:
            oth = c1.enter_context(nc.sbuf_tensor("mixed_high", [P, 6, NCH, CH], F32R))
            otl = c1.enter_context(nc.sbuf_tensor("mixed_low", [P, 6, NCH, CH], F32R))
            stage_merge(nc, a, d, ident, oa, obp, own, oth[:, :, :, :].rearrange("p k c n -> p k (c n)"),
                        otl[:, :, :, :].rearrange("p k c n -> p k (c n)"))
            stage_out_projection(nc, a, d, oth, otl)
        stage_mlp(nc, a, d, 0, 0)
        stage_recurrent(nc, a, o, d, 1, proj, kiwi, own)
        stage_mlp(nc, a, d, 1, 2, o["y_t"])


def topk_round(nc, link, work, m8, n):
    j, r = ROUNDS[n]
    v = work[:, WORK_OFF[j]:WORK_OFF[j] + P * (j + 1)]
    link(nc.vector.max(m8[:, :], v))
    link(nc.vector.match_replace(v, m8[:, :], v, SENT))
    if r == TOPK // 8 - 1:
        link(nc.vector.tensor_scalar(v, v, SENT, NEG, ALU.not_equal, ALU.mult))


def stage_start(nc, a, xh, xl, rstd, ident, table):
    with ExitStack() as ctx:
        def sb(name, shape, dt=F32):
            return ctx.enter_context(nc.sbuf_tensor(name, shape, dt))

        def sem(name):
            return ctx.enter_context(nc.semaphore(name))

        xraw = sb("s0_x", [P, 2, TOK])
        xv = sb("s0_xg", [P, 2, TOK])
        sq = sb("s0_sq", [P, 2, TOK])
        ssum = sb("s0_sum", [P, TOK])
        gain = sb("s0_gain", [P, KD])
        ones = sb("s0_ones", [P, 2])
        relb = sb("s0_relb", [NBUCKET + 1, NBH])
        pick = sb("s0_pick", [NBUCKET + 1, NTAB])
        tab = sb("s0_tab", [NBH, NTAB])
        ms = sb("s0_ms", [P, 2, NT])
        ps_t = [ctx.enter_context(nc.psum_tensor(f"s0_ps{i}", [P, 512], F32)) for i in range(7)]
        NTC = -(-NTAB // 512)
        assert NTC <= 6
        x_in = [sem(f"s0_x_in{i}") for i in range(2)]
        gain_in, tab_in = sem("s0_gain_in"), sem("s0_tab_in")
        high, squared, scaled, low, summed = (sem(f"s0_{n}") for n in ("high", "squared", "scaled", "low", "summed"))
        filled, tab_mm, tab_sb, tab_out = (sem(f"s0_{n}") for n in ("filled", "tab_mm", "tab_sb", "tab_out"))
        sum_mm, ms_dve, root = (sem(f"s0_{n}") for n in ("sum_mm", "ms_dve", "root"))
        block = ctx.enter_context(nc.Block())

        @block.sync
        def _(sp):
            sp.dma_start(gain[:, :], a["norm_mix0"]).then_inc(gain_in, 16)
            for k in range(KD):
                if k >= 2:
                    sp.wait_ge(squared, k - 1)
                    sp.wait_ge(scaled, k - 1)
                sp.dma_start(xraw[:, k % 2, :], a["xt"][k]).then_inc(x_in[k % 2], 16)
                if k == 1:
                    sp.wait_ge(filled, 1)
                    sp.dma_start(relb[0:NBUCKET, :], a["rel_bias"]).then_inc(tab_in, 16)
                    sp.dma_start(pick[:, :], a["bias_pick"]).then_inc(tab_in, 16)
            sp.wait_ge(tab_sb, NTC)
            sp.dma_start(table, tab[:, :]).then_inc(tab_out, 16)
            sp.wait_ge(tab_out, 16)

        @block.gpsimd
        def _(pool):
            nc.gpsimd.memset(relb[:, :], 1.0).then_inc(filled, 1)
            nc.gpsimd.memset(ones[:, :], 1.0).then_inc(filled, 1)
            nc.gpsimd.memset(ident[:, :], 0.0).then_inc(filled, 1)
            pool.wait_ge(filled, 3)
            nc.gpsimd.affine_select(out=ident[:, :], in_=ident[:, :], compare_op=ALU.not_equal, fill=1.0,
                                    base=0, pattern=[[-1, P]], channel_multiplier=1).then_inc(filled, 1)
            for k in range(KD):
                pool.wait_ge(squared, k + 1)
                if k == 0:
                    continue
                if k >= 2:
                    pool.wait_ge(summed, k - 1)
                first = sq[:, 0, :] if k == 1 else ssum[:, :]
                nc.gpsimd.tensor_tensor(ssum[:, :], first, sq[:, k % 2, :], ALU.add).then_inc(summed, 1)

        @block.scalar
        def _(act):
            act.wait_ge(gain_in, 16)
            for k in range(KD):
                act.wait_ge(x_in[k % 2], 16 * (k // 2 + 1))
                nc.scalar.activation(xh[:, k, :], xraw[:, k % 2, :], ACT.Copy, scale=gain[:, k:k + 1]).then_inc(high, 1)
                if k >= 2:
                    act.wait_ge(summed, k - 1)
                nc.scalar.activation(sq[:, k % 2, :], xraw[:, k % 2, :], ACT.Square).then_inc(squared, 1)
            for c in range(NTC):
                w = min(512, NTAB - 512 * c)
                act.wait_ge(tab_mm, c + 1)
                nc.scalar.activation(tab[:, 512 * c:512 * c + w], ps_t[c][0:NBH, 0:w], ACT.Copy).then_inc(tab_sb, 1)
            act.wait_ge(ms_dve, 1)
            nc.scalar.activation(ms[:, 1, :], ms[:, 0, :], ACT.Sqrt).then_inc(root, 1)

        @block.vector
        def _(dve):
            dve.wait_ge(gain_in, 16)
            for k in range(KD):
                dve.wait_ge(x_in[k % 2], 16 * (k // 2 + 1))
                if k >= 2:
                    dve.wait_ge(low, k - 1)
                nc.vector.tensor_scalar(xv[:, k % 2, :], xraw[:, k % 2, :], gain[:, k:k + 1], None, ALU.mult).then_inc(scaled, 1)
                dve.wait_ge(high, k + 1)
                dve.wait_ge(scaled, k + 1)
                nc.vector.tensor_tensor(xl[:, k, :], xv[:, k % 2, :], xh[:, k, :].bitcast(F32), ALU.subtract).then_inc(low, 1)
            dve.wait_ge(sum_mm, 1)
            nc.vector.tensor_scalar(ms[:, 0, :], ps_t[6][:, 0:NT], 1.0 / D, EPS, ALU.mult, ALU.add).then_inc(ms_dve, 1)
            dve.wait_ge(root, 1)
            nc.vector.reciprocal(rstd[:, :], ms[:, 1, :]).then_inc(ms_dve, 1)

        @block.tensor
        def _(pe):
            pe.wait_ge(filled, 4)
            pe.wait_ge(tab_in, 32)
            for c in range(NTC):
                w = min(512, NTAB - 512 * c)
                nc.tensor.matmul(ps_t[c][0:NBH, 0:w], relb[:, :], pick[:, 512 * c:512 * c + w],
                                 start=True, stop=True).then_inc(tab_mm, 1)
            pe.wait_ge(summed, KD - 1)
            for i in range(NT):
                c0 = tile_col(i)
                last = nc.tensor.matmul(ps_t[6][:, i:i + 1], ssum[:, c0:c0 + P], ones[:, 0:1], start=True, stop=True)
            last.then_inc(sum_mm, 1)


def stage_project(nc, a, xh, xl, rstd, ident, work, proj, kiwi, smask, table, strips, wstrips):
    NGR = len(GROUPS)
    SELS = [(j, h) for j in SEL_TILES for h in range(IH)]
    SR = STOPK // 8
    SREST = STOPK % 8
    SPAD = 8 - SREST
    with ExitStack() as ctx:
        def sb(name, shape, dt=F32):
            return ctx.enter_context(nc.sbuf_tensor(name, shape, dt))

        def sem(name):
            return ctx.enter_context(nc.semaphore("p1_" + name))

        NST = 3
        wh = [sb(f"w_high{i}", [P, KD, 512], F32R) for i in range(2)]
        wl = [sb(f"w_low{i}", [P, KD, 512], F32R) for i in range(2)]
        NRAW = 3
        wraw = sb("w_raw", [P, NRAW, 512])
        st = sb("rows", [P, NST, 512])
        sqr = sb("rows_sq", [P, 2, 512])
        gains = sb("gain_rows", [P, N_GAIN, HD])
        hs = sb("head_sums", [P, 2, 8])
        hm = sb("head_means", [P, 2, 8])
        hr = sb("head_roots", [P, 2, 8])
        hi = sb("head_inverse", [P, 2, 8])
        kk = sb("kiwi_sb", [P, NT, 136])
        wsc = sb("index_weights", [P, NT, 8])
        kit = sb("index_keys_t", [P, TS + SEQ])
        qt = sb("index_queries_t", [P, 2, 512])
        qst = sb("sample_queries_t", [HD, DB, IH * DT])
        rl = sb("relu_scores", [P, 2, SEQ])
        kpt = sb("page_keys_t", [HD, DB * NPAGE, PAGE])
        wks = sb("sample_work", [TS, SKEYS + SPAD])
        m8 = sb("top8", [P, 8])
        wt = sb("sample_w_t", [TS, DB])
        wts = sb("sample_w_scaled", [TS, DB])
        wb = sb("sample_w_blocks", [TS, DB, TS])
        same = sb("same_mask", [TS, DT])
        late = sb("later_mask", [TS, DT])
        pt = sb("pages", [1, DB * NPAGE], I32)
        ps = [ctx.enter_context(nc.psum_tensor(f"proj_ps{i}", [P, 512], F32)) for i in range(3)]
        pss = [ctx.enter_context(nc.psum_tensor(f"score_ps{i}", [P, 1024], F32)) for i in range(2)]
        psx = ctx.enter_context(nc.psum_tensor("turn_ps", [P, 512], F32))

        names = ("w_high w_low proj copied squared summed meaned rooted inverted normed gained "
                 "small_in pages_in keys_in kiwi_copied kiwi_out wt_in w_scaled turned turn_taken "
                 "scored relued added masked topk wt_ready zeroed s_mixed s_taken mask_out strips_out").split()
        S = {n: sem(n) for n in names}
        stored = [sem(f"stored{i}") for i in range(NST)]
        w_in = [sem(f"w_in{i}") for i in range(NRAW)]
        block = ctx.enter_context(nc.Block())

        def width(gi):
            return GROUPS[gi][1]

        def rows_n(gi, i):
            return NT * gi + i

        def stored_total(n):
            return 16 * sum(len(GROUPS[m // NT][2]) for m in range(n % NST, n + 1, NST))

        def kinds(gi):
            name = GROUPS[gi][0]
            if name == "qa":
                return [(0, 8, 0, True)]
            if name == "kikv":
                return [(0, AG, 1, False)]
            if name[:2] == "qk":
                g = int(name[2])
                return [(0, BH, 2 + 2 * g, True), (BH, BH, 3 + 2 * g, False)]
            return []

        NORMED = [(gi, i) for gi in range(NGR) if kinds(gi) for i in range(NT)]
        NORM_AT = {x: n for n, x in enumerate(NORMED)}
        GAIN_OPS = {x: sum(len(kinds(y[0])) for y in NORMED[:n + 1]) for n, x in enumerate(NORMED)}
        TURN_Q = {0: 4, **{j: 5 + n for n, j in enumerate(SEL_TILES)}}

        TURN_ROWS = {0: TURN_Q[0], **{j + 1: TURN_Q[j] for j in SEL_TILES}}
        KEY_TURNS = [(0, TS + 3 * P), (TS + 3 * P, TS + 7 * P), (TS + 7 * P, TS + 8 * P)]

        @block.sync
        def _(sp):
            sp.dma_start(pt[:, :], a["page_table"]).then_inc(S["pages_in"], 16)
            sp.dma_start(gains[:, :, :], a["head_gains"].partition_broadcast(P)).then_inc(S["small_in"], 16)
            sp.dma_start(same[:, :], a["same_step"]).then_inc(S["small_in"], 16)
            sp.dma_start(late[:, :], a["later_step"]).then_inc(S["small_in"], 16)

            def load_w(gi, k):
                u = KD * gi + k
                if u >= NRAW:
                    sp.wait_ge(S["w_low"], u - NRAW + 1)
                sp.dma_start(wraw[:, u % NRAW, 0:width(gi)],
                             a["w_in"][k, :, GOFF[gi]:GOFF[gi + 1]]).then_inc(w_in[u % NRAW], 16)

            for k in range(KD):
                load_w(0, k)
            sp.wait_ge(S["pages_in"], 16)

            def load_page(n):
                page = sp.value_load(pt[0:1, n:n + 1], min_val=0, max_val=a["kidx_t"].shape[0] - 1)
                sp.dma_start(kpt[:, n, :], a["kidx_t"][bass.ds(page, 1), :, :].rearrange("o d n -> d (o n)")
                             ).then_inc(S["keys_in"], 16)

            def store(gi, i):
                r, c = tile_rows(i), tile_col(i)
                n = rows_n(gi, i)
                if kinds(gi):
                    sp.wait_ge(S["gained"], GAIN_OPS[gi, i])
                sp.wait_ge(S["copied"], n + 1)
                for c0, w, off in GROUPS[gi][2]:
                    sp.dma_start(proj[c:c + r, off:off + w], st[0:r, n % NST, c0:c0 + w]).then_inc(stored[n % NST], 16)

            shifts = [(strips[h:h + 2], h * NTAB, 2, SEQ) for h in range(0, AH, 2)]
            shifts += [(wstrips[BH * g:BH * (g + 1)], (AH + BH * g) * NTAB + TAB_OFF_B[g], BH, 2 * P) for g in range(NG)]
            steps = [(gi, i) for gi in range(NGR) for i in range(NT)]
            for x, (gi, i) in enumerate(steps):
                if gi == 1:
                    for n in range(2 * i, min(2 * i + 2, DB * NPAGE)):
                        load_page(n)
                if gi == 1 and i < len(shifts):
                    dst, off, nh, w = shifts[i]
                    sp.dma_start(dst, bass.AP(tensor=table.tensor, offset=off + P - 1, ap=[[NTAB, nh], [-1, P], [1, w]])
                                 ).then_inc(S["strips_out"], 16)
                if gi + 1 < NGR and i < KD:
                    load_w(gi + 1, i)
                if gi == 0:
                    r, c = tile_rows(i), tile_col(i)
                    sp.wait_ge(S["kiwi_copied"], i + 1)
                    sp.dma_start(kiwi[c:c + r, :], kk[0:r, i, 64:136]).then_inc(S["kiwi_out"], 16)
                    if i == 1:
                        sp.wait_ge(S["kiwi_out"], 16 * 2)
                        for h in range(IH):
                            src = bass.AP(tensor=kiwi.tensor, offset=64 + h, ap=[[72, DT], [72 * DT, DB]])
                            with nc.allow_non_contiguous_dma(reason="512 words, once"):
                                sp.dma_start(wt[DT * h:DT * h + DT, :], src).then_inc(S["wt_in"], 16)
                if x >= 2 and steps[x - 2][0] != 1:
                    store(*steps[x - 2])
            store(*steps[-2])
            store(*steps[-1])
            sp.wait_ge(S["topk"], 2 * SR + 2 * (SREST > 0) + 1)
            sp.dma_start(smask, wks[:, 0:SKEYS]).then_inc(S["mask_out"], 16)
            sp.wait_ge(S["mask_out"], 16)
            sp.wait_ge(S["strips_out"], 16 * len(shifts))
            for q in range(NST):
                sp.wait_ge(stored[q], stored_total(NT * NGR - NST + q))
            sp.wait_ge(S["kiwi_out"], 16 * NT)

        def split_unit_low(pool, gi, k):
            u = KD * gi + k
            w = width(gi)
            pool.wait_ge(S["w_high"], u + 1)
            if k == 0 and gi >= 2:
                pool.wait_ge(S["proj"], NT * (gi - 1))
            nc.gpsimd.tensor_tensor(wl[gi % 2][:, k, 0:w], wraw[:, u % NRAW, 0:w],
                                    wh[gi % 2][:, k, 0:w].bitcast(F32), ALU.subtract).then_inc(S["w_low"], 1)

        @block.gpsimd
        def _(pool):
            for k in range(KD):
                split_unit_low(pool, 0, k)
            pool.wait_ge(S["small_in"], 48)
            for gi in range(NGR):
                for i in range(NT):
                    if gi + 1 < NGR and i < KD:
                        split_unit_low(pool, gi + 1, i)
                    for h0, hn, row, _ in kinds(gi):
                        n = rows_n(gi, i)
                        pool.wait_ge(S["normed"], NORM_AT[gi, i] + 1)
                        v = st[:, n % NST, HD * h0:HD * (h0 + hn)].rearrange("p (h d) -> p h d", h=hn)
                        nc.gpsimd.tensor_tensor(v, v, gains[:, row:row + 1, :].broadcast_to([P, hn, HD]),
                                                ALU.mult).then_inc(S["gained"], 1)
                if gi == 1:
                    for n, j in enumerate(SEL_TILES):
                        pool.wait_ge(S["added"], IH * (n + 1))
                        v = work[:, WORK_OFF[j] + P * j:WORK_OFF[j] + P * (j + 1)]
                        nc.gpsimd.affine_select(out=v, in_=v, compare_op=ALU.is_ge, fill=NEG, base=0,
                                                pattern=[[-1, P]], channel_multiplier=1).then_inc(S["masked"], 1)

        def take_turn(act, j):
            act.wait_ge(S["turned"], TURN_Q[j])
            if j - 2 in SEL_TILES:
                act.wait_ge(S["scored"], SELS.index((j - 2, IH - 1)) + 1)
            nc.scalar.activation(qt[:, j % 2, :], psx[:, :], ACT.Copy).then_inc(S["turn_taken"], 1)

        @block.scalar
        def _(act):
            def relu(s):
                j, h = SELS[s]
                w = P * (j + 1)
                act.wait_ge(S["scored"], s + 1)
                if s >= 2:
                    act.wait_ge(S["added"], s - 1)
                nc.scalar.activation(rl[:, s % 2, 0:w], pss[s % 2][:, 0:w], ACT.Relu).then_inc(S["relued"], 1)

            def root(gi, i):
                m = NORM_AT[gi, i]
                act.wait_ge(S["meaned"], sum(len(kinds(y[0])) for y in NORMED[:m + 1]))
                if m >= 2:
                    act.wait_ge(S["inverted"], m - 1)
                nh = sum(x[1] for x in kinds(gi))
                nc.scalar.activation(hr[:, m % 2, 0:nh], hm[:, m % 2, 0:nh], ACT.Sqrt).then_inc(S["rooted"], 1)

            pending = None
            for gi in range(NGR):
                for i in range(NT):
                    p = NT * gi + i
                    w = width(gi)
                    act.wait_ge(S["proj"], p + 1)
                    if gi == 0:
                        nc.scalar.activation(kk[:, i, 0:64], ps[p % 3][:, 0:64], ACT.Copy, scale=rstd[:, i:i + 1])
                        nc.scalar.activation(kk[:, i, 64:136], ps[p % 3][:, 0:72], ACT.Copy,
                                             scale=rstd[:, i:i + 1]).then_inc(S["kiwi_copied"], 1)
                    n = rows_n(gi, i)
                    if n >= NST:
                        before = n - NST
                        if GROUPS[before // NT][2]:
                            act.wait_ge(stored[n % NST], stored_total(before))
                        elif before - NT in TURN_ROWS:
                            act.wait_ge(S["turned"], TURN_ROWS[before - NT])
                        else:
                            act.wait_ge(S["copied"], before + 1)
                    c0 = KIWI if gi == 0 else 0
                    nc.scalar.activation(st[:, n % NST, 0:w - c0], ps[p % 3][:, c0:w], ACT.Copy,
                                         scale=rstd[:, i:i + 1]).then_inc(S["copied"], 1)
                    if gi == 1:
                        if i == 0:
                            for t, (x0, x1) in enumerate(KEY_TURNS):
                                act.wait_ge(S["turned"], t + 1)
                                nc.scalar.activation(kit[:, x0:x1], psx[:, 0:x1 - x0], ACT.Copy).then_inc(S["turn_taken"], 1)
                        if i == 1:
                            act.wait_ge(S["turned"], TURN_Q[0])
                            nc.scalar.activation(
                                qst[:, :, :].rearrange("d b (h t) -> d h b t", t=DT),
                                psx[0:HD, :].rearrange("d (h b t) -> d h b t", h=IH, t=DT), ACT.Copy).then_inc(S["turn_taken"], 1)
                        if i - 2 in TURN_Q and i >= 4:
                            take_turn(act, i - 2)
                        if i - 3 in TURN_Q and i >= 5:
                            for h in range(IH):
                                relu(SELS.index((i - 3, h)))
                    if kinds(gi):
                        m = NORM_AT[gi, i]
                        if m >= 2:
                            act.wait_ge(S["summed"], m - 1)
                        act.wait_ge(S["copied"], n + 1)
                        nh = sum(x[1] for x in kinds(gi))
                        nc.scalar.activation(sqr[:, m % 2, 0:HD * nh], st[:, n % NST, 0:HD * nh],
                                             ACT.Square).then_inc(S["squared"], 1)
                        if pending:
                            root(*pending)
                        pending = (gi, i)
                    elif pending:
                        root(*pending)
                        pending = None
                if gi == 1:
                    take_turn(act, 7)
                    for j in (6, 7):
                        for h in range(IH):
                            relu(SELS.index((j, h)))
                    for b in range(DB):
                        s = len(SELS) + b
                        act.wait_ge(S["scored"], s + 1)
                        if b < 2:
                            act.wait_ge(S["added"], s - 1)
                        else:
                            act.wait_ge(S["s_mixed"], b - 1)
                        nc.scalar.activation(rl[0:TS, s % 2, 0:SKEYS], pss[s % 2][0:TS, 0:SKEYS],
                                             ACT.Relu).then_inc(S["relued"], 1)
            if pending:
                root(*pending)

        @block.tensor
        def _(pe):
            def project(gi, i):
                p = NT * gi + i
                w, c = width(gi), tile_col(i)
                if i == 0:
                    pe.wait_ge(S["w_low"], KD * (gi + 1))
                if p >= 3:
                    pe.wait_ge(S["copied"], p - 2)
                passes = [(x, y, k) for k in range(KD) for x, y in ((xh, wh), (xh, wl), (xl, wh))]
                for n, (x, y, k) in enumerate(passes):
                    last = nc.tensor.matmul(ps[p % 3][:, 0:w], x[:, k, c:c + P], y[gi % 2][:, k, 0:w],
                                            start=(n == 0), stop=(n == len(passes) - 1))
                last.then_inc(S["proj"], 1)

            def turn_free(t):
                if t > 1:
                    pe.wait_ge(S["turn_taken"], t - 1)

            def turn_queries(j):
                pe.wait_ge(S["copied"], NT + (0 if j == 0 else j + 1) + 1)
                turn_free(TURN_Q[j])
                if j == 0:
                    for h in range(IH):
                        last = nc.tensor.transpose(psx[0:HD, TS * h:TS * h + TS], st[0:TS, NT % NST, HD * h:HD * h + HD],
                                                   ident[0:TS, 0:TS])
                else:
                    for q in range(4):
                        last = nc.tensor.transpose(psx[:, P * q:P * q + P], st[:, (NT + j + 1) % NST, P * q:P * q + P],
                                                   ident[:, :])
                last.then_inc(S["turned"], 1)

            def scores(j):
                pe.wait_ge(S["turn_taken"], TURN_Q[j])
                w = P * (j + 1)
                for h in range(IH):
                    s = SELS.index((j, h))
                    b = 64 * (h % 2)
                    if s >= 2:
                        pe.wait_ge(S["relued"], s - 1)
                    for x in range(0, w, 512):
                        y = min(512, w - x)
                        last = nc.tensor.matmul(pss[s % 2][:, x:x + y],
                                                qt[b:b + HD, j % 2, P * (h // 2):P * (h // 2) + P],
                                                kit[b:b + HD, TS + x:TS + x + y], start=True, stop=True)
                    last.then_inc(S["scored"], 1)

            for i in range(NT):
                project(0, i)
            project(1, 0)
            pe.wait_ge(S["kiwi_copied"], NT)
            for t, (x0, x1) in enumerate(KEY_TURNS):
                turn_free(t + 1)
                for i in range(NT):
                    if x0 <= tile_col(i) < x1:
                        r = tile_rows(i)
                        last = nc.tensor.transpose(psx[:, tile_col(i) - x0:tile_col(i) - x0 + r], kk[0:r, i, 0:P],
                                                   ident[0:r, 0:r])
                last.then_inc(S["turned"], 1)
            for i in range(1, NT):
                project(1, i)
                if i == 1:
                    turn_queries(0)
                if i - 2 in SEL_TILES:
                    turn_queries(i - 2)
                if i - 3 in SEL_TILES:
                    scores(i - 3)
            turn_queries(7)
            scores(6)
            scores(7)
            pe.wait_ge(S["keys_in"], 16 * DB * NPAGE)
            pe.wait_ge(S["wt_ready"], 1 + DB)

            def mix(b):
                s = len(SELS) + b
                pe.wait_ge(S["relued"], s + 1)
                nc.tensor.matmul(psx[0:TS, 0:SKEYS], wb[:, b, :], rl[0:TS, s % 2, 0:SKEYS],
                                 start=(b == 0), stop=(b == DB - 1)).then_inc(S["s_mixed"], 1)

            pe.wait_ge(S["turn_taken"], TURN_Q[7])
            for b in range(DB):
                s = len(SELS) + b
                pe.wait_ge(S["relued"], s - 1)
                for q in range(NPAGE):
                    nc.tensor.matmul(pss[s % 2][0:TS, PAGE * q:PAGE * (q + 1)], qst[:, b, :], kpt[:, NPAGE * b + q, :],
                                     start=True, stop=True)
                nc.tensor.matmul(pss[s % 2][0:TS, PAST:SKEYS], qst[:, b, :], kit[0:HD, DT * b:DT * (b + 1)],
                                 start=True, stop=True).then_inc(S["scored"], 1)
                if b:
                    mix(b - 1)
            mix(DB - 1)
            for gi in range(2, NGR):
                for i in range(NT):
                    project(gi, i)

        @block.vector
        def _(dve):
            tk = [0]

            def link(ins):
                tk[0] += 1
                ins.then_inc(S["topk"], 1)
                dve.wait_ge(S["topk"], tk[0])

            def split_high(gi, k):
                u = KD * gi + k
                w = width(gi)
                dve.wait_ge(w_in[u % NRAW], 16 * (u // NRAW + 1))
                if k == 0 and gi >= 2:
                    dve.wait_ge(S["proj"], NT * (gi - 1))
                nc.vector.tensor_copy(wh[gi % 2][:, k, 0:w], wraw[:, u % NRAW, 0:w]).then_inc(S["w_high"], 1)

            def add_scores(j):
                w = P * (j + 1)
                v = work[:, WORK_OFF[j]:WORK_OFF[j] + w]
                for h in range(IH):
                    s = SELS.index((j, h))
                    dve.wait_ge(S["relued"], s + 1)
                    if h == 0:
                        nc.vector.tensor_scalar(v, rl[:, s % 2, 0:w], wsc[:, j + 1, 0:1], None, ALU.mult).then_inc(S["added"], 1)
                    else:
                        dve.wait_ge(S["added"], s)
                        nc.vector.scalar_tensor_tensor(out=v, in0=rl[:, s % 2, 0:w], scalar=wsc[:, j + 1, h:h + 1], in1=v,
                                                       op0=ALU.mult, op1=ALU.add).then_inc(S["added"], 1)

            def norm_sum(gi, i):
                m = NORM_AT[gi, i]
                nh = sum(x[1] for x in kinds(gi))
                dve.wait_ge(S["squared"], m + 1)
                if m >= 2:
                    dve.wait_ge(S["rooted"], m - 1)
                nc.vector.reduce_sum(hs[:, m % 2, 0:nh], sqr[:, m % 2, 0:HD * nh].rearrange("p (h d) -> p h d", h=nh),
                                     AX_X).then_inc(S["summed"], 1)
                dve.wait_ge(S["summed"], m + 1)
                for h0, hn, _, query in kinds(gi):
                    f = 1.0 if query else 1.0 / HD
                    nc.vector.tensor_scalar(hm[:, m % 2, h0:h0 + hn], hs[:, m % 2, h0:h0 + hn], f, EPS * HD * f,
                                            ALU.mult, ALU.add).then_inc(S["meaned"], 1)

            def norm_apply(gi, i):
                m, n = NORM_AT[gi, i], rows_n(gi, i)
                nh = sum(x[1] for x in kinds(gi))
                dve.wait_ge(S["rooted"], m + 1)
                nc.vector.reciprocal(hi[:, m % 2, 0:nh], hr[:, m % 2, 0:nh]).then_inc(S["inverted"], 1)
                dve.wait_ge(S["inverted"], m + 1)
                v = st[:, n % NST, 0:HD * nh].rearrange("p (h d) -> p h d", h=nh)
                r = hi[:, m % 2, 0:nh].rearrange("p (h o) -> p h o", o=1).broadcast_to([P, nh, HD])
                nc.vector.tensor_tensor(v, v, r, ALU.mult).then_inc(S["normed"], 1)

            def topk_sample():
                for r in range(SR):
                    link(nc.vector.max(m8[0:TS, :], wks[:, 0:SKEYS]))
                    link(nc.vector.match_replace(wks[:, 0:SKEYS], m8[0:TS, :], wks[:, 0:SKEYS], SENT))
                if SREST:
                    link(nc.vector.max(m8[0:TS, :], wks[:, :]))
                    link(nc.vector.match_replace(wks[:, :], m8[0:TS, :], wks[:, :], SENT))
                link(nc.vector.tensor_scalar(wks[:, 0:SKEYS], wks[:, 0:SKEYS], SENT, NEG, ALU.not_equal, ALU.mult))

            for k in range(KD):
                split_high(0, k)
            for i in range(NT):
                if i < KD:
                    split_high(1, i)
                norm_sum(0, i)
                if i:
                    norm_apply(0, i - 1)
            norm_apply(0, NT - 1)
            nc.vector.memset(wb[:, :, :], 0.0).then_inc(S["zeroed"], 1)
            nc.vector.memset(wks[:, SKEYS:SKEYS + SPAD], HUGE).then_inc(S["zeroed"], 1)
            dve.wait_ge(S["kiwi_copied"], NT)
            nc.vector.tensor_scalar(wsc[:, :, :], kk[:, :, 128:136], IH ** -0.5, HD ** -0.5, ALU.mult, ALU.mult).then_inc(S["w_scaled"], 1)
            dve.wait_ge(S["wt_in"], 16 * IH)
            nc.vector.tensor_scalar(wts[:, :], wt[:, :], IH ** -0.5, HD ** -0.5, ALU.mult, ALU.mult).then_inc(S["wt_ready"], 1)
            dve.wait_ge(S["small_in"], 48)
            dve.wait_ge(S["wt_ready"], 1)
            dve.wait_ge(S["zeroed"], 2)
            for b in range(DB):
                nc.vector.tensor_scalar(wb[:, b, DT * b:DT * (b + 1)], same[:, :], wts[:, b:b + 1], None,
                                        ALU.mult).then_inc(S["wt_ready"], 1)
            dve.wait_ge(S["w_scaled"], 1)
            for k in range(KD):
                if k < 2:
                    split_high(2, k)
            for j in SEL_TILES:
                add_scores(j)
                if j < 7:
                    split_high(2, j)
            split_high(2, 7)
            dve.wait_ge(S["s_mixed"], DB)
            nc.vector.tensor_copy(wks[:, 0:SKEYS], psx[0:TS, 0:SKEYS]).then_inc(S["s_taken"], 1)
            dve.wait_ge(S["s_taken"], 1)
            nc.vector.tensor_tensor(wks[:, PAST:SKEYS], wks[:, PAST:SKEYS], late[:, :], ALU.add).then_inc(S["s_taken"], 1)
            dve.wait_ge(S["s_taken"], 2)
            topk_sample()
            steps = [(gi, i) for gi in range(2, NGR) for i in range(NT)]
            before, r0 = None, 0
            for n, (gi, i) in enumerate(steps):
                if gi + 1 < NGR and i < KD:
                    split_high(gi + 1, i)
                if kinds(gi):
                    norm_sum(gi, i)
                    if before:
                        norm_apply(*before)
                    before = (gi, i)
                elif before:
                    norm_apply(*before)
                    before = None
                r1 = ROUNDS_1 * (n + 1) // len(steps)
                for r in range(r0, r1):
                    if ROUNDS[r][1] == 0:
                        dve.wait_ge(S["masked"], SEL_TILES.index(ROUNDS[r][0]) + 1)
                    topk_round(nc, link, work, m8, r)
                r0 = r1


class SparseKeys:

    def __init__(self, nc, ctx):
        self.strip = ctx.enter_context(nc.sbuf_tensor("sa_bias_strip", [P, AH, SEQ], F32))
        self.kr = ctx.enter_context(nc.sbuf_tensor("sa_keys", [P, 8, P], F32))
        self.v = ctx.enter_context(nc.sbuf_tensor("sa_values", [P, 8, P], F32))
        self.all_in = ctx.enter_context(nc.semaphore("sa_all_in"))

    LOADS = 3

    def load(self, sp, proj, strips):
        rows = proj[TS:TS + SEQ, :].rearrange("(n p) c -> p n c", p=P)
        sp.dma_start(self.kr[:, :, :], rows[:, :, 512:640]).then_inc(self.all_in, 16)
        sp.dma_start(self.v[:, :, :], rows[:, :, 640:768]).then_inc(self.all_in, 16)
        sp.dma_start(self.strip[:, :, :], strips.rearrange("h p n -> p h n")).then_inc(self.all_in, 16)


def stage_sparse(nc, a, ident, work, proj, oa, keys, smp, table, smask, used):
    ITEMS = [(j, h) for j in range(SEQ // P) for h in range(AH)]
    NI = len(ITEMS)
    LAST_J = SEQ // P - 1
    with ExitStack() as ctx:
        def sb(name, shape, dt=F32):
            return ctx.enter_context(nc.sbuf_tensor("sa_" + name, shape, dt))

        def sem(name):
            return ctx.enter_context(nc.semaphore("sa_" + name))

        strip, kr, v = keys.strip, keys.kr, keys.v
        kt = sb("keys_t", [P, SEQ])
        q = sb("queries", [P, 2, 512])
        qt = sb("queries_t", [P, 2, 512])
        um = sb("bias_mask", [P, 2, SEQ])
        s = sb("scores", [P, 3, SEQ])
        pt = sb("probs_t", [P, 2, SEQ])
        mx = sb("row_max", [P, 4])
        nm = sb("neg_max", [P, 4])
        ls = sb("row_sum", [P, 2, AH])
        li = sb("inv_sum", [P, 2, AH])
        ob = sb("out_rows", [P, 2, 512])
        pss = [ctx.enter_context(nc.psum_tensor(f"sa_ps_s{i}", [P, SEQ], F32)) for i in range(2)]
        pst = [ctx.enter_context(nc.psum_tensor(f"sa_ps_t{i}", [P, 512], F32)) for i in range(2)]
        pso = ctx.enter_context(nc.psum_tensor("sa_ps_o", [P, 512], F32))
        psx = ctx.enter_context(nc.psum_tensor("sa_ps_x", [P, 512], F32))
        topk = sem("topk")
        m8 = sb("top8", [P, 8])
        q_in = [sem(f"q_in{i}") for i in range(2)]
        o_out = [sem(f"o_out{i}") for i in range(2)]
        (turned, turn_taken, scored, masked, maxed, negated, exped, probs_turned, probs_taken, pv_done, inverted,
         normed) = (sem(n) for n in ("turned", "turn_taken", "scored", "masked", "maxed", "negated", "exped",
                                     "probs_turned", "probs_taken", "pv_done", "inverted", "normed"))
        block = ctx.enter_context(nc.Block())

        def units(t):
            return sum(-(-(j + 1) // 4) for j, _ in ITEMS[:t])

        UNITS = [units(t) for t in range(NI + 1)]
        MASKED = [t for t in range(NI) if ITEMS[t][0] in SEL_TILES]

        @block.sync
        def _(sp):
            def load_q(j):
                if j >= 2:
                    sp.wait_ge(turned, 2 + j - 1)
                dst = q[:, j % 2, :].rearrange("p (r g d) -> p g r d", r=REP, g=AG)
                for g in range(AG):
                    sp.dma_start(dst[:, g], proj[TS + P * j:TS + P * (j + 1), 256 * g:256 * (g + 1)].rearrange(
                        "p (r d) -> p r d", r=REP)).then_inc(q_in[j % 2], 16)

            load_q(0)
            load_q(1)
            for j in range(SEQ // P):
                sp.wait_ge(normed, j + 1)
                sp.dma_start(oa[TS + P * j:TS + P * (j + 1), :], ob[:, j % 2, :]).then_inc(o_out[j % 2], 16)
                if j + 2 <= LAST_J:
                    load_q(j + 2)
                if j == 0:
                    smp.load(nc, sp, a, proj, table, smask)
                elif j <= 2:
                    smp.load_window(sp, a, 1, j - 1, smp.kb[j - 1], smp.vb[j - 1], smp.win_in[j - 1])
                elif j < LAST_J:
                    for n in range(4 * (j - 3), 4 * (j - 2)):
                        smp.load_page(sp, a, n)
            for i in range(2):
                sp.wait_ge(o_out[i], 16 * 4)
            smp.loaded(sp)

        @block.gpsimd
        def _(pool):
            nc.gpsimd.sem_clear(range(used[0], used[-1] + 1))
            for m, t in enumerate(MASKED):
                j, h = ITEMS[t]
                w = P * (j + 1)
                if m >= 2:
                    pool.wait_ge(maxed, MASKED[m - 2] + 1)
                if h == 0 and (j, TOPK // 8 - 1) in ROUNDS[ROUNDS_2:]:
                    pool.wait_ge(topk, sum(2 + (r == TOPK // 8 - 1) for x, r in ROUNDS[ROUNDS_2:] if x <= j))
                nc.gpsimd.tensor_tensor(um[:, m % 2, 0:w], strip[:, h, P * (7 - j):SEQ],
                                        work[:, WORK_OFF[j]:WORK_OFF[j] + w], ALU.add).then_inc(masked, 1)

        @block.scalar
        def _(act):
            def take_turn(n):
                act.wait_ge(turned, n + 1)
                if n < 2:
                    dst = kt[:, 512 * n:512 * (n + 1)]
                else:
                    j = n - 2
                    if j >= 2:
                        act.wait_ge(scored, AH * (j - 1))
                    dst = qt[:, j % 2, :]
                nc.scalar.activation(dst, psx[:, :], ACT.Copy).then_inc(turn_taken, 1)

            for n in range(3):
                take_turn(n)
            for t in range(NI + 1):
                if t < NI:
                    j, h = ITEMS[t]
                    w = P * (j + 1)
                    act.wait_ge(maxed, t + 1)
                    if t >= 4:
                        act.wait_ge(exped, t - 3)
                    nc.scalar.mul(nm[:, t % 4:t % 4 + 1], mx[:, t % 4:t % 4 + 1], -1.0).then_inc(negated, 1)
                    act.wait_ge(negated, t + 1)
                    if h == 0 and j >= 2:
                        act.wait_ge(inverted, j - 1)
                    nc.scalar.activation(s[:, t % 3, 0:w], s[:, t % 3, 0:w], ACT.Exp, bias=nm[:, t % 4:t % 4 + 1],
                                         accum_out=ls[:, j % 2, h:h + 1]).then_inc(exped, 1)
                if t >= 1:
                    j, h = ITEMS[t - 1]
                    if t - 1 >= 2:
                        act.wait_ge(pv_done, t - 2)
                    for u in range(UNITS[t - 1], UNITS[t]):
                        x = 512 * (u - UNITS[t - 1])
                        y = min(512, P * (j + 1) - x)
                        act.wait_ge(probs_turned, u + 1)
                        nc.scalar.activation(pt[:, (t - 1) % 2, x:x + y], pst[u % 2][:, 0:y], ACT.Copy).then_inc(probs_taken, 1)
                    if h == 5 and j < LAST_J:
                        take_turn(3 + j)

        @block.tensor
        def _(pe):
            def turn_keys(n):
                if n:
                    pe.wait_ge(turn_taken, n)
                for i in range(4):
                    last = nc.tensor.transpose(psx[:, P * i:P * (i + 1)], kr[:, 4 * n + i, :], ident[:, :])
                last.then_inc(turned, 1)

            def turn_queries(j):
                pe.wait_ge(q_in[j % 2], 32 * (j // 2 + 1))
                pe.wait_ge(turn_taken, 2 + j)
                for i in range(4):
                    last = nc.tensor.transpose(psx[:, P * i:P * (i + 1)], q[:, j % 2, P * i:P * (i + 1)], ident[:, :])
                last.then_inc(turned, 1)

            def scores(t):
                j, h = ITEMS[t]
                b, r, w = HD * (h // REP), h % REP, P * (j + 1)
                if h == 0:
                    pe.wait_ge(turn_taken, 3 + j)
                if t >= 2:
                    pe.wait_ge(maxed, t - 1)
                for x in range(0, w, 512):
                    y = min(512, w - x)
                    last = nc.tensor.matmul(pss[t % 2][:, x:x + y], qt[b:b + HD, j % 2, P * r:P * (r + 1)],
                                            kt[b:b + HD, x:x + y], start=True, stop=True)
                last.then_inc(scored, 1)

            def turn_probs(t):
                j, h = ITEMS[t]
                pe.wait_ge(exped, t + 1)
                for u in range(UNITS[t], UNITS[t + 1]):
                    if u >= 2:
                        pe.wait_ge(probs_taken, u - 1)
                    k0 = 4 * (u - UNITS[t])
                    for k in range(k0, min(k0 + 4, j + 1)):
                        last = nc.tensor.transpose(pst[u % 2][:, P * (k - k0):P * (k - k0 + 1)],
                                                   s[:, t % 3, P * k:P * (k + 1)], ident[:, :])
                    last.then_inc(probs_turned, 1)

            def outputs(t):
                j, h = ITEMS[t]
                pe.wait_ge(probs_taken, UNITS[t + 1])
                if h == 0 and j:
                    pe.wait_ge(normed, j)
                g = h // REP
                for k in range(j + 1):
                    last = nc.tensor.matmul(pso[:, HD * h:HD * (h + 1)], pt[:, t % 2, P * k:P * (k + 1)],
                                            v[:, k, HD * g:HD * (g + 1)], start=(k == 0), stop=(k == j))
                last.then_inc(pv_done, 1)

            turn_keys(0)
            turn_keys(1)
            turn_queries(0)
            for t in range(NI + 2):
                if t < NI:
                    scores(t)
                if 1 <= t <= NI:
                    turn_probs(t - 1)
                    if ITEMS[t - 1][1] == 5 and ITEMS[t - 1][0] < LAST_J:
                        turn_queries(ITEMS[t - 1][0] + 1)
                if t >= 2:
                    outputs(t - 2)

        @block.vector
        def _(dve):
            tk = [0]

            def link(ins):
                tk[0] += 1
                ins.then_inc(topk, 1)
                dve.wait_ge(topk, tk[0])

            r0, spread = ROUNDS_2, AH * LAST_J - 4
            for t in range(NI + 2):
                if t < NI:
                    j, h = ITEMS[t]
                    w = P * (j + 1)
                    dve.wait_ge(scored, t + 1)
                    if t in MASKED:
                        m = MASKED.index(t)
                        dve.wait_ge(masked, m + 1)
                        add = um[:, m % 2, 0:w]
                    else:
                        add = strip[:, h, P * (7 - j):SEQ]
                    if t >= 3:
                        dve.wait_ge(probs_turned, UNITS[t - 2])
                    if t >= 4:
                        dve.wait_ge(negated, t - 3)
                    nc.vector.tensor_tensor_reduce(out=s[:, t % 3, 0:w], in0=pss[t % 2][:, 0:w], in1=add, scale=1.0,
                                                   scalar=NEG, op0=ALU.add, op1=ALU.max,
                                                   accum_out=mx[:, t % 4:t % 4 + 1]).then_inc(maxed, 1)
                r1 = ROUNDS_2 + (len(ROUNDS) - ROUNDS_2) * min(t + 1, spread) // spread
                for n in range(r0, r1):
                    topk_round(nc, link, work, m8, n)
                r0 = r1
                if t >= 2 and ITEMS[t - 2][1] == AH - 1:
                    j = ITEMS[t - 2][0]
                    dve.wait_ge(pv_done, t - 1)
                    nc.vector.reciprocal(li[:, j % 2, :], ls[:, j % 2, :]).then_inc(inverted, 1)
                    dve.wait_ge(inverted, j + 1)
                    if j >= 2:
                        dve.wait_ge(o_out[j % 2], 16 * (j // 2))
                    nc.vector.tensor_tensor(
                        ob[:, j % 2, :].rearrange("p (h d) -> p h d", h=AH), pso[:, :].rearrange("p (h d) -> p h d", h=AH),
                        li[:, j % 2, :].rearrange("p (h o) -> p h o", o=1).broadcast_to([P, AH, HD]), ALU.mult
                    ).then_inc(normed, 1)


OBW = BW + 2 * BH


def stage_window(nc, a, ident, work, proj, wstrips, obp, keys, strips):
    JOBS = []
    for g in range(NG):
        d = DIL[g]
        n = SEQ // d
        if n >= P:
            JOBS += [(g, [(TS + c + d * P * i, P)], i > 0) for c in range(d) for i in range(n // P)]
        else:
            JOBS += [(g, [(TS + c + x, n) for x in range(P // n)], False) for c in range(0, d, P // n)]
    NJ = len(JOBS)
    with ExitStack() as ctx:
        def sb(name, shape, dt=F32):
            return ctx.enter_context(nc.sbuf_tensor("sw_" + name, shape, dt))

        def sem(name):
            return ctx.enter_context(nc.semaphore("sw_" + name))

        NR, AHEAD = 8, 6
        m8 = sb("top8", [P, 8])
        tb = [sb(f"bias{g}", [P, BH, 2 * P]) for g in range(NG)]
        rows = sb("rows", [P, NR, 3 * BW])
        qk = sb("turned", [P, 4, 512])
        s = sb("scores", [P, 3, BH * 2 * P])
        pt = sb("probs_t", [P, 2, SEQ])
        nm = sb("neg_max", [P, 2, BH])
        ob = sb("out_rows", [P, 4, OBW])
        pss = [ctx.enter_context(nc.psum_tensor(f"sw_ps_s{i}", [P, 1024], F32)) for i in range(2)]
        pst = [ctx.enter_context(nc.psum_tensor(f"sw_ps_t{i}", [P, 512], F32)) for i in range(2)]
        pso = ctx.enter_context(nc.psum_tensor("sw_ps_o", [P, 512], F32))
        psx = ctx.enter_context(nc.psum_tensor("sw_ps_x", [P, 512], F32))
        tb_in = sem("tb_in")
        rows_in = [sem(f"rows_in{i}") for i in range(NR)]
        o_out = [sem(f"o_out{i}") for i in range(4)]
        (topk, fenced, turned, turn_taken, scored, maxed, negated, exped, probs_turned, probs_taken, pv_done,
         copied) = (sem(n) for n in ("topk", "fenced", "turned", "turn_taken", "scored", "maxed", "negated", "exped",
                                     "probs_turned", "probs_taken", "pv_done", "copied"))
        block = ctx.enter_context(nc.Block())
        RUNS = [len(JOBS[t][1]) for t in range(NJ)]

        def slot_total(count, t, n):
            return 16 * sum(count[x] for x in range(t % n, t + 1, n))

        def blocks(t):
            return [(h, x) for h in range(BH) for x in ((0, P) if JOBS[t][2] else (P,))]

        def place(h):
            return 2 * P * (2 * (h % 2) + h // 2)

        UNITS = [0]
        for _t in range(NJ):
            UNITS.append(UNITS[-1] + len(blocks(_t)) // 4)

        def dram_rows(dram, row, n, g, c0, c1):
            return dram[row:row + DIL[g] * (n - 1) + 1:DIL[g], c0:c1]

        @block.sync
        def _(sp):
            def load(t):
                g, runs, _ = JOBS[t]
                if t >= NR:
                    sp.wait_ge(pv_done, t - NR + 2)
                at = 0
                for row, n in runs:
                    sp.dma_start(rows[at:at + n, t % NR, :],
                                 dram_rows(proj, row, n, g, 768 + 768 * g, 768 + 768 * (g + 1))).then_inc(rows_in[t % NR], 16)
                    at += n

            load(0)
            load(1)
            for g in range(NG):
                sp.dma_start(tb[g][:, :, :], wstrips[BH * g:BH * (g + 1)].rearrange("h p n -> p h n")).then_inc(tb_in, 16)
            for t in range(2, AHEAD):
                load(t)
            keys.load(sp, proj, strips)
            for t in range(NJ):
                if t + AHEAD < NJ:
                    load(t + AHEAD)
                sp.wait_ge(copied, t + 1)
                g, runs, _ = JOBS[t]
                at = 0
                for row, n in runs:
                    sp.dma_start(dram_rows(obp[g], row, n, g, 0, OBW), ob[at:at + n, t % 4, :]).then_inc(o_out[t % 4], 16)
                    at += n
            for t in range(NJ - 4, NJ):
                sp.wait_ge(o_out[t % 4], slot_total(RUNS, t, 4))
            sp.wait_ge(keys.all_in, 16 * keys.LOADS)

        @block.gpsimd
        def _(pool):
            n = SEQ // DIL[2]
            pool.wait_ge(tb_in, 16 * NG)
            nc.gpsimd.memset(tb[2][n:P, :, P:P + n], NEG).then_inc(fenced, 1)

        @block.scalar
        def _(act):
            for t in range(NJ + 2):
                if t < NJ:
                    act.wait_ge(turned, t + 1)
                    if t >= 4:
                        act.wait_ge(scored, t - 2)
                    nc.scalar.activation(qk[:, t % 4, :], psx[:, :], ACT.Copy).then_inc(turn_taken, 1)
                if 1 <= t <= NJ:
                    x = t - 1
                    c0 = 0 if JOBS[x][2] else P
                    act.wait_ge(maxed, BH * (x + 1))
                    if x >= 2:
                        act.wait_ge(exped, BH * (x - 1))
                    nc.scalar.mul(nm[:, x % 2, :], ob[:, x % 4, BW:BW + BH], -1.0).then_inc(negated, 1)
                    act.wait_ge(negated, x + 1)
                    for h in range(BH):
                        nc.scalar.activation(s[:, x % 3, place(h) + c0:place(h) + 2 * P], s[:, x % 3, place(h) + c0:place(h) + 2 * P], ACT.Exp, bias=nm[:, x % 2, h:h + 1],
                                             accum_out=ob[:, x % 4, BW + BH + h:BW + BH + h + 1]).then_inc(exped, 1)
                if t >= 2:
                    x = t - 2
                    if x >= 2:
                        act.wait_ge(pv_done, x - 1)
                    for u in range(UNITS[x], UNITS[x + 1]):
                        act.wait_ge(probs_turned, u + 1)
                        c = 512 * (u - UNITS[x])
                        nc.scalar.activation(pt[:, x % 2, c:c + 512], pst[u % 2][:, :], ACT.Copy).then_inc(probs_taken, 1)

        @block.tensor
        def _(pe):
            def turn_rows(t):
                pe.wait_ge(rows_in[t % NR], slot_total(RUNS, t, NR))
                if t:
                    pe.wait_ge(turn_taken, t)
                for i in range(4):
                    last = nc.tensor.transpose(psx[:, P * i:P * (i + 1)], rows[:, t % NR, P * i:P * (i + 1)], ident[:, :])
                last.then_inc(turned, 1)

            def scores(t):
                pe.wait_ge(turn_taken, t + 1)
                if t >= 2:
                    pe.wait_ge(maxed, BH * (t - 1))
                for h in range(BH):
                    pair, b = h // 2, HD * (h % 2)
                    for back in ((1, 0) if JOBS[t][2] else (0,)):
                        x = place(h) + P * (1 - back)
                        last = nc.tensor.matmul(pss[t % 2][:, x:x + P], qk[b:b + HD, t % 4, P * pair:P * (pair + 1)],
                                                qk[b:b + HD, (t - back) % 4, P * (2 + pair):P * (3 + pair)],
                                                start=True, stop=True)
                last.then_inc(scored, 1)

            def turn_probs(t):
                pe.wait_ge(exped, BH * (t + 1))
                todo = blocks(t)
                for u in range(UNITS[t], UNITS[t + 1]):
                    if u >= 2:
                        pe.wait_ge(probs_taken, u - 1)
                    for i in range(4):
                        h, x = todo[4 * (u - UNITS[t]) + i]
                        last = nc.tensor.transpose(pst[u % 2][:, P * i:P * (i + 1)],
                                                   s[:, t % 3, place(h) + x:place(h) + x + P], ident[:, :])
                    last.then_inc(probs_turned, 1)

            def outputs(t):
                pe.wait_ge(probs_taken, UNITS[t + 1])
                if t:
                    pe.wait_ge(copied, t)
                per = len(blocks(t)) // BH
                for i, (h, x) in enumerate(blocks(t)):
                    back = 1 if x == 0 else 0
                    last = nc.tensor.matmul(pso[:, HD * h:HD * (h + 1)], pt[:, t % 2, P * i:P * (i + 1)],
                                            rows[:, (t - back) % NR, 2 * BW + HD * h:2 * BW + HD * (h + 1)],
                                            start=(i % per == 0), stop=(i % per == per - 1))
                last.then_inc(pv_done, 1)

            for t in range(NJ + 3):
                if t < NJ:
                    turn_rows(t)
                if 1 <= t <= NJ:
                    scores(t - 1)
                if 2 <= t <= NJ + 1:
                    turn_probs(t - 2)
                if t >= 3:
                    outputs(t - 3)

        @block.vector
        def _(dve):
            tk = [0]

            def link(ins):
                tk[0] += 1
                ins.then_inc(topk, 1)
                dve.wait_ge(topk, tk[0])

            r0 = ROUNDS_1
            dve.wait_ge(tb_in, 16 * NG)
            for t in range(NJ + 2):
                if t < NJ:
                    g, _, prev = JOBS[t]
                    if g == 2:
                        dve.wait_ge(fenced, 1)
                    c0 = 0 if prev else P
                    dve.wait_ge(scored, t + 1)
                    if t >= 3:
                        dve.wait_ge(probs_turned, UNITS[t - 2])
                    if t >= 4:
                        dve.wait_ge(o_out[t % 4], slot_total(RUNS, t - 4, 4))
                    for h in range(BH):
                        x, y = place(h) + c0, place(h) + 2 * P
                        nc.vector.tensor_tensor_reduce(out=s[:, t % 3, x:y],
                                                       in0=pss[t % 2][:, x:y], in1=tb[g][:, h, c0:2 * P],
                                                       scale=1.0, scalar=NEG, op0=ALU.add, op1=ALU.max,
                                                       accum_out=ob[:, t % 4, BW + h:BW + h + 1]).then_inc(maxed, 1)
                if t >= 2:
                    x = t - 2
                    dve.wait_ge(pv_done, x + 1)
                    nc.vector.tensor_copy(ob[:, x % 4, 0:BW], pso[:, 0:BW]).then_inc(copied, 1)
                r1 = ROUNDS_1 + (ROUNDS_2 - ROUNDS_1) * (t + 1) // (NJ + 2)
                for r in range(r0, r1):
                    topk_round(nc, link, work, m8, r)
                r0 = r1


class OwnRows:

    def __init__(self, nc, ctx, oas, obs):
        self.nc, self.oas, self.obs = nc, oas, obs
        self.a = ctx.enter_context(nc.sbuf_tensor("own_a", [P, 512], F32))
        self.b = ctx.enter_context(nc.sbuf_tensor("own_b", [P, NG, OBW], F32))
        self.all_in = ctx.enter_context(nc.semaphore("own_in"))

    LOADS = AH + NG * BH * 3

    def load_a(self, sp):
        for g in range(AG):
            for r in range(REP):
                src = bass.AP(tensor=self.oas.tensor, offset=(32 * g + DT * r) * P + HD * g, ap=[[64 * P, DB], [P, DT], [1, HD]])
                c = HD * (REP * g + r)
                sp.dma_start(self.a[0:TS, c:c + HD], src).then_inc(self.all_in, 16)

    def load_b(self, sp, g, part=None):
        base = g * (DB // 4) * P * OBW
        parts = [(h, c, w, off) for h in range(BH) for c, w, off in ((HD * h, HD, HD * h), (BW + h, 1, BW), (BW + BH + h, 1, BW + 1))]
        for x, (h, c, w, off) in enumerate(parts):
            if part is None or x % 3 == part:
                src = bass.AP(tensor=self.obs.tensor, offset=base + h * DT * OBW + off, ap=[[32 * OBW, DB], [OBW, DT], [1, w]])
                with self.nc.allow_non_contiguous_dma(reason="some of 64 words"):
                    sp.dma_start(self.b[0:TS, g, c:c + w], src).then_inc(self.all_in, 16)


class Samples:

    def __init__(self, nc, ctx):
        def sb(name, shape, dt=F32):
            return ctx.enter_context(nc.sbuf_tensor("ss_" + name, shape, dt))

        self.srow = sb("rows", [TS, PROJ_W])
        self.kpa = sb("page_keys", [P, DB * NPAGE, PAGE])
        self.vpa = sb("page_values", [P, DB * NPAGE, P])
        self.vna = sb("new_values_a", [DT, DB, P])
        self.smr = sb("masks", [P, DB // 2, SKEYS])
        self.ua = sb("bias_a", [P, SKEYS])
        self.ub = [sb(f"bias_b{g}", [P, WL[g] + DT]) for g in range(NG)]
        self.pages = sb("pages", [1, DB * NPAGE], I32)
        self.kb = [sb(f"window_keys{i}", [P, 4, 2 * WL[1]]) for i in range(2)]
        self.vb = [sb(f"window_values{i}", [P, 4, WL[1] // P, BW]) for i in range(2)]
        self.win_in = [ctx.enter_context(nc.semaphore(f"ss_win_in{i}")) for i in range(2)]
        self.pages_in, self.rows_in, self.kv_in, self.new_in, self.bias_in = (
            ctx.enter_context(nc.semaphore("ss_" + n)) for n in ("pages_in", "rows_in", "kv_in", "new_in", "bias_in"))

    N_ROWS, N_KV, N_NEW, N_BIAS = 1 + AG, 2 * DB * NPAGE, 1, 2 + DB + 4 * NG

    def load(self, nc, sp, a, proj, table, smask):
        sp.dma_start(self.pages[:, :], a["page_table"]).then_inc(self.pages_in, 16)
        qv = self.srow[:, 0:512].rearrange("p (r g d) -> p g r d", r=REP, g=AG)
        for g in range(AG):
            sp.dma_start(qv[:, g], proj[0:TS, 256 * g:256 * (g + 1)].rearrange("p (r d) -> p r d", r=REP)
                         ).then_inc(self.rows_in, 16)
        sp.dma_start(self.srow[:, 512:PROJ_W], proj[0:TS, 512:PROJ_W]).then_inc(self.rows_in, 16)
        for b in range(2):
            src = bass.AP(tensor=table.tensor, offset=SEQ - PAST - 1, ap=[[NTAB, AH], [-1, DT], [1, SKEYS]])
            sp.dma_start(self.ua[64 * b:64 * (b + 1), :], src).then_inc(self.bias_in, 16)
            for i in range(DB // 2):
                src = bass.AP(tensor=smask.tensor, offset=DT * (2 * i + b) * SKEYS, ap=[[0, AH], [SKEYS, DT], [1, SKEYS]])
                sp.dma_start(self.smr[64 * b:64 * (b + 1), i, :], src).then_inc(self.bias_in, 16)
        for g in range(NG):
            for b in range(4):
                src = bass.AP(tensor=table.tensor, offset=(AH + BH * g) * NTAB + TAB_OFF_S[g] + DT - 1,
                              ap=[[NTAB, BH], [-1, DT], [1, WL[g] + DT]])
                sp.dma_start(self.ub[g][32 * b:32 * (b + 1), :], src).then_inc(self.bias_in, 16)
        new = proj[0:TS, :].rearrange("(b t) c -> t b c", t=DT)
        sp.dma_start(self.vna[:, :, :], new[:, :, 640:768]).then_inc(self.new_in, 16)
        sp.wait_ge(self.pages_in, 16)

    @staticmethod
    def load_window(sp, a, g, i, kb, vb, win_in):
        sp.dma_start(kb[:, :, :], a[f"win_keys_t{g}"][4 * i:4 * (i + 1)].rearrange("b d k -> d b k")).then_inc(win_in, 16)
        for b in range(4):
            sp.dma_start(vb[:, b, :, :], a[f"win_cache{g}"][4 * i + b, :, BW:2 * BW].rearrange("(n p) c -> p n c", p=P)).then_inc(win_in, 16)

    def load_page(self, sp, a, n):
        page = sp.value_load(self.pages[0:1, n:n + 1], min_val=0, max_val=a["kv_keys_t"].shape[0] - 1)
        sp.dma_start(self.kpa[:, n, :], a["kv_keys_t"][bass.ds(page, 1), :, :].rearrange("o d n -> d (o n)")).then_inc(self.kv_in, 16)
        sp.dma_start(self.vpa[:, n, :], a["kv_values"][bass.ds(page, 1), :, :].rearrange("o n d -> n (o d)")).then_inc(self.kv_in, 16)

    def loaded(self, sp):
        for x, n in ((self.rows_in, self.N_ROWS), (self.kv_in, self.N_KV), (self.new_in, self.N_NEW), (self.bias_in, self.N_BIAS)):
            sp.wait_ge(x, 16 * n)
        for i in range(2):
            sp.wait_ge(self.win_in[i], 16 * 5)


def stage_sample(nc, a, ident, smp, proj, oas, obs, own):
    ITEMS = [("a", 0, i) for i in range(DB // 2)] + [("b", g, i) for g in (1, 0, 2) for i in range(DB // 4)]
    NI = len(ITEMS)
    NA = DB // 2
    with ExitStack() as ctx:
        def sb(name, shape, dt=F32):
            return ctx.enter_context(nc.sbuf_tensor("ss_" + name, shape, dt))

        def sem(name):
            return ctx.enter_context(nc.semaphore("ss_" + name))

        MAXW = max(WL)
        rest = ITEMS[NA + 2:]
        kb = smp.kb + [sb(f"keys{g}_{i}", [P, 4, 2 * WL[g]]) for _, g, i in rest]
        vb = smp.vb + [sb(f"values{g}_{i}", [P, 4, WL[g] // P, BW]) for _, g, i in rest]
        uma = sb("bias_mask_a", [P, NA, SKEYS])
        srow, kpa, vpa, vna, smr, ua, ub = smp.srow, smp.kpa, smp.vpa, smp.vna, smp.smr, smp.ua, smp.ub
        vnb = sb("new_values_b", [DT, NG, DB, BW])
        new_in = sem("new_b_in")
        qba = sb("queries_a", [P, DB, HD])
        kna = sb("new_keys_a", [P, TS])
        qbb = sb("queries_b", [P, NG, 2, DB, 32])
        knb = sb("new_keys_b", [P, NG, 2, TS])
        s = sb("scores", [P, 3, MAXW + DT])
        pt = sb("probs_t", [P, 2, 3 * P])
        nm = sb("neg_max", [P, 4])
        st = sb("stats", [P, 4, 2])
        ob = sb("out_rows", [P, 3, OBW])
        pss = [ctx.enter_context(nc.psum_tensor(f"ss_ps_s{i}", [P, 512], F32)) for i in range(2)]
        pst = [ctx.enter_context(nc.psum_tensor(f"ss_ps_t{i}", [P, 512], F32)) for i in range(2)]
        pso = [ctx.enter_context(nc.psum_tensor(f"ss_ps_o{i}", [P, 512], F32)) for i in range(2)]
        psx = [ctx.enter_context(nc.psum_tensor(f"ss_ps_x{i}", [P, 512], F32)) for i in range(2)]
        win_in = smp.win_in + [sem(f"win_in{i}") for i in range(2, NI - NA)]
        o_out = [sem(f"o_out{i}") for i in range(3)]
        (zeroed, turned, turn_taken, masked, scored, maxed, negated, exped, probs_turned, probs_taken, pv_done,
         inverted, copied) = (sem(n) for n in ("zeroed", "turned", "turn_taken", "masked", "scored", "maxed", "negated",
                                               "exped", "probs_turned", "probs_taken", "pv_done", "inverted", "copied"))
        block = ctx.enter_context(nc.Block())

        def keys(t):
            kind, g, _ = ITEMS[t]
            return PAST if kind == "a" else WL[g]

        @block.sync
        def _(sp):
            new = proj[0:TS, :].rearrange("(b t) c -> t b c", t=DT)
            for g in range(NG):
                sp.dma_start(vnb[:, g, :, :], new[:, :, 768 * (g + 1) + 2 * BW:768 * (g + 1) + 3 * BW]).then_inc(new_in, 16)
            for x, (_, g, i) in enumerate(rest):
                smp.load_window(sp, a, g, i, kb[x + 2], vb[x + 2], win_in[x + 2])
            for t in range(NI):
                kind, g, i = ITEMS[t]
                sp.wait_ge(copied, t + 1)
                if kind == "a":
                    sp.dma_start(oas[i], ob[:, t % 3, 0:P]).then_inc(o_out[t % 3], 16)
                else:
                    sp.dma_start(obs[g][i][:, 0:BW + 2], ob[:, t % 3, 0:BW + 2]).then_inc(o_out[t % 3], 16)
                if t == NA + 1:
                    for x in range(3):
                        sp.wait_ge(o_out[x], 16 * len([y for y in range(t) if y % 3 == x]))
                    own.load_a(sp)
            own.load_b(sp, ITEMS[NA][1])
            for x in range(3):
                sp.wait_ge(o_out[x], 16 * len([t for t in range(NI) if t % 3 == x]))

        @block.gpsimd
        def _(pool):
            nc.gpsimd.memset(qba[:, :, :], 0.0).then_inc(zeroed, 1)
            nc.gpsimd.memset(qbb[:, :, :, :, :], 0.0).then_inc(zeroed, 1)
            for i in range(NA):
                nc.gpsimd.tensor_tensor(uma[:, i, :], ua[:, :], smr[:, i, :], ALU.add).then_inc(masked, 1)

        @block.scalar
        def _(act):
            act.wait_ge(zeroed, 2)
            for n in range(2 + NG):
                act.wait_ge(turned, n + 1)
                x = psx[n % 2]
                if n == 0:
                    for g in range(AG):
                        last = nc.scalar.activation(
                            qba[HD * g:HD * (g + 1), :, 32 * g:32 * (g + 1)].rearrange("p b (r t) -> p r b t", t=DT),
                            x[HD * g:HD * (g + 1), 0:256].rearrange("p (r b t) -> p r b t", r=REP, t=DT), ACT.Copy)
                elif n == 1:
                    last = nc.scalar.activation(kna[:, :], x[:, 0:TS], ACT.Copy)
                else:
                    g = n - 2
                    for pair in range(2):
                        for hh in range(2):
                            h = 2 * pair + hh
                            nc.scalar.activation(qbb[HD * hh:HD * (hh + 1), g, pair, :, DT * h:DT * (h + 1)],
                                                 x[HD * hh:HD * (hh + 1), TS * pair:TS * (pair + 1)].rearrange(
                                                     "p (b t) -> p b t", t=DT), ACT.Copy)
                    last = nc.scalar.activation(knb[:, g, :, :], x[:, 2 * TS:4 * TS].rearrange("p (a t) -> p a t", a=2), ACT.Copy)
                last.then_inc(turn_taken, 1)
            for t in range(NI + 1):
                if t < NI:
                    w = keys(t) + DT
                    act.wait_ge(maxed, t + 1)
                    if t >= 4:
                        act.wait_ge(exped, t - 3)
                    nc.scalar.mul(nm[:, t % 4:t % 4 + 1], st[:, t % 4, 0:1], -1.0).then_inc(negated, 1)
                    act.wait_ge(negated, t + 1)
                    if t >= 4:
                        act.wait_ge(copied, t - 3)
                    nc.scalar.activation(s[:, t % 3, 0:w], s[:, t % 3, 0:w], ACT.Exp, bias=nm[:, t % 4:t % 4 + 1],
                                         accum_out=st[:, t % 4, 1:2]).then_inc(exped, 1)
                if t >= 1:
                    x = t - 1
                    w = keys(x)
                    act.wait_ge(probs_turned, x + 1)
                    if x >= 2:
                        act.wait_ge(pv_done, x - 1)
                    nc.scalar.activation(pt[:, x % 2, 0:w], pst[x % 2][:, 0:w], ACT.Copy)
                    nc.scalar.activation(pt[0:DT, x % 2, w:w + P], pst[x % 2][0:DT, w:w + P], ACT.Copy).then_inc(probs_taken, 1)

        @block.tensor
        def _(pe):
            def turn(n, parts):
                if n >= 2:
                    pe.wait_ge(turn_taken, n - 1)
                for i, c in enumerate(parts):
                    last = nc.tensor.transpose(psx[n % 2][:, TS * i:TS * (i + 1)], srow[:, c:c + P], ident[0:TS, 0:TS])
                last.then_inc(turned, 1)

            turn(0, [P * r for r in range(REP)])
            turn(1, [512])
            for g in range(NG):
                turn(2 + g, [768 * (g + 1) + P * i for i in range(4)])
            pe.wait_ge(turn_taken, 2 + NG)

            def scores(t):
                kind, g, i = ITEMS[t]
                w = keys(t)
                if t >= 2:
                    pe.wait_ge(maxed, t - 1)
                z = pss[t % 2]
                if kind == "a":
                    for bb in range(2):
                        b = 2 * i + bb
                        o = z[64 * bb:64 * (bb + 1), :]
                        for n in range(NPAGE):
                            nc.tensor.matmul(o[:, PAGE * n:PAGE * (n + 1)], qba[:, b, :], kpa[:, NPAGE * b + n, :], start=True, stop=True)
                        last = nc.tensor.matmul(o[:, w:w + DT], qba[:, b, :], kna[:, DT * b:DT * (b + 1)], start=True, stop=True)
                else:
                    x = t - NA
                    pe.wait_ge(win_in[x], 16 * 5)
                    for bb in range(4):
                        b = 4 * i + bb
                        o = z[32 * bb:32 * (bb + 1), :]
                        for pair in range(2):
                            nc.tensor.matmul(o[:, 0:w], qbb[:, g, pair, b, :], kb[x][:, bb, w * pair:w * (pair + 1)],
                                             start=(pair == 0), stop=(pair == 1), tile_position=(0, 32 * bb))
                        for pair in range(2):
                            last = nc.tensor.matmul(o[:, w:w + DT], qbb[:, g, pair, b, :], knb[:, g, pair, DT * b:DT * (b + 1)],
                                                    start=(pair == 0), stop=(pair == 1), tile_position=(0, 32 * bb))
                last.then_inc(scored, 1)

            def turn_probs(t):
                w = keys(t)
                pe.wait_ge(exped, t + 1)
                if t >= 2:
                    pe.wait_ge(probs_taken, t - 1)
                for n in range(w // P):
                    nc.tensor.transpose(pst[t % 2][:, P * n:P * (n + 1)], s[:, t % 3, P * n:P * (n + 1)], ident[:, :])
                nc.tensor.transpose(pst[t % 2][0:DT, w:w + P], s[:, t % 3, w:w + DT], ident[:, :]).then_inc(probs_turned, 1)

            def outputs(t):
                kind, g, i = ITEMS[t]
                w = keys(t)
                pe.wait_ge(probs_taken, t + 1)
                if t >= 2:
                    pe.wait_ge(copied, t - 1)
                if t == NA:
                    pe.wait_ge(new_in, 16 * NG)
                m, nb, ow = (64, 2, P) if kind == "a" else (32, 4, BW)
                for bb in range(nb):
                    b = nb * i + bb
                    o = pso[t % 2][m * bb:m * (bb + 1), 0:ow]
                    for n in range(w // P):
                        val = vpa[:, NPAGE * b + n, :] if kind == "a" else \
                            vb[t - NA][:, bb, n, :]
                        nc.tensor.matmul(o, pt[:, t % 2, P * n + m * bb:P * n + m * (bb + 1)], val, start=(n == 0), stop=False,
                                         tile_position=(0, m * bb))
                    val = vna[:, b, :] if kind == "a" else vnb[:, g, b, :]
                    last = nc.tensor.matmul(o, pt[0:DT, t % 2, w + m * bb:w + m * (bb + 1)], val, start=False, stop=True,
                                            tile_position=(0, m * bb))
                last.then_inc(pv_done, 1)

            for t in range(NI + 2):
                if t < NI:
                    scores(t)
                if 1 <= t <= NI:
                    turn_probs(t - 1)
                if t >= 2:
                    outputs(t - 2)

        @block.vector
        def _(dve):
            for t in range(NI + 2):
                if t < NI:
                    kind, g, i = ITEMS[t]
                    w = keys(t) + DT
                    dve.wait_ge(scored, t + 1)
                    if kind == "a":
                        dve.wait_ge(masked, i + 1)
                    if t >= 3:
                        dve.wait_ge(probs_turned, t - 2)
                    if t >= 4:
                        dve.wait_ge(negated, t - 3)
                        dve.wait_ge(copied, t - 3)
                    nc.vector.tensor_tensor_reduce(out=s[:, t % 3, 0:w], in0=pss[t % 2][:, 0:w],
                                                   in1=uma[:, i, :] if kind == "a" else ub[g][:, :], scale=1.0, scalar=NEG,
                                                   op0=ALU.add, op1=ALU.max, accum_out=st[:, t % 4, 0:1]).then_inc(maxed, 1)
                if t >= 2:
                    x = t - 2
                    dve.wait_ge(pv_done, x + 1)
                    if x >= 3:
                        dve.wait_ge(o_out[x % 3], 16 * (x // 3))
                    if ITEMS[x][0] == "a":
                        nc.vector.reciprocal(ob[:, x % 3, P:P + 1], st[:, x % 4, 1:2]).then_inc(inverted, 1)
                        dve.wait_ge(inverted, x + 1)
                        nc.vector.tensor_scalar(ob[:, x % 3, 0:P], pso[x % 2][:, 0:P], ob[:, x % 3, P:P + 1], None,
                                                ALU.mult).then_inc(copied, 1)
                    else:
                        nc.vector.tensor_copy(ob[:, x % 3, BW:BW + 2], st[:, x % 4, :])
                        nc.vector.tensor_copy(ob[:, x % 3, 0:BW], pso[x % 2][:, 0:BW]).then_inc(copied, 1)


def stage_merge(nc, a, d, ident, oa, obp, own, oth, otl):
    with ExitStack() as ctx:
        def sb(name, shape, dt=F32):
            return ctx.enter_context(nc.sbuf_tensor("sm_" + name, shape, dt))

        def sem(name):
            return ctx.enter_context(nc.semaphore("sm_" + name))

        ra = d.ssum[:, :, :].rearrange("p c n -> p (c n)")[:, 0:2 * 512].rearrange("p (s n) -> p s n", s=2)
        rb = sb("rows_b", [P, 2, NG, OBW])
        mm = sb("top", [P, 2, BH])
        df = sb("below", [P, 2, NG, BH])
        ww = sb("weights", [P, 2, NG, BH])
        lw = sb("weighted_sums", [P, 2, NG, BH])
        ll = sb("total", [P, 2, BH])
        wn = sb("shares", [P, 2, NG, BH])
        tt = sb("shared", [P, 2, NG, BW])
        om = sb("merged", [P, 2, BW])
        ps = [ctx.enter_context(nc.psum_tensor(f"sm_ps{i}", [P, 1024], F32)) for i in range(4)]
        rows_in = [sem(f"rows_in{i}") for i in range(2)]
        (step, below, weighed, shared, half, merged, turned, high, low, cleared) = (sem(n) for n in (
            "step", "below", "weighed", "shared", "half", "merged", "turned", "high", "low", "cleared"))
        block = ctx.enter_context(nc.Block())
        def rows_a(n):
            return own.a[:, :] if n == NT - 1 else ra[:, n % 2, :]

        def rows_b(n):
            return own.b[:, :, :] if n == NT - 1 else rb[:, n % 2, :, :]

        def wait_rows(eng, n):
            if n == NT - 1:
                eng.wait_ge(own.all_in, 16 * own.LOADS)
            else:
                eng.wait_ge(rows_in[n % 2], 16 * 2 * (n // 2 + 1))


        @block.sync
        def _(sp):
            for n in range(NT - 1):
                if n >= 2:
                    sp.wait_ge(turned, n - 1)
                x = rows_in[n % 2]
                c = tile_col(n + 1)
                sp.dma_start(ra[:, n % 2, :], oa[c:c + P, :]).then_inc(x, 16)
                sp.dma_start(rb[:, n % 2, :, :], obp[:, c:c + P, :].rearrange("g p n -> p g n")).then_inc(x, 16)
                if 1 <= n <= 6:
                    own.load_b(sp, 0 if n < 4 else NG - 1, (n - 1) % 3)
            d.load_first(sp)

        def order():
            for n in range(NT):
                i = n + 1 if n < NT - 1 else 0
                yield n, i, tile_rows(i), tile_col(i)

        def put_high(act, n):
            i = n + 1 if n < NT - 1 else 0
            r, c = tile_rows(i), tile_col(i)
            act.wait_ge(turned, n + 1)
            nc.scalar.activation(oth[:, :, c:c + r], ps[n % 4][:, 0:6 * P].rearrange("p (k t) -> p k t", k=6)[:, :, 0:r],
                                 ACT.Copy).then_inc(high, 1)

        def put_low(dve, n):
            i = n + 1 if n < NT - 1 else 0
            r, c = tile_rows(i), tile_col(i)
            dve.wait_ge(high, n + 1)
            nc.vector.tensor_tensor(otl[:, :, c:c + r], ps[n % 4][:, 0:6 * P].rearrange("p (k t) -> p k t", k=6)[:, :, 0:r],
                                    oth[:, :, c:c + r].bitcast(F32), ALU.subtract).then_inc(low, 1)


        @block.gpsimd
        def _(pool):
            for n, i, r, c in order():
                y = n % 2
                pool.wait_ge(shared, n + 1)
                if n >= 2:
                    pool.wait_ge(turned, n - 1)
                nc.gpsimd.tensor_tensor(om[0:r, y, :], tt[0:r, y, 0, :], tt[0:r, y, 1, :], ALU.add).then_inc(half, 1)
                pool.wait_ge(half, n + 1)
                nc.gpsimd.tensor_tensor(om[0:r, y, :], om[0:r, y, :], tt[0:r, y, 2, :], ALU.add).then_inc(merged, 1)

        @block.scalar
        def _(act):
            for n, i, r, c in order():
                act.wait_ge(below, n + 1)
                if n >= 2:
                    act.wait_ge(merged, n - 1)
                nc.scalar.activation(ww[0:r, n % 2, :, :], df[0:r, n % 2, :, :], ACT.Exp).then_inc(weighed, 1)
                if n >= 2:
                    put_high(act, n - 2)
            put_high(act, NT - 2)
            put_high(act, NT - 1)

        @block.tensor
        def _(pe):
            for n, i, r, c in order():
                wait_rows(pe, n)
                pe.wait_ge(merged, n + 1)
                if n >= 4:
                    pe.wait_ge(low, n - 3)
                for k in range(6):
                    src = rows_a(n)[0:r, P * k:P * (k + 1)] if k < 4 else om[0:r, n % 2, P * (k - 4):P * (k - 3)]
                    last = nc.tensor.transpose(ps[n % 4][:, P * k:P * k + r], src, ident[0:r, 0:r])
                last.then_inc(turned, 1)

        @block.vector
        def _(dve):
            nc.vector.memset(otl[:, :, TS + SEQ:TOK].bitcast(F32), 0.0).then_inc(cleared, 1)
            nc.vector.memset(oth[:, :, TS + SEQ:TOK].bitcast(F32), 0.0).then_inc(cleared, 1)
            count = [0]

            def link(ins):
                count[0] += 1
                ins.then_inc(step, 1)
                dve.wait_ge(step, count[0])

            for n, i, r, c in order():
                wait_rows(dve, n)
                y = n % 2

                def m(g):
                    return rows_b(n)[0:r, g, BW:BW + BH]

                link(nc.vector.tensor_tensor(mm[0:r, y, :], m(0), m(1), ALU.max))
                link(nc.vector.tensor_tensor(mm[0:r, y, :], mm[0:r, y, :], m(2), ALU.max))
                top = mm[0:r, y:y + 1, :].broadcast_to([r, NG, BH])
                nc.vector.tensor_tensor(df[0:r, y, :, :], rows_b(n)[0:r, :, BW:BW + BH], top, ALU.subtract).then_inc(below, 1)
                dve.wait_ge(weighed, n + 1)
                link(nc.vector.tensor_tensor(lw[0:r, y, :, :], ww[0:r, y, :, :], rows_b(n)[0:r, :, BW + BH:OBW], ALU.mult))
                link(nc.vector.tensor_tensor(ll[0:r, y, :], lw[0:r, y, 0, :], lw[0:r, y, 1, :], ALU.add))
                link(nc.vector.tensor_tensor(ll[0:r, y, :], ll[0:r, y, :], lw[0:r, y, 2, :], ALU.add))
                link(nc.vector.reciprocal(ll[0:r, y, :], ll[0:r, y, :]))
                tot = ll[0:r, y:y + 1, :].broadcast_to([r, NG, BH])
                link(nc.vector.tensor_tensor(wn[0:r, y, :, :], ww[0:r, y, :, :], tot, ALU.mult))
                if n >= 2:
                    dve.wait_ge(merged, n - 1)
                for g in range(NG):
                    share = wn[0:r, y, g, :].rearrange("p (h o) -> p h o", o=1).broadcast_to([r, BH, HD])
                    last = nc.vector.tensor_tensor(tt[0:r, y, g, :].rearrange("p (h d) -> p h d", h=BH),
                                                   rows_b(n)[0:r, g, 0:BW].rearrange("p (h d) -> p h d", h=BH), share, ALU.mult)
                last.then_inc(shared, 1)
                if n >= 2:
                    put_low(dve, n - 2)
            put_low(dve, NT - 2)
            put_low(dve, NT - 1)

NF = 4
NBLK = FF // (NF * P)
BLK_U, BLK_R = 2 * NF, NF + KD
U_OUT = 0
U_MLP = [U_OUT + KD, U_OUT + KD + NBLK * BLK_U + 3 * KD]
U_REC = U_MLP[0] + NBLK * BLK_U
U_REC_OUT = U_REC + 2 * KD
U_END = U_MLP[1] + NBLK * BLK_U
R_OUT = 0
R_MLP = [KD, 0]
R_REC = R_MLP[0] + 1 + NBLK * BLK_R
R_REC_OUT = R_REC + 1 + 4 * KD
R_MLP[1] = R_REC_OUT + KD
SEG = CONVW - 1 + DT
PCOL = DB * SEG
EXT = PCOL + CONVW - 1 + SEQ
CONV = EXT - (CONVW - 1)
CC = -(-CONV // NCH)
NPAR = 3 + CONVW + 4
PAR_CONV, PAR_CB, PAR_GA, PAR_GX, PAR_LRU = 3, 3 + CONVW, 4 + CONVW, 5 + CONVW, 6 + CONVW


XPARTS = 4


class Dense:

    def __init__(self, nc, ctx, a):
        self.nc, self.a = nc, a

        def sb(name, shape, dt=F32):
            return ctx.enter_context(nc.sbuf_tensor(name, shape, dt))

        def sem(name):
            return ctx.enter_context(nc.semaphore("d_" + name))

        self.x = sb("x_t", [P, KD, NCH, CH])
        self.gh = sb("xg_high", [P, KD, NCH, CH], F32R)
        self.gl = sb("xg_low", [P, KD, NCH, CH], F32R)
        self.raw = sb("unit_raw", [P, 2, KD * P])
        self.wh = [sb(f"unit_high{i}", [P, KD * P], F32R) for i in range(2)]
        self.wl = [sb(f"unit_low{i}", [P, KD * P], F32R) for i in range(2)]
        self.par = sb("params", [P, NPAR, KD])
        self.ones = sb("ones_square", [P, P])
        self.ssum = sb("square_sum", [P, NCH, CH])
        self.rstd = sb("rstd_all", [P, NCH, CH])
        self.w_in = [sem(f"w_in{i}") for i in range(2)]
        self.w_high, self.w_low = sem("w_high"), sem("w_low")
        self.made = sem("made")
        self.taken = [sem(f"taken{i}") for i in range(2)]
        self.x_high, self.x_low, self.x_squared, self.x_summed = (
            sem(n) for n in ("x_high", "x_low", "x_squared", "x_summed"))
        self.par_in = sem("par_in")
        self.x_in = [sem(f"x_in{i}") for i in range(XPARTS)]
        self.root_done, self.rstd_done, self.ready = sem("root_done"), sem("rstd_done"), sem("ready")

    def load_first(self, sp):
        for u in range(2):
            sp.dma_start(self.raw[:, u, :], self.a["w_units"][u]).then_inc(self.w_in[u], 16)
        sp.dma_start(self.par[:, :, :], self.a["dense_params"]).then_inc(self.par_in, 16)
        for i in range(XPARTS):
            k = slice(KD // XPARTS * i, KD // XPARTS * (i + 1))
            sp.dma_start(self.x[:, k, :, :].rearrange("p k c n -> p k (c n)"), self.a["xt"][k].rearrange("k p n -> p k n")
                         ).then_inc(self.x_in[i], 16)

    def load(self, sp, u, slot):
        sp.wait_ge(self.w_low, u - 1)
        sp.wait_ge(self.ready, 1)
        sp.dma_start(self.raw[:, slot, :], self.a["w_units"][bass.ds(u, 1), :, :].rearrange("o p n -> p (o n)")
                     ).then_inc(self.w_in[slot], 16)

    def split_high(self, dve, slot, half, made):
        dve.wait_ge(self.w_in[slot], 16 * half + 16)
        dve.wait_ge(self.made, made)
        self.nc.vector.tensor_copy(self.wh[slot][:, :], self.raw[:, slot, :]).then_inc(self.w_high, 1)

    def split_low(self, pool, u, slot):
        pool.wait_ge(self.w_high, u + 1)
        self.nc.gpsimd.tensor_tensor(self.wl[slot][:, :], self.raw[:, slot, :], self.wh[slot][:, :].bitcast(F32),
                                     ALU.subtract).then_inc(self.w_low, 1)

    def product(self, pe, ps, wslot, at, nk, high, low, k_ready=None, ks=None):
        for k in ks or range(nk):
            if k_ready:
                k_ready(k)
            wk = slice(P * (at + k), P * (at + k + 1))
            for n, (w, v) in enumerate(((self.wh, high), (self.wl, high), (self.wh, low))):
                for c in range(NCH):
                    last = self.nc.tensor.matmul(ps[:, c, 0:CH], w[wslot][:, wk], v[:, k, c, :],
                                                 start=(k == 0 and n == 0), stop=(k == nk - 1 and n == 2))
        if k == nk - 1:
            last.then_inc(self.made, 1)

    def part_high(self, act, n, gain):
        self.nc.scalar.activation(self.gh[:, n, :, :], self.x[:, n, :, :], ACT.Copy, scale=self.par[:, gain, n:n + 1]
                                  ).then_inc(self.x_high, 1)

    def part_low(self, dve, n, seen, gain):
        dve.wait_ge(self.x_high, seen + n + 1)
        self.nc.vector.scalar_tensor_tensor(out=self.gl[:, n, :, :], in0=self.x[:, n, :, :], scalar=self.par[:, gain, n:n + 1],
                                            in1=self.gh[:, n, :, :].bitcast(F32), op0=ALU.mult, op1=ALU.subtract
                                            ).then_inc(self.x_low, 1)

    def square(self, act, sq, n, seen):
        if n >= 2:
            act.wait_ge(self.x_summed, (seen // KD) * (KD - 1) + n - 1)
        self.nc.scalar.activation(sq[n % 2], self.x[:, n, :, :], ACT.Square).then_inc(self.x_squared, 1)

    def sum_up(self, pool, sq, n, seen):
        pool.wait_ge(self.x_squared, seen + n + 1)
        if n == 0:
            return
        if n >= 2:
            pool.wait_ge(self.x_summed, (seen // KD) * (KD - 1) + n - 1)
        first = sq[0] if n == 1 else self.ssum[:, :, :]
        self.nc.gpsimd.tensor_tensor(self.ssum[:, :, :], first, sq[n % 2], ALU.add).then_inc(self.x_summed, 1)

    def sums_pe(self, pe, ps, nth, ring):
        pe.wait_ge(self.x_summed, (KD - 1) * (nth + 1))
        pe.wait_ge(self.taken[ring % 2], ring // 2)
        for c in range(NCH):
            last = self.nc.tensor.matmul(ps[ring % 2][:, c, 0:CH], self.ones[:, :], self.ssum[:, c, :], start=True, stop=True)
        last.then_inc(self.made, 1)

    def sums_dve(self, dve, ps, nth, ring):
        dve.wait_ge(self.made, ring + 1)
        self.nc.vector.tensor_scalar(self.rstd[:, :, :], ps[ring % 2][:, :, 0:CH], 1.0 / D, EPS, ALU.mult, ALU.add
                                     ).then_inc(self.taken[ring % 2], 1)
        dve.wait_ge(self.root_done, nth + 1)
        self.nc.vector.reciprocal(self.rstd[:, :, :], self.rstd[:, :, :]).then_inc(self.rstd_done, 1)
        dve.wait_ge(self.rstd_done, nth + 1)

    def sums_act(self, act, nth, ring):
        act.wait_ge(self.taken[ring % 2], ring // 2 + 1)
        self.nc.scalar.activation(self.rstd[:, :, :], self.rstd[:, :, :], ACT.Sqrt).then_inc(self.root_done, 1)


def slots(nc, ctx, tag):
    return [ctx.enter_context(nc.psum_tensor(f"{tag}_ps{i}", [P, NCH, 512], F32)) for i in range(2)]


def stage_out_projection(nc, a, d, oth, otl):
    with ExitStack() as ctx:
        sq = [ctx.enter_context(nc.sbuf_tensor(f"op_sq{i}", [P, NCH, CH], F32))[:, :, :] for i in range(2)]
        ps = slots(nc, ctx, "op")
        block = ctx.enter_context(nc.Block())

        @block.sync
        def _(sp):
            for u in range(2, KD + 2):
                d.load(sp, u, u % 2)

        @block.gpsimd
        def _(pool):
            nc.gpsimd.memset(d.ones[:, :], 1.0).then_inc(d.ready, 1)
            d.split_low(pool, 0, 0)
            d.split_low(pool, 1, 1)
            for n in range(KD):
                d.split_low(pool, n + 2, n % 2)
                d.sum_up(pool, sq, n, 0)

        @block.scalar
        def _(act):
            act.wait_ge(d.par_in, 16)
            for n in range(KD):
                act.wait_ge(d.taken[n % 2], n // 2 + 1)
                d.part_high(act, n, 0)
                d.square(act, sq, n, 0)

        @block.tensor
        def _(pe):
            for u in range(KD):
                pe.wait_ge(d.w_low, u + 1)
                if u >= 2:
                    pe.wait_ge(d.taken[u % 2], u // 2)
                d.product(pe, ps[u % 2], u % 2, 0, 6, oth, otl)

        @block.vector
        def _(dve):
            for u in range(2):
                dve.wait_ge(d.w_in[u], 16)
                nc.vector.tensor_copy(d.wh[u][:, :], d.raw[:, u, :]).then_inc(d.w_high, 1)
            dve.wait_ge(d.par_in, 16)
            for n in range(KD):
                dve.wait_ge(d.x_in[n // (KD // XPARTS)], 16)
                dve.wait_ge(d.made, n + 1)
                nc.vector.tensor_tensor(d.x[:, n, :, :], d.x[:, n, :, :], ps[n % 2][:, :, 0:CH], ALU.add
                                        ).then_inc(d.taken[n % 2], 1)
                d.split_high(dve, n % 2, (n + 2) // 2, n + 1)
                dve.wait_ge(d.taken[n % 2], n // 2 + 1)
                d.part_low(dve, n, 0, 0)


def stage_mlp(nc, a, d, layer, nth, y=None):
    U0, R0 = U_MLP[layer], R_MLP[layer] + 1
    FREE = 2
    seen = KD * (nth + 1)
    with ExitStack() as ctx:
        def sem(name):
            return ctx.enter_context(nc.semaphore(f"m{layer}_{name}"))

        def sb(name, shape, dt=F32):
            return ctx.enter_context(nc.sbuf_tensor(f"m{layer}_{name}", shape, dt))

        hh = sb("hidden_high", [P, NF, NCH, CH], F32R)
        hl = sb("hidden_low", [P, NF, NCH, CH], F32R)
        r = sb("relu", [P, 2, NCH, CH])
        v = sb("square", [P, 2, NCH, CH])
        ps = slots(nc, ctx, f"m{layer}")
        relu_scaled, h_high, squared, h_low, y_out = (sem(n) for n in ("relu_scaled", "h_high", "squared", "h_low", "y_out"))
        block = ctx.enter_context(nc.Block())

        def run(eng, up, down, last=None):
            up(0)
            with eng.Fori(0, NBLK - 1) as b:
                down(b)
                up(b + 1)
            (last or down)(NBLK - 1)

        def up_at(b, i):
            return (U0 + i + BLK_U * b, i % 2, (U0 + i) // 2 + BLK_U // 2 * b,
                    R0 + i + BLK_R * b, (R0 + i) % 2, (R0 + i) // 2 + BLK_R // 2 * b)

        def down_at(b, m):
            i, q = NF + m, NF + 2 * m
            return (U0 + i + BLK_U * b, i % 2, (U0 + i) // 2 + BLK_U // 2 * b,
                    R0 + q + BLK_R * b, (R0 + q) % 2, (R0 + q) // 2 + BLK_R // 2 * b)

        @block.sync
        def _(sp):
            def up(b):
                for i in range(NF):
                    u, slot = up_at(b, i)[:2]
                    d.load(sp, u + 2, slot)

            def down(b):
                for m in range(NF):
                    u, slot = down_at(b, m)[:2]
                    if not isinstance(u, int) or u + 2 < U_END:
                        d.load(sp, u + 2, slot)

            run(sp, up, down)
            if y is not None:
                for n in range(KD):
                    _, _, _, _, slot, used = down_at(NBLK - 1, n // 2)
                    sp.wait_ge(d.taken[(slot + n) % 2], used + (slot + n % 2) // 2 + 1)
                    sp.dma_start(y[n], d.x[:, n, :, :].rearrange("p c n -> p (c n)")).then_inc(y_out, 16)
                sp.wait_ge(y_out, 16 * KD)

        @block.gpsimd
        def _(pool):
            nc.gpsimd.sem_inc(squared, FREE)
            nc.gpsimd.sem_inc(h_low, FREE)

            def up(b):
                for i in range(NF):
                    u, slot = up_at(b, i)[:2]
                    n = NF * b + i
                    d.split_low(pool, u + 2, slot)
                    pool.wait_ge(h_high, n + 1)
                    pool.wait_ge(squared, n + 1 + FREE)
                    nc.gpsimd.tensor_tensor(hl[:, i, :, :], v[:, i % 2, :, :], hh[:, i, :, :].bitcast(F32), ALU.subtract
                                            ).then_inc(h_low, 1)

            def down(b):
                for m in range(NF):
                    u, slot = down_at(b, m)[:2]
                    if not isinstance(u, int) or u + 2 < U_END:
                        d.split_low(pool, u + 2, slot)
                    if isinstance(b, int) and y is None:
                        for n in (2 * m, 2 * m + 1):
                            d.sum_up(pool, [v[:, 0, :, :], v[:, 1, :, :]], n, seen)

            run(pool, up, down)

        @block.scalar
        def _(act):
            if layer:
                for n in range(KD):
                    d.part_high(act, n, 2)
            d.sums_act(act, nth, R_MLP[layer])

            def up(b):
                for i in range(NF):
                    _, _, _, use, slot, _ = up_at(b, i)
                    n = NF * b + i
                    act.wait_ge(d.made, use + 1)
                    act.wait_ge(squared, n + 1)
                    nc.scalar.activation(r[:, i % 2, :, :], ps[slot][:, :, 0:CH], ACT.Relu).then_inc(d.taken[slot], 1)
                    act.wait_ge(relu_scaled, n + 1)
                    nc.scalar.activation(hh[:, i, :, :], r[:, i % 2, :, :], ACT.Square).then_inc(h_high, 1)

            def down(b):
                if isinstance(b, int) and y is None:
                    for n in range(KD):
                        _, _, _, _, slot, used = down_at(b, n // 2)
                        act.wait_ge(d.taken[(slot + n) % 2], used + (slot + n % 2) // 2 + 1)
                        d.part_high(act, n, layer + 1)
                        d.square(act, [v[:, 0, :, :], v[:, 1, :, :]], n, seen)

            run(act, up, down)

        @block.tensor
        def _(pe):
            d.sums_pe(pe, ps, nth, R_MLP[layer])

            def up(b):
                for i in range(NF):
                    u, wslot, _, _, slot, used = up_at(b, i)
                    pe.wait_ge(d.w_low, u + 1)
                    pe.wait_ge(d.taken[slot], used)
                    d.product(pe, ps[slot], wslot, 0, KD, d.gh, d.gl,
                              (lambda k: pe.wait_ge(d.x_low, seen - KD + k + 1)) if isinstance(b, int) and b == 0 and i == 0 else None)

            def down(b):
                for m in range(NF):
                    u, wslot, _, _, slot, used = down_at(b, m)
                    pe.wait_ge(d.w_low, u + 1)
                    for ks in ([range(NF - 1), range(NF - 1, NF)] if m == 0 else [range(NF)]):
                        for x in range(2):
                            s = (slot + x) % 2
                            if ks[0] == 0:
                                pe.wait_ge(d.taken[s], used + (slot + x) // 2)
                            d.product(pe, ps[s], wslot, NF * x, NF, hh, hl,
                                      (lambda k: pe.wait_ge(h_low, NF * b + k + 1 + FREE)) if m == 0 and x == 0 else None, ks)

            run(pe, up, down)

        @block.vector
        def _(dve):
            if layer:
                for n in range(KD):
                    d.part_low(dve, n, seen - KD, 2)
            d.sums_dve(dve, ps, nth, R_MLP[layer])

            def up(b):
                for i in range(NF):
                    _, wslot, half, use, slot, used = up_at(b, i)
                    n = NF * b + i
                    dve.wait_ge(d.taken[slot], used + 1)
                    nc.vector.tensor_tensor(r[:, i % 2, :, :], r[:, i % 2, :, :], d.rstd[:, :, :], ALU.mult).then_inc(relu_scaled, 1)
                    d.split_high(dve, wslot, half + 1, use + 1)
                    dve.wait_ge(relu_scaled, n + 1)
                    dve.wait_ge(h_low, n + 1)
                    nc.vector.tensor_tensor(v[:, i % 2, :, :], r[:, i % 2, :, :], r[:, i % 2, :, :], ALU.mult).then_inc(squared, 1)

            def down(b):
                for m in range(NF):
                    u, wslot, half, use, slot, used = down_at(b, m)
                    for x in range(2):
                        s, n = (slot + x) % 2, 2 * m + x
                        dve.wait_ge(d.made, use + x + 1)
                        nc.vector.tensor_tensor(d.x[:, n, :, :], d.x[:, n, :, :], ps[s][:, :, 0:CH], ALU.add).then_inc(d.taken[s], 1)
                    if not isinstance(u, int) or u + 2 < U_END:
                        d.split_high(dve, wslot, half + 1, use + 2)
                    if isinstance(b, int) and y is None:
                        for x in range(2):
                            dve.wait_ge(d.taken[(slot + x) % 2], used + (slot + x) // 2 + 1)
                            d.part_low(dve, 2 * m + x, seen, layer + 1)

            run(dve, up, down)


def stage_recurrent(nc, a, o, d, nth, proj, kiwi, own):
    seen = KD * (nth + 1)
    R1 = R_REC + 1
    ORDER = [("x", 0), ("g", 0)]
    for _n in range(1, KD):
        ORDER += [("x", _n), ("g", _n), ("a", _n - 1), ("i", _n - 1)]
    ORDER += [("a", KD - 1), ("i", KD - 1)]
    USE = {k: R1 + i for i, k in enumerate(ORDER)}
    with ExitStack() as ctx:
        def sem(name):
            return ctx.enter_context(nc.semaphore("r_" + name))

        def sb(name, shape, dt=F32):
            return ctx.enter_context(nc.sbuf_tensor("r_" + name, shape, dt))

        xs = sb("conv_in", [P, EXT])
        cv = sb("conv", [P, 2, NCH, CC])
        ra = sb("decay", [P, NCH, CC])
        ig = sb("input_gate", [P, NCH, CC])
        th = sb("tanh", [P, NCH, CC])
        gm = [sb("gate", [P, TOK]), d.ssum[:, :, :].rearrange("p c n -> p (c n)")]
        hg = sb("gated", [P, KD, NCH, CH])
        st = sb("states", [P, KD, DB * 3])
        h0 = sb("first_state", [P, KD, DB + 1])
        gw = own.a[:, :].rearrange("p (s x n) -> p s x n", s=2, x=2)
        so = own.b[:, :, :].rearrange("p g n -> p (g n)")[:, 0:KD * 36].rearrange("p (k n) -> p k n", k=KD)
        ls = sb("log_sigmoid", [P, 8, KD])
        ps = slots(nc, ctx, "r")
        names = ("small_in states_copied conv_done tails gelu tanh decay squared_a "
                 "dual root gated_in drive fixed scanned h_out hg_done gh gl lru pad st_out").split()
        S = {n: sem(n) for n in names}
        gw_in = [sem(f"gw_in{i}") for i in range(2)]
        cache_out = sem("cache_out")
        caches = [(o["kv_a"], proj[:, 512:768]), (o["ki"], kiwi[:, 0:IDX])]
        for g in range(NG):
            wp, ws, c = min(WIN[g], SEQ), WL[g], 768 * (g + 1) + BW
            caches += [(o[f"p_win{g}"], proj[TS + SEQ - wp:TS + SEQ, c:c + 2 * BW]),
                       (o[f"s_win{g}"][:, 0:ws - DT, :], a[f"win_cache{g}"][:, DT:ws, :]),
                       (o[f"s_win{g}"][:, ws - DT:ws, :], proj[0:TS, c:c + 2 * BW].rearrange("(b t) c -> b t c", t=DT))]
        block = ctx.enter_context(nc.Block())
        flat = {id(t): t[:, :, :].rearrange("p c n -> p (c n)") for t in (ra, ig, th)}
        raf, igf, thf = (flat[id(t)] for t in (ra, ig, th))
        sqf = xs[:, 0:NCH * CC]
        xsq = [t[:, :, 0:CH] for t in (ra, ig)]
        LRU_STEPS = 12
        LS8, NLS8 = 6, 7

        def samples(v, width):
            return v[:, 0:PCOL].rearrange("p (b s) -> p b s", s=SEG)[:, :, SEG - width:SEG]

        @block.sync
        def _(sp):
            sp.dma_start(st[:, :, :], a["conv_states"]).then_inc(S["small_in"], 16)
            sp.dma_start(h0[:, :, :], a["first_states"]).then_inc(S["small_in"], 16)

            def load_gates(n):
                if n >= 2:
                    sp.wait_ge(d.made, USE["i", n - 2] + 1)
                sp.dma_start(gw[:, n % 2, :, :], a["gate_w"][n]).then_inc(gw_in[n % 2], 16)

            for n in range(KD):
                if n < 2:
                    load_gates(n)
                for x in range(2):
                    d.load(sp, U_REC + 2 * n + x + 2, x)
                if n >= 2:
                    load_gates(n)
                sp.dma_start(*caches[n]).then_inc(cache_out, 16)
            for n in range(KD):
                d.load(sp, U_REC_OUT + n + 2, n % 2)
                if KD + n < len(caches):
                    sp.dma_start(*caches[KD + n]).then_inc(cache_out, 16)
            sp.wait_ge(cache_out, 16 * len(caches))
            sp.wait_ge(S["h_out"], KD)
            sp.wait_ge(S["tails"], KD)
            sp.dma_start(o["state_out"], so[:, :, :]).then_inc(S["st_out"], 16)
            sp.wait_ge(S["st_out"], 16)

        @block.gpsimd
        def _(pool):
            nc.gpsimd.memset(xs[:, :], 0.0).then_inc(S["pad"], 1)
            nc.gpsimd.memset(cv[:, :, :, :], 0.0).then_inc(S["pad"], 1)
            nc.gpsimd.memset(hg[:, :, NCH - 1, TS + SEQ - CH * (NCH - 1):CH], 0.0).then_inc(S["pad"], 1)
            for n in range(KD + 1):
                if n < KD:
                    for x in range(2):
                        d.split_low(pool, U_REC + 2 * n + x + 2, x)
                if n >= 1:
                    m = n - 1
                    pool.wait_ge(S["decay"], m + 1)
                    pool.wait_ge(S["conv_done"], 4 * min(m + 2, KD))
                    pool.wait_ge(S["tails"], min(m + 2, KD))
                    if m == KD - 1:
                        pool.wait_ge(S["dual"], m)
                    nc.gpsimd.tensor_tensor(sqf, raf, raf, ALU.mult).then_inc(S["squared_a"], 1)
                    pool.wait_ge(S["conv_done"], 4 * (m + 1))
                    nc.gpsimd.tensor_tensor(ig[:, :, :], ig[:, :, :], cv[:, m % 2, :, :], ALU.mult).then_inc(S["gated_in"], 1)
            for n in range(KD):
                d.split_low(pool, U_REC_OUT + n + 2, n % 2)
                d.sum_up(pool, xsq, n, seen)

        @block.scalar
        def _(act):
            d.sums_act(act, nth, R_REC)
            lru = d.par[:, PAR_LRU, :]
            nc.scalar.activation(ls[:, 0, :], lru, ACT.Abs).then_inc(S["lru"], 1)
            act.wait_ge(S["lru"], 1)
            nc.scalar.activation(ls[:, 1, :], ls[:, 0, :], ACT.Exp, scale=-1.0).then_inc(S["lru"], 1)
            act.wait_ge(S["lru"], 3)
            nc.scalar.activation(ls[:, 3, :], ls[:, 2, :], ACT.Ln).then_inc(S["lru"], 1)

            def gelu(n):
                use = USE["g", n]
                act.wait_ge(d.taken[use % 2], use // 2 + 1)
                nc.scalar.activation(gm[n % 2][:, :], gm[n % 2][:, :], ACT.Gelu_apprx_tanh).then_inc(S["gelu"], 1)

            def part(k):
                act.wait_ge(S["hg_done"], 2 * (k + 1))
                nc.scalar.activation(d.gh[:, k, :, :], hg[:, k, :, :], ACT.Copy).then_inc(S["gh"], 1)

            gelu(0)
            for n in range(1, KD + 1):
                m = n - 1
                if m == 0:
                    act.wait_ge(S["lru"], LRU_STEPS)
                for kind, dst, bias in (("a", ra, PAR_GA), ("i", ig, PAR_GX)):
                    use = USE[kind, m]
                    act.wait_ge(d.made, use + 1)
                    if m:
                        act.wait_ge(S["scanned"], m)
                    nc.scalar.activation(dst[:, :, :], ps[use % 2][:, :, 0:CC], ACT.Sigmoid, bias=d.par[:, bias, m:m + 1]
                                         ).then_inc(d.taken[use % 2], 1)
                act.wait_ge(d.taken[USE["a", m] % 2], USE["a", m] // 2 + 1)
                act.wait_ge(d.taken[USE["i", m] % 2], USE["i", m] // 2 + 1)
                if m:
                    act.wait_ge(S["hg_done"], 2 * m)
                    act.wait_ge(S["h_out"], m)
                nc.scalar.activation(thf, raf, ACT.Tanh, scale=ls[:, NLS8, m:m + 1]).then_inc(S["tanh"], 1)
                act.wait_ge(S["tanh"], m + 1)
                nc.scalar.activation(raf, raf, ACT.Exp, scale=ls[:, LS8, m:m + 1]).then_inc(S["decay"], 1)
                act.wait_ge(S["decay"], m + 1)
                act.wait_ge(S["dual"], m + 1)
                nc.scalar.activation(thf, thf, ACT.Sqrt).then_inc(S["root"], 1)
                if n < KD:
                    gelu(n)
                if n == KD - 1:
                    act.wait_ge(d.made, USE["g", KD - 1] + 1)
                    act.wait_ge(S["pad"], 3)
                    for k in range(KD - 2):
                        part(k)
                elif n == KD:
                    part(KD - 2)
                    part(KD - 1)
            for n in range(KD):
                r = R_REC_OUT + n
                act.wait_ge(d.taken[r % 2], r // 2 + 1)
                d.square(act, xsq, n, seen)

        @block.tensor
        def _(pe):
            d.sums_pe(pe, ps, nth, R_REC)

            def inputs(n):
                for x, kind in enumerate("xg"):
                    use, u = USE[kind, n], U_REC + 2 * n + x
                    pe.wait_ge(d.w_low, u + 1)
                    pe.wait_ge(d.taken[use % 2], use // 2)
                    d.product(pe, ps[use % 2], x, 0, KD, d.gh, d.gl,
                              (lambda k: pe.wait_ge(d.x_low, seen - KD + k + 1)) if n == 0 and x == 0 else None)

            def gates(n):
                pe.wait_ge(gw_in[n % 2], 16 * (n // 2 + 1))
                pe.wait_ge(S["conv_done"], 4 * (n + 1))
                for x, kind in enumerate("ai"):
                    use = USE[kind, n]
                    pe.wait_ge(d.taken[use % 2], use // 2)
                    for c in range(NCH):
                        last = nc.tensor.matmul(ps[use % 2][:, c, 0:CC], gw[:, n % 2, x, :], cv[:, n % 2, c, :],
                                                start=True, stop=True)
                    last.then_inc(d.made, 1)

            inputs(0)
            for n in range(1, KD):
                inputs(n)
                gates(n - 1)
            gates(KD - 1)
            early, late = range(KD - 2), range(KD - 2, KD)
            for n, ks in [(0, early), (1, early), (0, late), (1, late)] + [(n, range(KD)) for n in range(2, KD)]:
                r = R_REC_OUT + n
                if ks[0] == 0:
                    pe.wait_ge(d.w_low, U_REC_OUT + n + 1)
                    pe.wait_ge(d.taken[r % 2], r // 2)
                d.product(pe, ps[r % 2], n % 2, 0, KD, d.gh, d.gl,
                          (lambda k: pe.wait_ge(S["gl"], k + 1)) if n == 0 else None, ks)

        @block.vector
        def _(dve):
            def lru_step(ins):
                ins.then_inc(S["lru"], 1)

            d.sums_dve(dve, ps, nth, R_REC)
            e, u, ln, den, val = (ls[:, i, :] for i in (1, 2, 3, 4, 5))
            dve.wait_ge(S["lru"], 2)
            lru_step(nc.vector.tensor_scalar(u, e, 1.0, None, ALU.add))
            dve.wait_ge(S["lru"], 4)
            lru_step(nc.vector.tensor_scalar(den, u, 1.0, 1e-30, ALU.subtract, ALU.max))
            dve.wait_ge(S["lru"], 5)
            lru_step(nc.vector.reciprocal(val, den))
            dve.wait_ge(S["lru"], 6)
            lru_step(nc.vector.tensor_tensor(val, val, e, ALU.mult))
            dve.wait_ge(S["lru"], 7)
            lru_step(nc.vector.tensor_tensor(val, val, ln, ALU.mult))
            dve.wait_ge(S["lru"], 8)
            lru_step(nc.vector.scalar_tensor_tensor(out=den, in0=u, scalar=1.0, in1=e, op0=ALU.is_equal, op1=ALU.mult))
            dve.wait_ge(S["lru"], 9)
            lru_step(nc.vector.tensor_tensor(val, val, den, ALU.add))
            dve.wait_ge(S["lru"], 10)
            lru_step(nc.vector.scalar_tensor_tensor(out=den, in0=d.par[:, PAR_LRU, :], scalar=0.0, in1=val,
                                                    op0=ALU.min, op1=ALU.subtract))
            dve.wait_ge(S["lru"], 11)
            nc.vector.tensor_scalar(ls[:, LS8, :], den, LRU_C, None, ALU.mult)
            lru_step(nc.vector.tensor_scalar(ls[:, NLS8, :], den, -LRU_C, None, ALU.mult))
            dve.wait_ge(S["small_in"], 32)
            dve.wait_ge(S["pad"], 3)

            def convolve(n):
                use = USE["x", n]
                z = ps[use % 2]
                dve.wait_ge(d.made, use + 1)
                if n:
                    dve.wait_ge(S["tails"], n)
                    dve.wait_ge(S["conv_done"], 4 * n)
                if n >= 2:
                    dve.wait_ge(S["dual"], n - 1)
                nc.vector.memset(xs[:, PCOL:PCOL + CONVW - 1], 0.0).then_inc(S["states_copied"], 1)
                nc.vector.tensor_copy(xs[:, 0:PCOL].rearrange("p (b s) -> p b s", s=SEG)[:, :, 0:CONVW - 1],
                                      st[:, n, :].rearrange("p (b s) -> p b s", b=DB)).then_inc(S["states_copied"], 1)
                nc.vector.tensor_tensor(samples(xs, DT), z[:, 0, 0:TS].rearrange("p (b t) -> p b t", b=DB),
                                        d.rstd[:, 0, 0:TS].rearrange("p (b t) -> p b t", b=DB), ALU.mult)
                at = PCOL + CONVW - 1
                for c in range(NCH):
                    lo, hi = (TS if c == 0 else 0), (CH if c < NCH - 1 else TS + SEQ - CH * (NCH - 1))
                    last = nc.vector.tensor_tensor(xs[:, at:at + hi - lo], z[:, c, lo:hi], d.rstd[:, c, lo:hi], ALU.mult)
                    at += hi - lo
                last.then_inc(d.taken[use % 2], 1)
                dve.wait_ge(d.taken[use % 2], use // 2 + 1)
                if n >= 2:
                    dve.wait_ge(d.made, USE["i", n - 2] + 1)
                    dve.wait_ge(S["gated_in"], n - 1)
                dve.wait_ge(S["states_copied"], 2 * (n + 1))
                v = cv[:, n % 2, :, :].rearrange("p c n -> p (c n)")[:, 0:CONV]
                par = lambda i: d.par[:, i, n:n + 1]
                nc.vector.tensor_scalar(v, xs[:, 0:CONV], par(PAR_CONV), par(PAR_CB), ALU.mult, ALU.add).then_inc(S["conv_done"], 1)
                for i in range(1, CONVW):
                    dve.wait_ge(S["conv_done"], 4 * n + i)
                    nc.vector.scalar_tensor_tensor(out=v, in0=xs[:, i:i + CONV], scalar=par(PAR_CONV + i), in1=v,
                                                   op0=ALU.mult, op1=ALU.add).then_inc(S["conv_done"], 1)
                nc.vector.tensor_copy(so[:, n, 0:24].rearrange("p (b s) -> p b s", b=DB), samples(xs, CONVW - 1))
                nc.vector.tensor_copy(so[:, n, 24:27], xs[:, EXT - (CONVW - 1):EXT]).then_inc(S["tails"], 1)

            def scale_gate(n):
                use = USE["g", n]
                dve.wait_ge(d.made, use + 1)
                if n >= 2:
                    dve.wait_ge(S["hg_done"], 2 * (n - 1))
                nc.vector.tensor_tensor(gm[n % 2][:, :].rearrange("p (c n) -> p c n", c=NCH), ps[use % 2][:, :, 0:CH],
                                        d.rstd[:, :, :], ALU.mult).then_inc(d.taken[use % 2], 1)

            def recur(m):
                dve.wait_ge(S["squared_a"], m + 1)
                dve.wait_ge(S["tanh"], m + 1)
                nc.vector.scalar_tensor_tensor(out=thf, in0=sqf, scalar=1.0, in1=thf, op0=ALU.add, op1=ALU.mult).then_inc(S["dual"], 1)
                dve.wait_ge(S["root"], m + 1)
                dve.wait_ge(S["gated_in"], m + 1)
                nc.vector.tensor_tensor(igf, igf, thf, ALU.mult).then_inc(S["drive"], 1)
                dve.wait_ge(S["drive"], m + 1)
                last_of = lambda v: v[:, 0:PCOL].rearrange("p (b s) -> p b s", s=SEG)[:, :, SEG - 1:SEG]
                nc.vector.memset(last_of(raf), 0.0).then_inc(S["fixed"], 1)
                nc.vector.tensor_copy(last_of(igf), h0[:, m, 1:DB + 1].rearrange("p (b o) -> p b o", o=1)).then_inc(S["fixed"], 1)
                dve.wait_ge(S["fixed"], 2 * (m + 1))
                nc.vector.tensor_tensor_scan(thf[:, 0:CONV], raf[:, 0:CONV], igf[:, 0:CONV], h0[:, m, 0:1], ALU.mult, ALU.add
                                             ).then_inc(S["scanned"], 1)
                dve.wait_ge(S["scanned"], m + 1)
                dve.wait_ge(S["gelu"], m + 1)
                hgf = hg[:, m, :, :].rearrange("p c n -> p (c n)")
                seq = lambda v: v[:, 0:TS].rearrange("p (b t) -> p b t", b=DB)
                nc.vector.tensor_tensor(seq(hgf), thf[:, 0:PCOL].rearrange("p (b s) -> p b s", s=SEG)[:, :, 0:DT],
                                        seq(gm[m % 2][:, :]), ALU.mult).then_inc(S["hg_done"], 1)
                nc.vector.tensor_tensor(hgf[:, TS:TS + SEQ], thf[:, PCOL:CONV], gm[m % 2][:, TS:TS + SEQ], ALU.mult
                                        ).then_inc(S["hg_done"], 1)
                nc.vector.tensor_copy(so[:, m, 27:35].rearrange("p (b o) -> p b o", o=1),
                                      thf[:, 0:PCOL].rearrange("p (b s) -> p b s", s=SEG)[:, :, DT - 1:DT])
                nc.vector.tensor_copy(so[:, m, 35:36], thf[:, CONV - 1:CONV]).then_inc(S["h_out"], 1)

            def part_low(k):
                dve.wait_ge(S["gh"], k + 1)
                nc.vector.tensor_tensor(d.gl[:, k, :, :], hg[:, k, :, :], d.gh[:, k, :, :].bitcast(F32), ALU.subtract
                                        ).then_inc(S["gl"], 1)

            for n in range(KD):
                convolve(n)
                d.split_high(dve, 0, (U_REC + 2 * n + 2) // 2, USE["x", n] + 1)
                scale_gate(n)
                d.split_high(dve, 1, (U_REC + 2 * n + 3) // 2, USE["g", n] + 1)
                if n:
                    recur(n - 1)
            for k in range(KD - 2):
                part_low(k)
            recur(KD - 1)
            for k in range(KD - 2, KD):
                part_low(k)
            for n in range(KD):
                r = R_REC_OUT + n
                dve.wait_ge(d.made, r + 1)
                nc.vector.tensor_tensor(d.x[:, n, :, :], d.x[:, n, :, :], ps[r % 2][:, :, 0:CH], ALU.add
                                        ).then_inc(d.taken[r % 2], 1)
                d.split_high(dve, n % 2, (U_REC_OUT + n + 2) // 2, r + 1)


def device_inputs(x):
    f = lambda v: np.ascontiguousarray(v, dtype=np.float32)
    tok = np.zeros((TOK, D), np.float32)
    tok[0:TS] = np.asarray(x["x_sample"]).reshape(TS, D)
    tok[TS:TS + SEQ] = np.asarray(x["x_prompt"]).reshape(SEQ, D)
    w = np.asarray(x["attn_w_in"])[0]
    qa, ka, va, qi, ki, wi, hb = np.split(w, [512, 640, 768, 1280, 1344, 1352], axis=1)
    hb = hb.reshape(D, NG, 3, BW)
    w = np.concatenate([ki, wi, ka, va, qi, qa, *[hb[:, g, 0:2].reshape(D, 2 * BW) for g in range(NG)],
                        *[hb[:, g, 2] for g in range(NG)]], axis=1).reshape(KD, P, IN_W)
    norms = [np.asarray(x["a_q_norm"])[0], np.asarray(x["a_k_norm"])[0]]
    for g in range(NG):
        norms += [np.asarray(x["b_q_norm"])[0, g], np.asarray(x["b_k_norm"])[0, g]]
    steps = np.arange(TS) % DT
    d = {
        "xt": f(tok.T.reshape(KD, P, TOK)),
        "norm_mix0": f(np.asarray(x["norm_mix"])[0].reshape(KD, P).T),
        "rel_bias": f(x["rel_bias"]),
        "bias_pick": bias_selector(),
        "w_in": f(w),
        "head_gains": f(np.stack(norms)),
        "same_step": f(steps[:, None] == np.arange(DT)[None]),
        "later_step": f(np.where(np.arange(DT)[None] > steps[:, None], NEG, 0.0)),
        "page_table": np.ascontiguousarray(np.asarray(x["page_table"]).reshape(1, -1), dtype=np.int32),
        "kv_keys_t": f(np.asarray(x["cache_a_kv"])[0, :, :, 0].reshape(-1, PAGE, P).transpose(0, 2, 1)),
        "kv_values": f(np.asarray(x["cache_a_kv"])[0, :, :, 1].reshape(-1, PAGE, P)),
        "kidx_t": f(np.asarray(x["cache_a_kidx"])[0].transpose(0, 2, 1)),
    }
    for g in range(NG):
        c = np.asarray(x[f"cache_b_kv_w{WIN[g]}"])[0]
        d[f"win_keys_t{g}"] = f(c[:, :, 0].reshape(DB, WL[g], 2, P).transpose(0, 3, 2, 1).reshape(DB, P, 2 * WL[g]))
        d[f"win_cache{g}"] = f(c.reshape(DB, WL[g], 2 * BW))
    units = np.zeros((U_END, P, KD, P), np.float32)

    def tiles(w):
        return np.asarray(w).reshape(w.shape[0] // P, P, w.shape[1] // P, P)

    units[U_OUT:U_OUT + KD, :, 0:6] = tiles(np.asarray(x["attn_w_out"])[0]).transpose(2, 1, 0, 3)
    for l in range(2):
        up = tiles(np.asarray(x["mlp_w1"])[l]).transpose(2, 1, 0, 3)
        down = tiles(np.asarray(x["mlp_w2"])[l])
        for b in range(NBLK):
            u = U_MLP[l] + BLK_U * b
            units[u:u + NF] = up[NF * b:NF * (b + 1)]
            for m in range(NF):
                units[u + NF + m] = down[NF * b:NF * (b + 1), :, 2 * m:2 * m + 2].transpose(1, 2, 0, 3).reshape(P, KD, P)
    rec = tiles(np.asarray(x["rec_w_in"])[0]).transpose(2, 1, 0, 3)
    units[U_REC:U_REC_OUT:2] = rec[KD:]
    units[U_REC + 1:U_REC_OUT:2] = rec[:KD]
    units[U_REC_OUT:U_REC_OUT + KD] = tiles(np.asarray(x["rec_w_out"])[0]).transpose(2, 1, 0, 3)
    d["w_units"] = units.reshape(U_END, P, KD * P)
    par = [np.asarray(x["norm_mlp"])[0], np.asarray(x["norm_mix"])[1], np.asarray(x["norm_mlp"])[1],
           *np.asarray(x["rec_conv_w"])[0], np.asarray(x["rec_conv_b"])[0], np.asarray(x["rec_gate_a_b"])[0],
           np.asarray(x["rec_gate_x_b"])[0], np.asarray(x["rec_lru_a"])[0]]
    d["dense_params"] = f(np.stack(par).reshape(NPAR, KD, P).transpose(2, 0, 1))
    d["conv_states"] = f(np.asarray(x["state_c_conv"])[0].reshape(DB, CONVW - 1, KD, P).transpose(3, 2, 0, 1).reshape(P, KD, -1))
    h0 = np.zeros((P, KD, DB + 1), np.float32)
    h0[:, :, 0:DB] = np.asarray(x["state_c_h"])[0].reshape(DB, KD, P).transpose(2, 1, 0)
    d["first_states"] = h0
    d["gate_w"] = f(np.stack([np.asarray(x["rec_gate_a_w"])[0], np.asarray(x["rec_gate_x_w"])[0]], 2))
    return d


def device_outputs():
    out = {"y_t": (KD, P, TOK), "kv_a": (TS + SEQ, 2 * AG * HD), "ki": (TS + SEQ, IDX), "state_out": (P, KD, 36)}
    for g in range(NG):
        out[f"p_win{g}"] = (min(WIN[g], SEQ), 2 * BW)
        out[f"s_win{g}"] = (DB, WL[g], 2 * BW)
    return out


def results(r):
    y = r["y_t"].reshape(D, TOK).T
    kv = r["kv_a"].reshape(TS + SEQ, 2, AG, HD)
    so = r["state_out"].transpose(2, 1, 0).reshape(36, D)
    shape = lambda v, *s: np.ascontiguousarray(v).reshape(s)
    pw = [shape(r[f"p_win{g}"], 1, 1, min(WIN[g], SEQ), 2, BH, HD) for g in range(NG)]
    sw = [shape(r[f"s_win{g}"], 1, DB, WL[g], 2, BH, HD) for g in range(NG)]
    return (shape(y[TS:TS + SEQ], 1, SEQ, D), shape(y[0:TS], DB, DT, D),
            shape(kv[TS:], 1, 1, SEQ, 2, AG, HD), shape(r["ki"][TS:], 1, 1, SEQ, IDX), *pw,
            shape(so[35], 1, 1, D), shape(so[24:27], 1, 1, CONVW - 1, D),
            shape(kv[:TS], 1, DB, DT, 2, AG, HD), shape(r["ki"][:TS], 1, DB, DT, IDX), *sw,
            shape(so[27:35], 1, DB, D), shape(so[0:24], 1, DB, CONVW - 1, D))


def kernel(**inputs):
    from concourse import bacc
    from concourse.bass_utils import run_bass_kernel_spmd

    arrays = device_inputs(inputs)
    nc = bacc.Bacc("TRN2", target_bir_lowering=False, num_devices=1)
    a = {k: nc.dram_tensor(k, v.shape, mybir.dt.from_np(v.dtype), kind="ExternalInput").ap() for k, v in arrays.items()}
    o = {k: nc.dram_tensor(k, s, F32, kind="ExternalOutput").ap() for k, s in device_outputs().items()}
    build_program(nc, a, o)
    r = run_bass_kernel_spmd(nc, [arrays], core_ids=[0])
    return results(r.results[0])
```
